# Optimizing a Trainium2 kernel written in Bass

```python
import jax
import jax.numpy as jnp
from jax import lax
import numpy as np
import math

D_MODEL = 1024
BATCH = 1
SEQ = 256
DEPTH = 1

D_RNN = D_MODEL
N_LRU_BLOCKS = 16
LRU_BLOCK = D_RNN // N_LRU_BLOCKS
CONV_WIDTH = 4
LRU_C = 8.0
N_HEADS = 16
HEAD_DIM = 64
N_KV_GROUPS = 4
HEADS_PER_GROUP = N_HEADS // N_KV_GROUPS
D_ATTN = N_HEADS * HEAD_DIM
D_KV = N_KV_GROUPS * HEAD_DIM
CMP_LEN = 32
CMP_STRIDE = 16
CMP_HIDDEN = 256
SEL_LEN = 64
SEL_TOPK = 16
WINDOW = 512
Q_BLOCK = 64
FORCE_SCORE = 1e4
R_SEL = SEL_LEN // CMP_STRIDE
R_CMP = CMP_LEN // CMP_STRIDE
ALIBI_MAX_BIAS = 8.0
D_FF = 2816
D_PLE = 256
NORM_EPS = 1e-6

_IN_SIZES = (D_RNN, D_RNN, D_ATTN, D_KV, D_KV, D_KV, D_KV, D_KV, D_KV, 3 * N_HEADS, D_MODEL, D_MODEL)
D_IN = sum(_IN_SIZES)
IN_SPLITS = tuple(int(c) for c in np.cumsum(_IN_SIZES)[:-1])


def rmsnorm(x, g):
    x32 = x.astype(jnp.float32)
    y = x32 * lax.rsqrt(jnp.mean(x32 * x32, axis=-1, keepdims=True) + NORM_EPS)
    return (y * g.astype(jnp.float32)).astype(x.dtype)

def alibi_slopes():
    h = jnp.arange(1, N_HEADS + 1, dtype=jnp.float32)
    return jnp.exp2(-ALIBI_MAX_BIAS * h / N_HEADS)

def masked_softmax(s, mask):
    s = jnp.where(mask, s.astype(jnp.float32), -jnp.inf)
    m = jnp.max(s, axis=-1, keepdims=True)
    m = jnp.where(jnp.isfinite(m), m, 0.0)
    e = jnp.where(mask, jnp.exp(s - m), 0.0)
    return e / jnp.maximum(jnp.sum(e, axis=-1, keepdims=True), 1e-30)

def causal_conv(x, w, b):
    S = x.shape[1]
    xp = jnp.pad(x, ((0, 0), (CONV_WIDTH - 1, 0), (0, 0)))
    y = b
    for k in range(CONV_WIDTH):
        y = y + xp[:, k:k + S] * w[k]
    return y

def _lru_combine(c1, c2):
    a1, b1 = c1
    a2, b2 = c2
    return a1 * a2, a2 * b1 + b2

def rg_lru(xc, wa, ba, wx, bx, lam):
    B, S, _ = xc.shape
    xb = xc.reshape(B, S, N_LRU_BLOCKS, LRU_BLOCK)
    r = jax.nn.sigmoid(jnp.einsum('bsnd,nde->bsne', xb, wa).reshape(B, S, D_RNN) + ba)
    i = jax.nn.sigmoid(jnp.einsum('bsnd,nde->bsne', xb, wx).reshape(B, S, D_RNN) + bx)
    log_a = (-LRU_C * r.astype(jnp.float32)) * jax.nn.softplus(-lam.astype(jnp.float32))
    a = jnp.exp(log_a)
    b = jnp.sqrt(-jnp.expm1(2.0 * log_a)) * (i * xc).astype(jnp.float32)
    _, h = lax.associative_scan(_lru_combine, (a, b), axis=1)
    return h.astype(xc.dtype)

def compress(kv, pos, w1, w2):
    B, S, G, dh = kv.shape
    c = kv.reshape(B, S // CMP_STRIDE, CMP_STRIDE, G, dh)
    blk = jnp.concatenate([c[:, :-1], c[:, 1:]], axis=2)
    blk = blk + pos[:, None, :]
    nc = blk.shape[1]
    blk = blk.transpose(0, 1, 3, 2, 4).reshape(B, nc, G, CMP_LEN * dh)
    return jax.nn.gelu(blk @ w1) @ w2

def nsa(q, kc, vc, ks, vs, kw, vw, gates, slopes):
    B, S = q.shape[0], q.shape[1]
    G, R, dh = N_KV_GROUPS, HEADS_PER_GROUP, HEAD_DIM
    NQ = S // Q_BLOCK
    NB = S // SEL_LEN
    NC = kc.shape[1]
    topk = min(SEL_TOPK, NB)
    scale = HEAD_DIM ** -0.5
    slopes_g = slopes.reshape(G, R)[None, :, :, None, None]
    cmp_end = jnp.arange(NC) * CMP_STRIDE + (CMP_LEN - 1)
    kc_t = kc.transpose(0, 2, 1, 3)
    vc_t = vc.transpose(0, 2, 1, 3)
    ks_blk = ks.reshape(B, NB, SEL_LEN, G, dh).transpose(0, 3, 1, 2, 4)
    vs_blk = vs.reshape(B, NB, SEL_LEN, G, dh).transpose(0, 3, 1, 2, 4)
    kw_pad = jnp.pad(kw, ((0, 0), (WINDOW, 0), (0, 0), (0, 0)))
    vw_pad = jnp.pad(vw, ((0, 0), (WINDOW, 0), (0, 0), (0, 0)))
    q_blocks = q.reshape(B, NQ, Q_BLOCK, G, R, dh).transpose(1, 0, 2, 3, 4, 5)
    g_blocks = gates.reshape(B, NQ, Q_BLOCK, G, R, 3).transpose(1, 0, 2, 3, 4, 5)
    gather = jax.vmap(jax.vmap(lambda kb, idx: kb[idx]))
    blk_ids = jnp.arange(NB)

    def one_block(args):
        qb, qi, gi = args
        q0 = qb * Q_BLOCK
        t = q0 + jnp.arange(Q_BLOCK)
        qf = qi * scale
        dist_c = t[:, None] - cmp_end[None, :]
        s = jnp.einsum('bqgrd,bgcd->bgrqc', qf, kc_t) - slopes_g * dist_c
        p_cmp = masked_softmax(s, dist_c >= 0)
        o_cmp = jnp.einsum('bgrqc,bgcd->bqgrd', p_cmp.astype(vc_t.dtype), vc_t)
        imp = jnp.sum(p_cmp, axis=2)
        left = R_CMP - 1
        imp = jnp.pad(imp, ((0, 0), (0, 0), (0, 0), (left, R_SEL * NB - NC)))
        imp_slc = jnp.zeros(imp.shape[:3] + (NB,), jnp.float32)
        for m in range(R_SEL):
            for n in range(R_CMP):
                st = m - n + left
                imp_slc = imp_slc + imp[..., st:st + R_SEL * NB:R_SEL]
        cur = t // SEL_LEN
        valid = blk_ids[None, :] * SEL_LEN <= t[:, None]
        forced = (blk_ids[None, :] == 0) | (blk_ids[None, :] == cur[:, None]) | (blk_ids[None, :] == cur[:, None] - 1)
        score = jnp.where(valid, imp_slc, -1.0)
        score = jnp.where(forced & valid, FORCE_SCORE, score)
        _, idx = lax.top_k(score, topk)
        k_sel = gather(ks_blk, idx).reshape(B, G, Q_BLOCK, topk * SEL_LEN, dh)
        v_sel = gather(vs_blk, idx).reshape(B, G, Q_BLOCK, topk * SEL_LEN, dh)
        pos = (idx[..., None] * SEL_LEN + jnp.arange(SEL_LEN)).reshape(B, G, Q_BLOCK, topk * SEL_LEN)
        dist_s = t[None, None, :, None] - pos
        s = jnp.einsum('bqgrd,bgqkd->bgrqk', qf, k_sel) - slopes_g * dist_s[:, :, None]
        p_sel = masked_softmax(s, (dist_s >= 0)[:, :, None])
        o_slc = jnp.einsum('bgrqk,bgqkd->bqgrd', p_sel.astype(v_sel.dtype), v_sel)
        kwin = lax.dynamic_slice_in_dim(kw_pad, q0, WINDOW + Q_BLOCK, axis=1)
        vwin = lax.dynamic_slice_in_dim(vw_pad, q0, WINDOW + Q_BLOCK, axis=1)
        pos_w = q0 - WINDOW + jnp.arange(WINDOW + Q_BLOCK)
        dist_w = t[:, None] - pos_w[None, :]
        mask_w = (dist_w >= 0) & (dist_w < WINDOW) & (pos_w[None, :] >= 0)
        s = jnp.einsum('bqgrd,bkgd->bgrqk', qf, kwin) - slopes_g * dist_w
        p_win = masked_softmax(s, mask_w)
        o_win = jnp.einsum('bgrqk,bkgd->bqgrd', p_win.astype(vwin.dtype), vwin)
        g = jax.nn.sigmoid(gi)
        return g[..., 0:1] * o_cmp + g[..., 1:2] * o_slc + g[..., 2:3] * o_win

    o = lax.map(one_block, (jnp.arange(NQ), q_blocks, g_blocks))
    return o.transpose(1, 0, 2, 3, 4, 5).reshape(B, S, D_ATTN)

def first_inputs(seed: int = 0) -> dict:
    key = jax.random.key(seed)
    ks = jax.random.split(key, 32)
    f32 = jnp.float32

    def nrm(k, shape, fan_in):
        return jax.random.normal(k, shape, f32) * (fan_in ** -0.5)

    def gain(k):
        return 1.0 + 0.05 * jax.random.normal(k, (DEPTH, D_MODEL), f32)

    u = jax.random.uniform(ks[10], (DEPTH, D_RNN), f32, minval=0.9, maxval=0.999)
    s = u ** (1.0 / LRU_C)
    lam = jnp.log(s) - jnp.log1p(-s)
    return {
        'x': jax.random.normal(ks[0], (BATCH, SEQ, D_MODEL), f32),
        'p': jax.random.normal(ks[1], (DEPTH, BATCH, SEQ, D_PLE), f32),
        'norm_mix_pre': gain(ks[2]),
        'norm_mix_post': gain(ks[3]),
        'w_in': nrm(ks[4], (DEPTH, D_MODEL, D_IN), D_MODEL),
        'conv_w': nrm(ks[5], (DEPTH, CONV_WIDTH, D_RNN), CONV_WIDTH),
        'conv_b': 0.02 * jax.random.normal(ks[6], (DEPTH, D_RNN), f32),
        'lru_wa': nrm(ks[7], (DEPTH, N_LRU_BLOCKS, LRU_BLOCK, LRU_BLOCK), LRU_BLOCK),
        'lru_ba': 0.02 * jax.random.normal(ks[8], (DEPTH, D_RNN), f32),
        'lru_wx': nrm(ks[9], (DEPTH, N_LRU_BLOCKS, LRU_BLOCK, LRU_BLOCK), LRU_BLOCK),
        'lru_bx': 0.02 * jax.random.normal(ks[11], (DEPTH, D_RNN), f32),
        'lru_lambda': lam,
        'cmp_pos_k': 0.02 * jax.random.normal(ks[12], (DEPTH, CMP_LEN, HEAD_DIM), f32),
        'cmp_pos_v': 0.02 * jax.random.normal(ks[13], (DEPTH, CMP_LEN, HEAD_DIM), f32),
        'cmp_k_w1': nrm(ks[14], (DEPTH, CMP_LEN * HEAD_DIM, CMP_HIDDEN), CMP_LEN * HEAD_DIM),
        'cmp_k_w2': nrm(ks[15], (DEPTH, CMP_HIDDEN, HEAD_DIM), CMP_HIDDEN),
        'cmp_v_w1': nrm(ks[16], (DEPTH, CMP_LEN * HEAD_DIM, CMP_HIDDEN), CMP_LEN * HEAD_DIM),
        'cmp_v_w2': nrm(ks[17], (DEPTH, CMP_HIDDEN, HEAD_DIM), CMP_HIDDEN),
        'w_out': nrm(ks[18], (DEPTH, D_MODEL, D_MODEL), D_MODEL),
        'norm_ffn_pre': gain(ks[19]),
        'norm_ffn_post': gain(ks[20]),
        'ffn_w_gate_up': nrm(ks[21], (DEPTH, D_MODEL, 2 * D_FF), D_MODEL),
        'ffn_w_down': nrm(ks[22], (DEPTH, D_FF, D_MODEL), D_FF),
        'ple_w_proj': nrm(ks[23], (DEPTH, D_PLE, D_MODEL), D_PLE),
        'ple_w_gate': nrm(ks[24], (DEPTH, D_MODEL, D_MODEL), D_MODEL),
        'ple_b_gate': 0.02 * jax.random.normal(ks[25], (DEPTH, D_MODEL), f32),
    }

def first_block(x, p, norm_mix_pre, norm_mix_post, w_in, conv_w, conv_b, lru_wa, lru_ba, lru_wx, lru_bx,
              lru_lambda, cmp_pos_k, cmp_pos_v, cmp_k_w1, cmp_k_w2, cmp_v_w1, cmp_v_w2, w_out,
              norm_ffn_pre, norm_ffn_post, ffn_w_gate_up, ffn_w_down, ple_w_proj, ple_w_gate, ple_b_gate):
    B, S, _ = x.shape
    slopes = alibi_slopes()
    for i in range(DEPTH):
        h = rmsnorm(x, norm_mix_pre[i])
        z = h @ w_in[i]
        xr, gr, q, kc, vc, ksl, vsl, kw, vw, g_nsa, gm_rnn, gm_attn = jnp.split(z, IN_SPLITS, axis=-1)
        xr = causal_conv(xr, conv_w[i], conv_b[i])
        y_rnn = rg_lru(xr, lru_wa[i], lru_ba[i], lru_wx[i], lru_bx[i], lru_lambda[i]) * jax.nn.gelu(gr)
        kv_shape = (B, S, N_KV_GROUPS, HEAD_DIM)
        kc_c = compress(kc.reshape(kv_shape), cmp_pos_k[i], cmp_k_w1[i], cmp_k_w2[i])
        vc_c = compress(vc.reshape(kv_shape), cmp_pos_v[i], cmp_v_w1[i], cmp_v_w2[i])
        y_attn = nsa(q, kc_c, vc_c, ksl.reshape(kv_shape), vsl.reshape(kv_shape),
                     kw.reshape(kv_shape), vw.reshape(kv_shape), g_nsa, slopes)
        y = jax.nn.sigmoid(gm_rnn) * y_rnn + jax.nn.sigmoid(gm_attn) * y_attn
        x = x + rmsnorm(y @ w_out[i], norm_mix_post[i])
        h = rmsnorm(x, norm_ffn_pre[i])
        gate, up = jnp.split(h @ ffn_w_gate_up[i], 2, axis=-1)
        x = x + rmsnorm((jax.nn.silu(gate) * up) @ ffn_w_down[i], norm_ffn_post[i])
        x = x + jax.nn.sigmoid(x @ ple_w_gate[i] + ple_b_gate[i]) * (p[i] @ ple_w_proj[i])
    return x


DEPTH_2 = 2

N_A_LAYERS = DEPTH_2 // 2
N_B_LAYERS = DEPTH_2 - N_A_LAYERS
DN_ALPHA = (2.0 * DEPTH_2) ** 0.25
DN_BETA = (8.0 * DEPTH_2) ** -0.25
LN_EPS = 1e-5
HEAD_NORM_EPS = 1e-6
MIX_WIDTH = D_MODEL

MEM_LEN = 256
MEM_HEADS = 4
MEM_HEAD_DIM = D_MODEL // 16
MEM_WIDTH = MEM_HEADS * MEM_HEAD_DIM

GLA_HEADS = 4
GLA_DV = (MIX_WIDTH - MEM_WIDTH) // GLA_HEADS
GLA_DK = GLA_DV // 2
GLA_GATE_RANK = 16
GLA_TAU = 16.0
GLA_CHUNK = 64
GLA_QK_WIDTH = GLA_HEADS * GLA_DK
GLA_V_WIDTH = GLA_HEADS * GLA_DV

DIL_PAIRS = ((128, 1), (512, 4), (2048, 16))
DIL_GROUPS = len(DIL_PAIRS)
DIL_SLOTS = 6
DIL_HEAD_DIM = (MIX_WIDTH - MEM_WIDTH) // DIL_SLOTS
DIL_BLOCK = 128
DIL_Q_WIDTH = DIL_GROUPS * DIL_SLOTS * DIL_HEAD_DIM
DIL_KV_WIDTH = DIL_SLOTS * DIL_HEAD_DIM

PEER_N_KEYS = 128
PEER_EXPERTS = PEER_N_KEYS * PEER_N_KEYS
PEER_HEADS = 8
PEER_TOPK = 16
PEER_QDIM = 256
PEER_HALF = PEER_QDIM // 2
PEER_TOKEN_BLOCK = 128

A_Q0, A_Q1 = 0, GLA_QK_WIDTH
A_K0, A_K1 = A_Q1, A_Q1 + GLA_QK_WIDTH
A_V0, A_V1 = A_K1, A_K1 + GLA_V_WIDTH
A_R0, A_R1 = A_V1, A_V1 + GLA_V_WIDTH
A_G0, A_G1 = A_R1, A_R1 + GLA_GATE_RANK
A_M0, A_M1 = A_G1, A_G1 + MEM_WIDTH
A_IN_WIDTH = A_M1
B_Q0, B_Q1 = 0, DIL_Q_WIDTH
B_M0, B_M1 = B_Q1, B_Q1 + MEM_WIDTH
B_IN_WIDTH = B_M1


def _layer_norm(x, g, b):
    xf = x.astype(jnp.float32)
    mu = jnp.mean(xf, axis=-1, keepdims=True)
    var = jnp.mean(jnp.square(xf - mu), axis=-1, keepdims=True)
    y = (xf - mu) * lax.rsqrt(var + LN_EPS)
    return (y * g.astype(jnp.float32) + b.astype(jnp.float32)).astype(x.dtype)

def _gla(q, k, v, log_a):
    B, S, H, K = q.shape
    nc = S // GLA_CHUNK

    def chunks(t):
        return t.astype(jnp.float32).reshape(B, nc, GLA_CHUNK, H, -1).transpose(1, 0, 3, 2, 4)

    q_c = chunks(q) * (K ** -0.5)
    k_c, v_c, g_c = chunks(k), chunks(v), chunks(log_a)
    b = jnp.cumsum(g_c, axis=3)
    b_last = b[:, :, :, -1:, :]
    q_t = q_c * jnp.exp(b)
    k_t = k_c * jnp.exp(-b)
    k_end = k_c * jnp.exp(b_last - b)
    causal = jnp.tril(jnp.ones((GLA_CHUNK, GLA_CHUNK), dtype=bool))
    attn = jnp.where(causal, jnp.einsum('nbhck,nbhsk->nbhcs', q_t, k_t), 0.0)
    o_intra = jnp.einsum('nbhcs,nbhsv->nbhcv', attn, v_c)

    def step(state, inp):
        qt, ke, vc, dec = inp
        o = jnp.einsum('bhck,bhkv->bhcv', qt, state)
        state = dec[..., None] * state + jnp.einsum('bhck,bhcv->bhkv', ke, vc)
        return state, o

    s0 = jnp.zeros((B, H, K, v.shape[-1]), jnp.float32)
    _, o_inter = lax.scan(step, s0, (q_t, k_end, v_c, jnp.exp(b_last[:, :, :, 0, :])))
    return (o_intra + o_inter).transpose(1, 0, 3, 2, 4).reshape(B, S, H, -1)

def _dilated_group(q, k, v, window, dilation):
    B, S, H, E = q.shape
    L = S // dilation
    nb = -(-L // DIL_BLOCK)
    Lp = nb * DIL_BLOCK
    span = window // dilation

    def sub(t):
        return t.reshape(B, L, dilation, H, E).transpose(0, 2, 3, 1, 4)

    qs = jnp.pad(sub(q), ((0, 0), (0, 0), (0, 0), (0, Lp - L), (0, 0)))
    qs = qs.reshape(B, dilation, H, nb, DIL_BLOCK, E)

    def kv_blocks(t):
        tp = jnp.pad(sub(t), ((0, 0), (0, 0), (0, 0), (DIL_BLOCK, Lp - L), (0, 0)))
        prev = tp[:, :, :, :Lp].reshape(B, dilation, H, nb, DIL_BLOCK, E)
        cur = tp[:, :, :, DIL_BLOCK:].reshape(B, dilation, H, nb, DIL_BLOCK, E)
        return jnp.concatenate([prev, cur], axis=4)

    kb, vb = kv_blocks(k), kv_blocks(v)
    s = jnp.einsum('bdhnqe,bdhnke->bdhnqk', qs, kb,
                   preferred_element_type=jnp.float32) * (E ** -0.5)
    qi = jnp.arange(DIL_BLOCK)[:, None]
    kj = jnp.arange(2 * DIL_BLOCK)[None, :]
    rel = DIL_BLOCK + qi - kj
    band = (rel >= 0) & (rel <= span)
    not_front = (jnp.arange(nb)[:, None, None] > 0) | (kj[None] >= DIL_BLOCK)
    mask = band[None] & not_front
    s = jnp.where(mask, s, -jnp.inf)
    lse = jax.nn.logsumexp(s, axis=-1)
    p = jnp.exp(s - lse[..., None])
    o = jnp.einsum('bdhnqk,bdhnke->bdhnqe', p.astype(vb.dtype), vb,
                   preferred_element_type=jnp.float32)
    o = o.reshape(B, dilation, H, Lp, E)[:, :, :, :L].transpose(0, 3, 1, 2, 4).reshape(B, S, H, E)
    lse = lse.reshape(B, dilation, H, Lp)[..., :L].transpose(0, 3, 1, 2).reshape(B, S, H)
    return o, lse

def _dilated_attention(q_all, k, v):
    outs, lses = [], []
    for g, (window, dilation) in enumerate(DIL_PAIRS):
        o, l = _dilated_group(q_all[:, :, g], k, v, window, dilation)
        outs.append(o)
        lses.append(l)
    wts = jax.nn.softmax(jnp.stack(lses, axis=0), axis=0)
    return jnp.einsum('gbsh,gbshe->bshe', wts, jnp.stack(outs, axis=0))

def _mem_attn(qm, km, vm):
    s = jnp.einsum('bshe,bmhe->bhsm', qm, km,
                   preferred_element_type=jnp.float32) * (qm.shape[-1] ** -0.5)
    p = jax.nn.softmax(s, axis=-1)
    return jnp.einsum('bhsm,bmhe->bshe', p.astype(vm.dtype), vm)

def _peer(x, w_q, sub_keys, u, v):
    B, S, D = x.shape
    T = B * S
    xt = x.reshape(T, D)
    q = (xt @ w_q).reshape(T, PEER_HEADS, 2, PEER_HALF)
    s = jnp.einsum('thpe,pne->thpn', q, sub_keys, preferred_element_type=jnp.float32)
    top_s, top_i = lax.top_k(s, PEER_TOPK)
    cand = (top_s[:, :, 0, :, None] + top_s[:, :, 1, None, :]).reshape(
        T, PEER_HEADS, PEER_TOPK * PEER_TOPK)
    best_s, best_j = lax.top_k(cand, PEER_TOPK)
    idx_a = jnp.take_along_axis(top_i[:, :, 0], best_j // PEER_TOPK, axis=-1)
    idx_b = jnp.take_along_axis(top_i[:, :, 1], best_j % PEER_TOPK, axis=-1)
    expert = idx_a * PEER_N_KEYS + idx_b
    gate = jax.nn.softmax(best_s, axis=-1)
    nblk = T // PEER_TOKEN_BLOCK

    def block(args):
        xb, eb, gb = args
        h = jnp.einsum('td,thkd->thk', xb, u[eb], preferred_element_type=jnp.float32)
        a = (jax.nn.gelu(h, approximate=False) * gb).astype(xb.dtype)
        return jnp.einsum('thk,thkd->td', a, v[eb])

    out = lax.map(block, (xt.reshape(nblk, PEER_TOKEN_BLOCK, D),
                          expert.reshape(nblk, PEER_TOKEN_BLOCK, PEER_HEADS, PEER_TOPK),
                          gate.reshape(nblk, PEER_TOKEN_BLOCK, PEER_HEADS, PEER_TOPK)))
    return out.reshape(B, S, D).astype(x.dtype)

def second_inputs(seed: int = 0) -> dict:
    key = jax.random.key(seed)
    ks = jax.random.split(key, 20)
    n = jax.random.normal
    D = D_MODEL
    return {
        'x': n(ks[0], (BATCH, SEQ, D), jnp.float32),
        'mem': n(ks[1], (BATCH, MEM_LEN, D), jnp.float32),
        'a_w_in': n(ks[2], (N_A_LAYERS, D, A_IN_WIDTH), jnp.float32) * D ** -0.5,
        'a_w_gate2': n(ks[3], (N_A_LAYERS, GLA_GATE_RANK, GLA_QK_WIDTH), jnp.float32) * GLA_GATE_RANK ** -0.5,
        'a_b_gate': 0.02 * n(ks[4], (N_A_LAYERS, GLA_QK_WIDTH), jnp.float32),
        'a_norm_g': 1.0 + 0.02 * n(ks[5], (N_A_LAYERS, GLA_V_WIDTH), jnp.float32),
        'b_w_in': n(ks[6], (N_B_LAYERS, D, B_IN_WIDTH), jnp.float32) * D ** -0.5,
        'shared_w_kv': n(ks[7], (D, 2 * DIL_KV_WIDTH), jnp.float32) * D ** -0.5,
        'w_mem_kv': n(ks[8], (DEPTH_2, D, 2 * MEM_WIDTH), jnp.float32) * D ** -0.5,
        'w_out': n(ks[9], (DEPTH_2, MIX_WIDTH, D), jnp.float32) * (MIX_WIDTH ** -0.5 * DN_BETA),
        'ln_mix_g': 1.0 + 0.02 * n(ks[10], (DEPTH_2, D), jnp.float32),
        'ln_mix_b': 0.02 * n(ks[11], (DEPTH_2, D), jnp.float32),
        'ln_ffn_g': 1.0 + 0.02 * n(ks[12], (DEPTH_2, D), jnp.float32),
        'ln_ffn_b': 0.02 * n(ks[13], (DEPTH_2, D), jnp.float32),
        'peer_w_q': n(ks[14], (DEPTH_2, D, PEER_HEADS * PEER_QDIM), jnp.float32) * D ** -0.5,
        'peer_sub_keys': n(ks[15], (DEPTH_2, 2, PEER_N_KEYS, PEER_HALF), jnp.float32) * PEER_HALF ** -0.5,
        'peer_u': n(ks[16], (DEPTH_2, PEER_EXPERTS, D), jnp.float32) * D ** -0.5,
        'peer_v': n(ks[17], (DEPTH_2, PEER_EXPERTS, D), jnp.float32) * (DN_BETA * PEER_HEADS ** -0.5),
    }

def second_block(x, mem, a_w_in, a_w_gate2, a_b_gate, a_norm_g, b_w_in, shared_w_kv,
              w_mem_kv, w_out, ln_mix_g, ln_mix_b, ln_ffn_g, ln_ffn_b,
              peer_w_q, peer_sub_keys, peer_u, peer_v):
    B, S, _ = x.shape
    shared_k = None
    shared_v = None
    for l in range(DEPTH_2):
        mkv = (mem @ w_mem_kv[l]).reshape(B, MEM_LEN, 2, MEM_HEADS, MEM_HEAD_DIM)
        if l < N_A_LAYERS:
            h = x @ a_w_in[l]
            q = h[..., A_Q0:A_Q1].reshape(B, S, GLA_HEADS, GLA_DK)
            k = h[..., A_K0:A_K1].reshape(B, S, GLA_HEADS, GLA_DK)
            v = h[..., A_V0:A_V1].reshape(B, S, GLA_HEADS, GLA_DV)
            r = h[..., A_R0:A_R1]
            g_pre = (h[..., A_G0:A_G1] @ a_w_gate2[l] + a_b_gate[l]).astype(jnp.float32)
            log_a = (jax.nn.log_sigmoid(g_pre) / GLA_TAU).reshape(B, S, GLA_HEADS, GLA_DK)
            o = _gla(q, k, v, log_a)
            o = o * lax.rsqrt(jnp.mean(jnp.square(o), axis=-1, keepdims=True) + HEAD_NORM_EPS)
            o = o.reshape(B, S, GLA_V_WIDTH) * a_norm_g[l].astype(jnp.float32)
            mix = (jax.nn.silu(r.astype(jnp.float32)) * o).astype(x.dtype)
            qm = h[..., A_M0:A_M1]
        else:
            h = x @ b_w_in[l - N_A_LAYERS]
            qd = h[..., B_Q0:B_Q1].reshape(B, S, DIL_GROUPS, DIL_SLOTS, DIL_HEAD_DIM)
            mix = _dilated_attention(qd, shared_k, shared_v).reshape(B, S, DIL_KV_WIDTH).astype(x.dtype)
            qm = h[..., B_M0:B_M1]
        mo = _mem_attn(qm.reshape(B, S, MEM_HEADS, MEM_HEAD_DIM),
                       mkv[:, :, 0], mkv[:, :, 1]).reshape(B, S, MEM_WIDTH).astype(x.dtype)
        y = jnp.concatenate([mix, mo], axis=-1) @ w_out[l]
        x = _layer_norm(DN_ALPHA * x + y, ln_mix_g[l], ln_mix_b[l])
        f = _peer(x, peer_w_q[l], peer_sub_keys[l], peer_u[l], peer_v[l])
        x = _layer_norm(DN_ALPHA * x + f, ln_ffn_g[l], ln_ffn_b[l])
        if l == N_A_LAYERS - 1:
            kv = (x @ shared_w_kv).reshape(B, S, 2, DIL_SLOTS, DIL_HEAD_DIM)
            shared_k = kv[:, :, 0]
            shared_v = kv[:, :, 1]
    return x


def setup_inputs(seed=0):
    out = dict(first_inputs(seed))
    for name, value in second_inputs(seed + 1).items():
        if name != "x":
            out[name + "_2"] = value
    return out


def reference(
    x, p, norm_mix_pre, norm_mix_post, w_in, conv_w, conv_b, lru_wa, lru_ba, lru_wx, lru_bx,
    lru_lambda, cmp_pos_k, cmp_pos_v, cmp_k_w1, cmp_k_w2, cmp_v_w1, cmp_v_w2, w_out,
    norm_ffn_pre, norm_ffn_post, ffn_w_gate_up, ffn_w_down, ple_w_proj, ple_w_gate, ple_b_gate,
    mem_2, a_w_in_2, a_w_gate2_2, a_b_gate_2, a_norm_g_2, b_w_in_2, shared_w_kv_2, w_mem_kv_2,
    w_out_2, ln_mix_g_2, ln_mix_b_2, ln_ffn_g_2, ln_ffn_b_2, peer_w_q_2, peer_sub_keys_2,
    peer_u_2, peer_v_2,
):
    x = first_block(
        x, p, norm_mix_pre, norm_mix_post, w_in, conv_w, conv_b, lru_wa, lru_ba, lru_wx, lru_bx,
        lru_lambda, cmp_pos_k, cmp_pos_v, cmp_k_w1, cmp_k_w2, cmp_v_w1, cmp_v_w2, w_out,
        norm_ffn_pre, norm_ffn_post, ffn_w_gate_up, ffn_w_down, ple_w_proj, ple_w_gate,
        ple_b_gate,
    )
    return second_block(
        x, mem_2, a_w_in_2, a_w_gate2_2, a_b_gate_2, a_norm_g_2, b_w_in_2, shared_w_kv_2,
        w_mem_kv_2, w_out_2, ln_mix_g_2, ln_mix_b_2, ln_ffn_g_2, ln_ffn_b_2, peer_w_q_2,
        peer_sub_keys_2, peer_u_2, peer_v_2,
    )


_drawn_inputs = setup_inputs


def setup_inputs(seed=0):
    import zlib

    import numpy as np

    out = dict(_drawn_inputs(seed))
    spreads = {}
    factors = {'lru_ba': 8.0,
     'lru_bx': 6.978,
     'cmp_pos_k': 24.531,
     'cmp_pos_v': 4.184,
     'ple_b_gate': 8.0,
     'a_b_gate_2': 8.0,
     'a_norm_g_2': 20.153}
    for name, (base, spread) in spreads.items():
        noise = np.random.default_rng([zlib.crc32(name.encode()), seed]).standard_normal(out[name].shape)
        drawn = base * np.exp(spread * noise) if base else spread * noise
        out[name] = jnp.asarray(drawn.astype(out[name].dtype))
    for name, factor in factors.items():
        out[name] = (out[name] * factor).astype(out[name].dtype)
    return out
```

```python
from contextlib import ExitStack

import numpy as np

import concourse.bass as bass
from concourse import mybir

F32 = mybir.dt.float32
U32 = mybir.dt.uint32
ALU = mybir.AluOpType
ACT = mybir.ActivationFunctionType
AX = mybir.AxisListType.X

P = 128
D = 1024
S = 256
NT = S // P
NK = D // P
SLOT = 1024
RING = 12
NEG = -1e30

HEADS, HD, GROUPS = 16, 64, 4
NCMP = 15
FF = 2816
NF = FF // P
PLE = 256
GH, GDK, GDV = 4, 96, 192
CH = 64
NCH = S // CH
DSLOTS, DGROUPS = 6, 3
MH = 4
PH, PN, PK = 8, 128, 16
EXPERTS = PN * PN
ALPHA = 4.0 ** 0.25
GBUF = 16
BODY = 32
TURNS = P // BODY
TH = BODY // 16
NROW = 6

BLOCKS = [(2 * (j // 4) + s) * 4 + j % 4 for j in range(8) for s in range(2)]
SLOPES = [2.0 ** (-8.0 * (b + 1) / HEADS) for b in BLOCKS]

UNITS = [(j, s, t) for j in range(8) for s in range(2) for t in range(NT)]
NZ = 12


def attention_order():
    order = []
    for u in range(len(UNITS) + 3):
        if u < len(UNITS):
            order.append(("score", u))
        if u % 2 == 0 and u // 2 < NZ:
            order.append(("gate", u // 2))
        if 0 <= u - 2 < len(UNITS):
            order.append(("turn", u - 2))
        if 0 <= u - 3 < len(UNITS):
            order.append(("value", u - 3))
    return order


def pipelined(n):
    order = []
    for u in range(n + 3):
        if u < n:
            order.append(("score", u))
        if 0 <= u - 2 < n:
            order.append(("turn", u - 2))
        if 0 <= u - 3 < n:
            order.append(("value", u - 3))
    return order


def peer_head_order():
    return [step for h in range(PH + 1) for step in (("q", h), ("s", h - 1))
            if 0 <= step[1] < PH]


MEM_UNITS = [(m, t) for m in range(2) for t in range(NT)]
DIL_UNITS = [(s, t) for s in range(DSLOTS) for t in range(NT)]


def ffn_order():
    order = []
    for f in range(NF + 1):
        if f < NF:
            order += [("gate", f), ("up", f)]
        if f >= 1:
            order.append(("down", f - 1))
    return order


def job_plan():
    ids, drains, banks = {}, [], []
    state = {"bank": 0}

    def plan(stage, n, drain, fixed=None):
        for i in range(n):
            ids[(stage, i)] = len(drains)
            drains.append(drain)
            if fixed is None:
                banks.append(state["bank"])
                state["bank"] = (state["bank"] + 1) % 8
            else:
                banks.append(fixed[i % len(fixed)])

    for l in range(2):
        plan(f"mem_k{l}", 1, "act")
        plan(f"mem_v{l}", 2, "act")
    plan("xT_mix", 4, "dve")
    plan("xr", 4, "act")
    plan("kc", 1, "dve")
    plan("vc", 1, "dve")
    plan("lru_r", 4, "act")
    plan("lru_i", 4, "act")
    plan("k_sel", 1, "act")
    plan("k_win", 1, "act")
    plan("v_sw", 2, "act")
    plan("nsa_gate", 1, "act")
    plan("q", 4, "act")
    plan("hid_k", 2, "act")
    plan("hid_v", 2, "act")
    plan("k_cmp", 1, "dve")
    plan("v_cmp", 1, "dve")
    plan("cmp_score", 4, "dve")
    plan("cmp_turn", 8, "act")
    for kind, u in attention_order():
        drain = {"score": "dve", "gate": "act", "turn": "act", "value": "dve"}[kind]
        ids[("att_" + kind, u)] = len(drains)
        drains.append(drain)
        banks.append(state["bank"])
        state["bank"] = (state["bank"] + 1) % 8
    plan("mix_out", 4, "dve")
    plan("xT_ffn", 4, "dve")
    plan("ffn_gu", NF, "dve", [0, 1, 2, 3])
    plan("ffn_down", 4, "dve", [4, 5, 6, 7])
    state["bank"] = 0
    plan("xT_ple", 4, "dve")
    plan("ple_gate", 4, "dve")
    plan("ple_proj", 4, "dve")
    for l in range(2):
        plan(f"xT_in{l}", 4, "dve")
        if l == 0:
            plan("gla_q", 2, "act")
            plan("gla_k", 2, "act")
            plan("gla_g1", 1, "act")
            plan("gla_gate", 2, "dve")
            plan("qm0", 1, "act")
            plan("gla_v", 4, "act")
            plan("gla_r", 4, "act")
            plan("gla_kendT", 2, "dve")
            plan("gla_intra", 1, "dve")
            plan("gla_kv", 6, "dve")
            plan("gla_o", 4, "dve")
            plan("gla_mixT", 3, "act")
        else:
            plan("dil_k", 3, "act")
            plan("dil_v", 4, "act")
            plan("dil_q", 9, "act")
            plan("qm1", 1, "act")
            for kind, u in pipelined(len(DIL_UNITS)):
                n = 2 if kind == "score" and DIL_UNITS[u][1] else 1
                for i in range(n):
                    ids[("dil_" + kind, 2 * u + i)] = len(drains)
                    drains.append({"score": "dve", "turn": "act", "value": "dve"}[kind])
                    banks.append(state["bank"])
                    state["bank"] = (state["bank"] + 1) % 8
        for kind, u in pipelined(len(MEM_UNITS)):
            for i in range(2 if kind == "score" else 1):
                ids[(f"mem_{kind}{l}", 2 * u + i)] = len(drains)
                drains.append({"score": "dve", "turn": "act", "value": "dve"}[kind])
                banks.append(state["bank"])
                state["bank"] = (state["bank"] + 1) % 8
        plan(f"out{l}", 4, "dve")
        plan(f"xT_peer{l}", 4, "dve")
        for kind, h in peer_head_order():
            ids[(f"peer_{kind}{l}", h)] = len(drains)
            drains.append("act")
            banks.append(state["bank"])
            state["bank"] = (state["bank"] + 1) % 8
    before, last = [], {}
    for n, b in enumerate(banks):
        before.append(last.get(b))
        last[b] = n
    freed = []
    seen = {"act": 0, "dve": 0}
    for d in drains:
        seen[d] += 1
        freed.append(seen[d])
    return ids, drains, banks, before, freed



def slots_of_columns(w, width=P):
    k, n = w.shape
    out = []
    for c in range(0, n, width):
        blk = w[:, c:c + width]
        out.append(blk.reshape(k // P, P, blk.shape[1]).transpose(1, 0, 2).reshape(P, -1))
    return out


def slots_of_rows(w):
    k, n = w.shape
    per = max(1, SLOT // n)
    out = []
    for c in range(0, k, per * P):
        blk = w[c:c + per * P]
        out.append(blk.reshape(-1, P, n).transpose(1, 0, 2).reshape(P, -1))
    return out


def block_order(w, axis=-1):
    w = np.moveaxis(w, axis, -1)
    w = w.reshape(w.shape[:-1] + (16, 64))[..., BLOCKS, :].reshape(w.shape)
    return np.moveaxis(w, -1, axis)


def block_diagonal(w):
    out = np.zeros((P, 8, P), np.float32)
    for j in range(8):
        for s in range(2):
            out[64 * s:64 * s + 64, j, 64 * s:64 * s + 64] = w[BLOCKS[2 * j + s]]
    return out.reshape(P, -1)


def weight_slots(a):
    w_in = a["w_in"][0]
    cuts = dict(xr=(0, 1024), gr=(1024, 2048), q=(2048, 3072), kc=(3072, 3328), vc=(3328, 3584),
                ks=(3584, 3840), vs=(3840, 4096), kw=(4096, 4352), vw=(4352, 4608), g=(4608, 4656),
                gmr=(4656, 5680), gma=(5680, 6704))
    z = {n: w_in[:, i:j] for n, (i, j) in cuts.items()}
    out = []
    for l in range(2):
        out += slots_of_columns(a["w_mem_kv_2"][l][:, :256])
        out += slots_of_rows(a["w_mem_kv_2"][l][:, 256:])
    out += slots_of_columns(block_order(z["xr"]))
    out += slots_of_columns(z["kc"]) + slots_of_columns(z["vc"])
    out += [block_diagonal(a["lru_wa"][0]), block_diagonal(a["lru_wx"][0])]
    out += slots_of_columns(z["ks"]) + slots_of_columns(z["kw"])
    out += slots_of_rows(np.concatenate([z["vs"], z["vw"]], 1))
    out += slots_of_columns(z["g"].reshape(D, 16, 3)[:, BLOCKS].transpose(0, 2, 1).reshape(D, 48), 48)
    out += slots_of_columns(block_order(z["q"]))
    out += slots_of_rows(a["cmp_k_w1"][0]) + slots_of_rows(a["cmp_v_w1"][0])
    out += slots_of_columns(block_order(z["gma"])) + slots_of_columns(block_order(z["gr"]))
    out += slots_of_columns(block_order(z["gmr"]))
    out += slots_of_rows(block_order(a["w_out"][0], 0))
    gate = slots_of_columns(a["ffn_w_gate_up"][0][:, :FF])
    up = slots_of_columns(a["ffn_w_gate_up"][0][:, FF:])
    down = slots_of_rows(a["ffn_w_down"][0])
    out += [{"gate": gate, "up": up, "down": down}[kind][f] for kind, f in ffn_order()]
    out += slots_of_rows(a["ple_w_gate"][0]) + slots_of_rows(a["ple_w_proj"][0])
    aw = a["a_w_in_2"][0]
    qk, vw = GH * GDK, GH * GDV
    out += slots_of_columns(aw[:, :2 * qk], GDK)
    g0 = 2 * qk + 2 * vw
    out += slots_of_columns(aw[:, g0:g0 + 16], 16)
    out += slots_of_columns(aw[:, g0 + 16:])
    out += slots_of_rows(aw[:, 2 * qk:2 * qk + vw]) + slots_of_rows(aw[:, 2 * qk + vw:g0])
    for l in range(2):
        if l:
            kv = a["shared_w_kv_2"]
            out += slots_of_columns(kv[:, :768]) + slots_of_rows(kv[:, 768:])
            bw = a["b_w_in_2"][0]
            q = bw[:, :2304].reshape(D, 3, 6, 128).transpose(0, 2, 1, 3).reshape(D, 2304)
            out += slots_of_columns(q) + slots_of_columns(bw[:, 2304:])
        out += slots_of_rows(a["w_out_2"][l])
        out += slots_of_columns(a["peer_w_q_2"][l])
    pad = -len(out) % RING
    w = np.zeros((len(out) + pad, P, SLOT), np.float32)
    for n, s in enumerate(out):
        w[n, :, :s.shape[1]] = s
    return w


def constant_columns(a):
    i = np.arange(P)[:, None]
    cols = {}

    def put(name, x):
        x = np.asarray(x, np.float32)
        full = np.zeros((P, x.reshape(x.shape[0], -1).shape[1]), np.float32)
        full[:x.shape[0]] = x.reshape(x.shape[0], -1)
        cols[name] = full

    put("ident", np.eye(P))
    dist = P + i - np.arange(S)[None, :]
    put("neg_dist", np.where(dist >= 0, -dist, NEG))
    t = (np.arange(NT)[None, :] * P + i)[:, :, None]
    dc = t - (np.arange(NCMP) * 16 + 31)[None, None, :]
    put("cmp_bias", np.where(dc[:, :, None] >= 0, -dc[:, :, None] * np.array(SLOPES)[None, None, :, None], NEG))
    put("cmp_mask", dc >= 0)
    put("tri", (np.arange(CH)[None, :] >= i % CH))
    j = np.arange(S)[None, :]
    rel = P + i - j
    m1 = [np.where((rel >= 0) & (rel <= 128), 0, NEG), np.where((rel >= 0) & (rel % 4 == 0), 0, NEG),
          np.where((rel >= 0) & (rel % 16 == 0), 0, NEG)]
    put("dil_mask1", np.stack(m1, 1))
    put("dil_mask0", np.stack([m[:, P:] for m in m1], 1))
    put("iota", np.broadcast_to(np.arange(PK), (P, PK)))
    put("eps", np.broadcast_to(np.array([1e-6, 1e-5, 1.0, 0.0]), (P, 4)))

    def col(v):
        return v.reshape(NK, P).T

    put("g_mix", col(a["norm_mix_pre"][0]))
    put("g_ffn", col(a["norm_ffn_pre"][0]))
    put("conv_w", np.stack([col(block_order(a["conv_w"][0][k])) for k in range(4)], 1))
    for name, key in (("conv_b", "conv_b"), ("lru_ba", "lru_ba"), ("lru_bx", "lru_bx"), ("lam", "lru_lambda")):
        put(name, col(block_order(a[key][0])))
    put("gla_b", a["a_b_gate_2"][0].reshape(GH, GDK).T)
    for n in "kv":
        put("pos_" + n, a[f"cmp_pos_{n}"][0].reshape(16, 2 * HD).T)
        put("w2_" + n, a[f"cmp_{n}_w2"][0].reshape(2, P, HD).transpose(1, 0, 2))
    put("w_gate2", a["a_w_gate2_2"][0])
    put("keysT", a["peer_sub_keys_2"].transpose(3, 0, 1, 2))
    put("pT", a["p"][0, 0].reshape(S, 2, P).transpose(2, 1, 0))
    return cols


ROWS = ["norm_mix_post", "norm_ffn_post", "ple_b_gate", "a_norm_g_2", "mix_g0", "mix_b0", "ffn_g0", "ffn_b0",
        "mix_g1", "mix_b1", "ffn_g1", "ffn_b1"]


def row_vectors(a):
    out = np.zeros((len(ROWS), D), np.float32)
    for n, name in enumerate(ROWS):
        if name in a:
            v = a[name][0]
        else:
            v = a[f"ln_{name[:3]}_{name[4]}_2"][int(name[5])]
        out[n, :v.shape[0]] = v
    return out



def build(nc, x_in, memT_in, weights, consts, where, rows_in, peer_u, peer_v, out, upto=None, dump=None):
    ids, drains, banks, before, freed_count = job_plan()
    n_slots = weights.shape[0]
    n_const = consts.shape[1]
    ctx = ExitStack()
    with ctx:
        def sb(name, shape, dt=F32):
            return ctx.enter_context(nc.sbuf_tensor(name, shape, dt))

        named = {}

        def sem(name):
            if name not in named:
                named[name] = ctx.enter_context(nc.semaphore(name))
            return named[name]

        ring = sb("weight_ring", [P, RING, SLOT])
        rows = sb("row_ring", [P, NROW, D])
        cst = sb("const_tile", [P, n_const])
        x = sb("x_tok", [P, NT, D])
        xT = sb("xT", [P, NK, S])
        mem_k = sb("mem_k", [P, 2, 2, S])
        mem_v = sb("mem_v", [P, 2, 2, S])
        arena = sb("arena", [P, 24300])
        ps = [ctx.enter_context(nc.psum_tensor(f"bank{b}", [P, 512], F32)) for b in range(8)]

        def c(name, *dims):
            lo, hi = where[name]
            v = cst[:, lo:hi]
            if len(dims) == 2:
                v = v.rearrange("p (a b) -> p a b", a=dims[0])
            if len(dims) == 3:
                v = v.rearrange("p (a b c) -> p a b c", a=dims[0], b=dims[1])
            return v

        def area(lo, *dims):
            n = int(np.prod(dims))
            assert lo + n <= 24300, (lo, dims)
            v = arena[:, lo:lo + n]
            if len(dims) == 2:
                v = v.rearrange("p (a b) -> p a b", a=dims[0])
            if len(dims) == 3:
                v = v.rearrange("p (a b c) -> p a b c", a=dims[0], b=dims[1])
            if len(dims) == 4:
                v = v.rearrange("p (a b c d) -> p a b c d", a=dims[0], b=dims[1], c=dims[2])
            return v

        ident = c("ident")
        xr_pad = area(0, NK, S + 3)
        xc = area(2080, NK, S)
        lru_a = area(4128, NK, S)
        lru_i = area(6176, NK, S)
        lru_t = area(8224, NK, S)
        gr = area(10272, NK, S)
        qT = area(12320, NK, S)
        memT = area(12320, NK, S)
        kT = [area(14368, 2, S), area(14880, 2, S)]
        v_sw = area(15392, NT, 512)
        gmr = area(16416, NK, S)
        gma = area(18464, NK, S)
        yT = area(20512, NK, S)
        xn = area(20512, NT, D)
        cmp_in = {n: [area(20512 + 1024 * (n == "v") + 512 * h, GROUPS, P) for h in range(2)] for n in "kv"}
        att_E = [area(512 * b, 2, S) for b in range(3)]
        att_E0 = [area(512 * b, 2, P) for b in range(3)]
        att_PT = [area(4128 + 512 * b, 4, P) for b in range(2)]
        att_diag = [area(5152 + 256 * b, 2, P) for b in range(3)]
        cmp_PT = area(6176, HEADS, S)
        small = 22560
        hidT = {n: area(small + 120 * (n == "v"), 2, 4 * NCMP) for n in "kv"}
        k_cmp = area(small + 240, 2, NCMP)
        v_cmp = area(small + 270, 256)
        nsa_g = area(small + 526, NT, 3, HEADS)
        cmp_s = area(small + 622, NT, HEADS, NCMP)
        stat = area(small + 1102, 128)
        lam_t = area(small + 1230, 10, NK)
        att_nm = area(small + 1310, 3, 2)
        att_sum = area(small + 1316, 3, 2)
        att_rec = area(small + 1322, 3, 2)
        cmp_st = area(small + 1328, NT, 4, HEADS)
        assert small + 1328 + 128 <= 24300
        gate_s = [area(256 * b, S) for b in range(2)]
        act_T = [area(512 + 256 * b, S) for b in range(3)]
        tmp_tok = area(2048, NT, D)
        gq = area(0, GH, S)
        gk = area(1024, GH, S)
        gf = area(2048, GH * S)
        ge = area(3072, GH * S)
        gb = area(4096, GH * S)
        geb = area(5120, GH * S)
        gt = area(6144, GH * S)
        gkt = area(7168, GH, S)
        gke = area(8192, GH, S)
        scan_mask = area(9216, GH * S)
        kendT = area(10240, NT, GH, GDK)
        attnT = area(11008, NT, GH, CH)
        gv = area(11520, NT, GH * GDV)
        grs = area(13056, NT, GH * GDV)
        state = area(14592, NCH - 1, GH * GDV)
        mixin = area(16896, NT, GH * GDV)
        mixT = area(18432, NK, S)
        qmT = area(20480, 2, S)
        g1T = area(20992, S)
        tmp_sq = area(21248, S)
        mem_E = [area(2048 + 512 * b, 2, S) for b in range(3)]
        mem_PT = [area(4096 + 512 * b, 4, P) for b in range(2)]
        mem_diag = [area(5120 + 256 * b, 2, P) for b in range(3)]
        dqT = area(0, 18, S)
        dkT = area(6144, DSLOTS, S)
        dv = area(7680, NT, 768)
        dil_E = [area(9216 + 768 * b, 3, S) for b in range(3)]
        dil_E0 = [area(9216 + 768 * b, 3, P) for b in range(3)]
        dil_PT = [area(11520 + 256 * b, 2, P) for b in range(2)]
        dil_diag = [area(12032 + 128 * b, P) for b in range(3)]
        gbuf = [area(1024 * b, D) for b in range(GBUF)]
        sc = [area(16384 + 2048 * t, 16, PN) for t in range(NT)]
        pq = [area(20480 + 512 * b, 2, S) for b in range(2)]
        rest = area(21504, 2 * TH * PN)
        onehot = area(21504, TH, PK, PK)
        top_v, top_i, top_f = (area(22016 + 64 * n, 2 * TH, PK) for n in range(3))
        best_v, best_j, pos_a, pos_b, sel_a, sel_b, pos_u = (area(22208 + 32 * n, TH, PK) for n in range(7))
        expert = [area(22432 + 128 * t, P) for t in range(NT)]
        gate_w = [area(22688 + 128 * t, PH, PK) for t in range(NT)]
        hdot = [area(22944 + 128 * t, P) for t in range(NT)]
        stage = area(23200, BODY)
        peer_st = area(23264, 64)
        acc = [xT[:, 4 * b:4 * b + 4, :].rearrange("p k s -> p (k s)") for b in range(2)]

        STAGES = ["mem", "z", "lru", "cmp", "att", "mix", "ffn", "ple", "gla", "memat0", "out0", "peer0",
                  "dil", "memat1", "out1", "peer1"]
        limit = len(STAGES) if upto is None else STAGES.index(upto) + 1

        def on(stage_name):
            return STAGES.index(stage_name) < limit

        def wait_filled(e, key):
            e.wait_ge(sem("psum_filled"), ids[key] + 1)

        def wait_drained(e, key):
            n = ids[key]
            e.wait_ge(sem("drained_by_" + drains[n]), freed_count[n])

        def bank(key):
            return ps[banks[ids[key]]]

        def counter(e):
            count, pending = {}, {}

            def done(ins, name, n=1):
                ins.then_inc(sem(name), n)
                count[name] = count.get(name, 0) + n
                pending[name] = count[name]
                return ins

            def settle():
                for name, v in pending.items():
                    e.wait_ge(sem(name), v)
                pending.clear()

            return done, settle, count

        block = ctx.enter_context(nc.Block())
        PASSES = [(kind, t) for t in range(NT) for kind in "uv"]

        wt = {"n": 0, "owed": 0}

        @block.tensor
        def _(pe):
            def next_weights():
                n = wt["n"]
                pe.wait_ge(sem(f"weight_loaded{n % RING}"), 16 * (n // RING + 1))
                if n:
                    wt["owed"] += 1
                wt["n"] = n + 1
                return ring[:, n % RING, :]

            def mm(o, lhsT, rhs, start, stop, end=False, turn=False):
                ins = pe.matmul(o, lhsT, rhs, start=start, stop=stop, is_transpose=turn or None)
                if end:
                    ins.then_inc(sem("psum_filled"), 1)
                elif wt["owed"]:
                    wt["owed"] -= 1
                    ins.then_inc(sem("weight_free"), 1)

            def begin(key):
                b = before[ids[key]]
                if b is not None:
                    pe.wait_ge(sem("drained_by_" + drains[b]), freed_count[b])
                return bank(key)

            def columns(stage_name, n, rhs, width=P):
                for pair in range((n + 1) // 2):
                    b = begin((stage_name, pair))
                    for i in range(2 * pair, min(n, 2 * pair + 2)):
                        w = next_weights()
                        at = (i % 2) * S
                        for k in range(NK):
                            mm(b[0:width, at:at + S], w[:, k * width:(k + 1) * width], rhs[:, k, :], k == 0,
                               k == NK - 1, end=(k == NK - 1 and (i % 2 == 1 or i == n - 1)))

            def token_rows(stage_name, lhs, nk, n, parts):
                bs = [begin((stage_name, i)) for i in range(NT * len(parts))]
                per = max(1, SLOT // n)
                for k in range(nk):
                    if k % per == 0:
                        w = next_weights()
                    for t in range(NT):
                        for h, (lo, width) in enumerate(parts):
                            at = (k % per) * n + lo
                            mm(bs[t * len(parts) + h][:, 0:width], lhs[:, k, t * P:(t + 1) * P], w[:, at:at + width],
                               k == 0, k == nk - 1, end=k == nk - 1)

            def turn_tokens(stage_name, src, ready, count):
                for pair in range(4):
                    b = begin((stage_name, pair))
                    for i in range(2):
                        for t in range(NT):
                            if pair == 0 and i == 0:
                                pe.wait_ge(sem(ready), count[t])
                            k = 2 * pair + i
                            mm(b[:, (i * 2 + t) * P:(i * 2 + t + 1) * P], src[:, t, k * P:(k + 1) * P], ident,
                               True, True, end=(i == 1 and t == 1), turn=True)

            half = [(0, 512), (512, 512)]
            pe.sem_inc(sem("weight_free"), RING)
            pe.wait_ge(sem("memT_loaded"), 16)
            for l in range(2):
                columns(f"mem_k{l}", 2, memT)
                token_rows(f"mem_v{l}", memT, NK, 256, [(0, 256)])
            if on("z"):
                pe.wait_ge(sem("consts_loaded"), 16)
                turn_tokens("xT_mix", xn, "xn_ready", [1, 2])
                wait_drained(pe, ("xT_mix", 3))
                columns("xr", NK, xT)
                for n in "kv":
                    b = begin((n + "c", 0))
                    for g in range(GROUPS):
                        if g % 2 == 0:
                            w = next_weights()
                        for par in range(2):
                            for k in range(NK):
                                mm(b[par * HD:(par + 1) * HD, g * P:(g + 1) * P],
                                   w[:, k * P + (g % 2) * HD:k * P + (g % 2 + 1) * HD], xT[:, k, par::2],
                                   k == 0, k == NK - 1, end=(g == 3 and par == 1 and k == NK - 1))
                for stage_name in ("lru_r", "lru_i"):
                    w = next_weights()
                    if stage_name == "lru_r":
                        pe.wait_ge(sem("conv_done"), 1)
                    for pair in range(4):
                        b = begin((stage_name, pair))
                        for i in range(2):
                            j = 2 * pair + i
                            mm(b[:, i * S:(i + 1) * S], w[:, j * P:(j + 1) * P], xc[:, j, :], True, True, end=i == 1)
                columns("k_sel", 2, xT)
                columns("k_win", 2, xT)
                token_rows("v_sw", xT, NK, 512, [(0, 512)])
                w = next_weights()
                b = begin(("nsa_gate", 0))
                for t in range(NT):
                    for k in range(NK):
                        mm(b[:, t * 48:(t + 1) * 48], xT[:, k, t * P:(t + 1) * P], w[:, k * 48:(k + 1) * 48],
                           k == 0, k == NK - 1, end=(t == 1 and k == NK - 1))
                columns("q", NK, xT)
            if on("cmp"):
                for n in "kv":
                    bs = [begin(("hid_" + n, h)) for h in range(2)]
                    wait_drained(pe, (n + "c", 0))
                    for lp in range(16):
                        if lp % 4 == 0:
                            w = next_weights()
                        src = cmp_in[n][lp // 8].rearrange("p g (c l) -> p g c l", l=8)
                        rhs = src[:, :, lp // 8:lp // 8 + NCMP, lp % 8]
                        for h in range(2):
                            at = (lp % 4) * 256 + h * P
                            mm(bs[h][:, 0:4 * NCMP].rearrange("p (g c) -> p g c", g=4), w[:, at:at + P], rhs,
                               lp == 0, lp == 15, end=lp == 15)
                wait_drained(pe, ("hid_v", 1))
                b = begin(("k_cmp", 0))
                for s in range(2):
                    for h in range(2):
                        rhs = hidT["k"][:, h, :].rearrange("p (m s c) -> p s m c", m=2, s=2)[:, s]
                        mm(b[s * HD:(s + 1) * HD, 0:2 * NCMP].rearrange("p (m c) -> p m c", m=2), c("w2_k", 2, HD)[:, h, :],
                           rhs, h == 0, h == 1, end=(s == 1 and h == 1))
                b = begin(("v_cmp", 0))
                for g in range(GROUPS):
                    for h in range(2):
                        mm(b[0:NCMP, g * HD:(g + 1) * HD], hidT["v"][:, h, g * NCMP:(g + 1) * NCMP],
                           c("w2_v", 2, HD)[:, h, :], h == 0, h == 1, end=(g == 3 and h == 1))
                wait_drained(pe, ("k_cmp", 0))
                wait_drained(pe, ("q", 3))
                for t in range(NT):
                    for s in range(2):
                        b = begin(("cmp_score", 2 * t + s))
                        for j in range(NK):
                            mm(b[:, j * NCMP:(j + 1) * NCMP], qT[s * HD:(s + 1) * HD, j, t * P:(t + 1) * P],
                               k_cmp[s * HD:(s + 1) * HD, j // 4, :], True, True, end=j == NK - 1)
                for t in range(NT):
                    pe.wait_ge(sem("cmp_probs"), t + 1)
                    for q4 in range(4):
                        b = begin(("cmp_turn", t * 4 + q4))
                        for i in range(4):
                            mm(b[0:NCMP, i * P:(i + 1) * P], cmp_s[:, t, q4 * 4 + i, :], ident, True, True, end=i == 3,
                               turn=True)
            if on("att"):
                wait_drained(pe, ("v_cmp", 0))
                wait_drained(pe, ("cmp_turn", 7))
                for kind, u in attention_order():
                    b = begin(("att_" + kind, u))
                    if kind == "gate":
                        for i in range(2):
                            w = next_weights()
                            for k in range(NK):
                                mm(b[:, i * S:(i + 1) * S], w[:, k * P:(k + 1) * P], xT[:, k, :], k == 0, k == NK - 1,
                                   end=(i == 1 and k == NK - 1))
                        continue
                    j, s, t = UNITS[u]
                    m, nk = j // 4, (t + 1) * P
                    h64 = slice(s * HD, (s + 1) * HD)
                    if kind == "score":
                        for br in range(2):
                            mm(b[:, br * nk:(br + 1) * nk], qT[h64, j, t * P:(t + 1) * P], kT[br][h64, m, 0:nk],
                               True, True, end=br == 1)
                    if kind == "turn":
                        pe.wait_ge(sem("att_diag"), u + 1)
                        E = att_E[u % 3] if t else att_E0[u % 3]
                        for br in range(2):
                            for kb in range(t + 1):
                                mm(b[:, (br * (t + 1) + kb) * P:(br * (t + 1) + kb + 1) * P],
                                   E[:, br, kb * P:(kb + 1) * P], att_diag[u % 3][:, br, :], True, True,
                                   end=(br == 1 and kb == t))
                    if kind == "value":
                        wait_drained(pe, ("att_turn", u))
                        g = 2 * m + s
                        hd = 2 * j + s
                        mm(b[h64, 0:P], v_cmp[0:NCMP, g * HD:(g + 1) * HD], cmp_PT[0:NCMP, hd, t * P:(t + 1) * P],
                           True, False)
                        for br in range(2):
                            for kb in range(t + 1):
                                last = br == 1 and kb == t
                                at = br * 256 + g * HD
                                mm(b[h64, 0:P], v_sw[:, kb, at:at + HD], att_PT[u % 2][:, br * (t + 1) + kb, :],
                                   False, last, end=last)
            if on("mix"):
                pe.wait_ge(sem("y_ready"), 1)
                token_rows("mix_out", yT, NK, D, half)
            if on("ffn"):
                turn_tokens("xT_ffn", xn, "xn_ready", [3, 4])
                wait_drained(pe, ("xT_ffn", 3))
                down = [begin(("ffn_down", i)) for i in range(4)]
                for kind, f in ffn_order():
                    w = next_weights()
                    if kind == "gate":
                        b = begin(("ffn_gu", f))
                    if kind in ("gate", "up"):
                        at = S * (kind == "up")
                        for k in range(NK):
                            mm(b[:, at:at + S], w[:, k * P:(k + 1) * P], xT[:, k, :], k == 0, k == NK - 1,
                               end=(kind == "up" and k == NK - 1))
                    else:
                        wait_drained(pe, ("ffn_gu", f))
                        for t in range(NT):
                            for h in range(2):
                                mm(down[2 * t + h][:, :], act_T[f % 3][:, t * P:(t + 1) * P],
                                   w[:, h * 512:(h + 1) * 512], f == 0, f == NF - 1, end=f == NF - 1)
            if on("ple"):
                turn_tokens("xT_ple", x, "x_ready", [1, 2])
                wait_drained(pe, ("xT_ple", 3))
                token_rows("ple_gate", xT, NK, D, half)
                token_rows("ple_proj", c("pT", 2, S), 2, D, half)
            for l in range(2):
                if l == 0 and on("gla"):
                    turn_tokens("xT_in0", x, "x_ready", [3, 4])
                    wait_drained(pe, ("xT_in0", 3))
                    columns("gla_q", GH, xT, GDK)
                    columns("gla_k", GH, xT, GDK)
                    b = begin(("gla_g1", 0))
                    w = next_weights()
                    for k in range(NK):
                        mm(b[0:16, 0:S], w[:, k * 16:(k + 1) * 16], xT[:, k, :], k == 0, k == NK - 1, end=k == NK - 1)
                    wait_drained(pe, ("gla_g1", 0))
                    for pair in range(2):
                        b = begin(("gla_gate", pair))
                        for i in range(2):
                            h = 2 * pair + i
                            mm(b[0:GDK, i * S:(i + 1) * S], c("w_gate2")[0:16, h * GDK:(h + 1) * GDK], g1T[0:16, :],
                               True, True, end=i == 1)
                    columns("qm0", 2, xT)
                    parts = [(0, 384), (384, 384)]
                    token_rows("gla_v", xT, NK, GH * GDV, parts)
                    token_rows("gla_r", xT, NK, GH * GDV, parts)
                    pe.wait_ge(sem("gla_decayed"), 1)
                    for t in range(NT):
                        b = begin(("gla_kendT", t))
                        for h in range(GH):
                            mm(b[:, h * GDK:(h + 1) * GDK], gke[0:GDK, h, t * P:(t + 1) * P], ident[0:GDK, 0:GDK],
                               True, True, end=h == GH - 1, turn=True)
                    b = begin(("gla_intra", 0))
                    for n in range(NCH):
                        for h in range(GH):
                            o = (n % 2) * CH
                            mm(b[o:o + CH, (n // 2) * 256 + h * CH:(n // 2) * 256 + (h + 1) * CH],
                               gkt[0:GDK, h, n * CH:(n + 1) * CH], gq[0:GDK, h, n * CH:(n + 1) * CH], True, True,
                               end=(n == NCH - 1 and h == GH - 1))
                    wait_drained(pe, ("gla_kendT", 1))
                    wait_drained(pe, ("gla_v", 3))
                    for n in range(NCH - 1):
                        o = slice((n % 2) * CH, (n % 2 + 1) * CH)
                        for hp in range(2):
                            b = begin(("gla_kv", 2 * n + hp))
                            for i in range(2):
                                h = 2 * hp + i
                                mm(b[0:GDK, i * GDV:(i + 1) * GDV], kendT[o, n // 2, h, :],
                                   gv[o, n // 2, h * GDV:(h + 1) * GDV], True, True, end=i == 1)
                    wait_drained(pe, ("gla_intra", 0))
                    pe.wait_ge(sem("gla_state"), NCH - 1)
                    for t in range(NT):
                        for hp in range(2):
                            b = begin(("gla_o", 2 * t + hp))
                            for par in range(2):
                                n = 2 * t + par
                                o = slice(par * CH, (par + 1) * CH)
                                for i in range(2):
                                    h = 2 * hp + i
                                    vcol = slice(h * GDV, (h + 1) * GDV)
                                    last = par == 1 and i == 1
                                    mm(b[o, i * GDV:(i + 1) * GDV], attnT[o, t, h, :], gv[o, t, vcol], True, n == 0)
                                    if n:
                                        mm(b[o, i * GDV:(i + 1) * GDV], gq[0:GDK, h, n * CH:(n + 1) * CH],
                                           state[0:GDK, n - 1, vcol], False, True, end=last)
                    pe.wait_ge(sem("mix_ready"), 2)
                    for pair in range(3):
                        b = begin(("gla_mixT", pair))
                        for i in range(2):
                            for t in range(NT):
                                k = 2 * pair + i
                                mm(b[:, (i * 2 + t) * P:(i * 2 + t + 1) * P], mixin[:, t, k * P:(k + 1) * P], ident,
                                   True, True, end=(i == 1 and t == 1), turn=True)
                if l == 1 and on("dil"):
                    turn_tokens("xT_in1", x, "x_ready", [7, 8])
                    wait_drained(pe, ("xT_in1", 3))
                    columns("dil_k", DSLOTS, xT)
                    token_rows("dil_v", xT, NK, 768, [(0, 384), (384, 384)])
                    columns("dil_q", 18, xT)
                    columns("qm1", 2, xT)
                    wait_drained(pe, ("dil_q", 8))
                    for kind, u in pipelined(len(DIL_UNITS)):
                        s, t = DIL_UNITS[u]
                        nk = (t + 1) * P
                        if kind == "score":
                            for part in range(t + 1):
                                b = begin(("dil_score", 2 * u + part))
                                gs = [0, 1, 2] if t == 0 else ([0, 1] if part == 0 else [2])
                                for g in gs:
                                    at = (g - gs[0]) * nk
                                    mm(b[:, at:at + nk], dqT[:, s * 3 + g, t * P:(t + 1) * P], dkT[:, s, 0:nk], True,
                                       True, end=g == gs[-1])
                        if kind == "turn":
                            b = begin(("dil_turn", 2 * u))
                            pe.wait_ge(sem("dil_diag"), u + 1)
                            E = dil_E[u % 3] if t else dil_E0[u % 3]
                            for kb in range(t + 1):
                                for g in range(3):
                                    mm(b[:, kb * P:(kb + 1) * P], E[:, g, kb * P:(kb + 1) * P], dil_diag[u % 3],
                                       g == 0, g == 2, end=(kb == t and g == 2))
                        if kind == "value":
                            b = begin(("dil_value", 2 * u))
                            wait_drained(pe, ("dil_turn", 2 * u))
                            for kb in range(t + 1):
                                mm(b[:, 0:P], dv[:, kb, s * P:(s + 1) * P], dil_PT[u % 2][:, kb, :], kb == 0, kb == t,
                                   end=kb == t)
                if on(f"memat{l}"):
                    wait_drained(pe, (f"qm{l}", 0))
                    for kind, u in pipelined(len(MEM_UNITS)):
                        m, t = MEM_UNITS[u]
                        if kind == "score":
                            for s in range(2):
                                b = begin((f"mem_score{l}", 2 * u + s))
                                h64 = slice(s * HD, (s + 1) * HD)
                                mm(b[:, 0:S], qmT[h64, m, t * P:(t + 1) * P], mem_k[h64, l, m, :], True, True, end=True)
                            continue
                        b = begin((f"mem_{kind}{l}", 2 * u))
                        if kind == "turn":
                            pe.wait_ge(sem("mem_diag"), l * len(MEM_UNITS) + u + 1)
                            for s in range(2):
                                for kb in range(2):
                                    mm(b[:, (2 * s + kb) * P:(2 * s + kb + 1) * P], mem_E[u % 3][:, s, kb * P:(kb + 1) * P],
                                       mem_diag[u % 3][:, s, :], True, True, end=(s == 1 and kb == 1))
                        if kind == "value":
                            wait_drained(pe, (f"mem_turn{l}", 2 * u))
                            for s in range(2):
                                h64 = slice(s * HD, (s + 1) * HD)
                                for kb in range(2):
                                    at = (2 * m + s) * HD
                                    mm(b[h64, 0:P], mem_v[:, l, kb, at:at + HD], mem_PT[u % 2][:, 2 * s + kb, :],
                                       kb == 0, kb == 1, end=(s == 1 and kb == 1))
                if on(f"out{l}"):
                    wait_drained(pe, (f"mem_value{l}", 2 * len(MEM_UNITS) - 2))
                    if l == 0:
                        wait_drained(pe, ("gla_mixT", 2))
                    token_rows(f"out{l}", mixT, NK, D, half)
                if on(f"peer{l}"):
                    n0 = 5 + 4 * l
                    turn_tokens(f"xT_peer{l}", x, "x_ready", [n0, n0 + 1])
                    wait_drained(pe, (f"xT_peer{l}", 3))
                    for kind, h in peer_head_order():
                        key = (f"peer_{kind}{l}", h)
                        b = begin(key)
                        if kind == "q":
                            for q in range(2):
                                w = next_weights()
                                for k in range(NK):
                                    mm(b[:, q * S:(q + 1) * S], w[:, k * P:(k + 1) * P], xT[:, k, :], k == 0,
                                       k == NK - 1, end=(q == 1 and k == NK - 1))
                        else:
                            wait_drained(pe, (f"peer_q{l}", h))
                            for t in range(NT):
                                for q in range(2):
                                    mm(b[:, (2 * t + q) * P:(2 * t + q + 1) * P], pq[h % 2][:, q, t * P:(t + 1) * P],
                                       c("keysT", 2, 2, PN)[:, l, q, :], True, True, end=(t == 1 and q == 1))
            if dump is not None:
                pe.sem_inc(sem("dbg_pe"), 1)

        @block.sync
        def _(sp):
            sp.dma_start(x[:, :, :], x_in.rearrange("(t p) d -> p t d", p=P)).then_inc(sem("x_loaded"), 16)
            sp.dma_start(memT[:, :, :], memT_in.rearrange("(k p) s -> p k s", p=P)).then_inc(sem("memT_loaded"), 16)
            with sp.Fori(0, -(-wt["n"] // RING)) as i:
                for s in range(RING):
                    sp.wait_ge(sem("weight_free"), i * RING + (s + 1))
                    sp.dma_start(ring[:, s, :], weights[bass.ds(i * RING + s, 1), :, :].rearrange("a p n -> p (a n)"))\
                      .then_inc(sem(f"weight_loaded{s}"), 16)
            if dump is None:
                sp.wait_ge(sem("x_final"), NT)
                sp.dma_start(out.rearrange("(t p) d -> p t d", p=P), x[:, :, :]).then_inc(sem("stored"), 16)
                sp.wait_ge(sem("stored"), 16)
            else:
                for en in ("act", "dve", "pe", "pool"):
                    sp.wait_ge(sem("dbg_" + en), 1)
                sp.dma_start(out.rearrange("(t p) d -> p t d", p=P), x[:, :, :]).then_inc(sem("stored"), 16)
                sp.wait_ge(sem("stored"), 16)

        @block.scalar
        def _(act):
            done, settle, count = counter(act)

            def drain(key, pieces):
                wait_filled(act, key)
                for n, (o, i, f, kw) in enumerate(pieces):
                    last = n == len(pieces) - 1
                    done(act.activation(o, i, f, **kw), "drained_by_act" if last else "act_step")

            def two(src):
                return src.rearrange("p (a s) -> p a s", a=2)

            def root(o, i, scale, eps, name):
                settle()
                done(act.activation(o, i, ACT.Sqrt, bias=c("eps")[:, eps:eps + 1], scale=scale), name)

            def rms_of_x(first):
                for t in range(NT):
                    if first:
                        act.wait_ge(sem("x_loaded"), 16)
                        act.wait_ge(sem("consts_loaded"), 16)
                    done(act.activation(xn[:, t, :], x[:, t, :], ACT.Square, accum_out=stat[:, t:t + 1]), "act_step")
                    root(stat[:, 2 + t:3 + t], stat[:, t:t + 1], 1.0 / D, 0, "rms_ready")

            def squares_of_product(stage_name):
                for i in range(4):
                    wait_filled(act, (stage_name, i))
                    t, h = i // 2, i % 2
                    done(act.activation(tmp_tok[:, t, h * 512:(h + 1) * 512], bank((stage_name, i))[:, :], ACT.Square,
                                        accum_out=stat[:, 8 + i:9 + i]), "post_squares")

            def softmax_unit(nm_sem, n, parts, exp_sem):
                act.wait_ge(sem(nm_sem), n)
                for k, (tile, nm, total) in enumerate(parts):
                    last = k == len(parts) - 1
                    done(act.activation(tile, tile, ACT.Exp, bias=nm, accum_out=total), exp_sem if last else "act_step")

            rms_of_x(True)
            for l in range(2):
                drain((f"mem_k{l}", 0), [(mem_k[:, l, :, :], two(bank((f"mem_k{l}", 0))[:, :]), ACT.Copy, {})])
                for mt in range(2):
                    key = (f"mem_v{l}", mt)
                    drain(key, [(mem_v[:, l, mt, :], bank(key)[:, 0:256], ACT.Copy, {})])
            if on("z"):
                act.wait_ge(sem("lam_abs"), 1)
                done(act.activation(lam_t[:, 1, :], lam_t[:, 0, :], ACT.Exp, scale=-1.0), "lam_exp")
                act.wait_ge(sem("lam_w"), 1)
                done(act.activation(lam_t[:, 3, :], lam_t[:, 2, :], ACT.Ln), "lam_ln")
                for i in range(4):
                    act.wait_ge(sem("pad_zeroed"), 1)
                    drain(("xr", i), [(xr_pad[:, 2 * i:2 * i + 2, 3:], two(bank(("xr", i))[:, :]), ACT.Copy, {})])
                for name, dst, bias in (("lru_r", lru_a, "lru_ba"), ("lru_i", lru_i, "lru_bx")):
                    for i in range(4):
                        b = bank((name, i))
                        drain((name, i), [(dst[:, 2 * i + h, :], b[:, h * S:(h + 1) * S], ACT.Sigmoid,
                                           dict(bias=c(bias)[:, 2 * i + h:2 * i + h + 1])) for h in range(2)])
                for n, br in (("k_sel", 0), ("k_win", 1)):
                    drain((n, 0), [(kT[br][:, :, :], two(bank((n, 0))[:, :]), ACT.Copy, {})])
                for t in range(NT):
                    drain(("v_sw", t), [(v_sw[:, t, :], bank(("v_sw", t))[:, :], ACT.Copy, {})])
                drain(("nsa_gate", 0), [(nsa_g.rearrange("p t b h -> p (t b h)"), bank(("nsa_gate", 0))[:, 0:96],
                                         ACT.Sigmoid, {})])
                for i in range(4):
                    drain(("q", i), [(qT[:, 2 * i:2 * i + 2, :], two(bank(("q", i))[:, :]), ACT.Copy,
                                      dict(scale=HD ** -0.5))])
                act.wait_ge(sem("lam_rate"), 1)
                settle()
                for j in range(NK):
                    done(act.activation(lru_t[:, j, :], lru_a[:, j, :], ACT.Tanh, scale=lam_t[:, 8, j:j + 1]), "lru_tanh")
                settle()
                for j in range(NK):
                    done(act.activation(lru_a[:, j, :], lru_a[:, j, :], ACT.Exp, scale=lam_t[:, 9, j:j + 1]), "lru_exp")
                act.wait_ge(sem("lru_b2"), 1)
                done(act.activation(lru_t.rearrange("p a s -> p (a s)"), lru_t.rearrange("p a s -> p (a s)"), ACT.Sqrt,
                                    scale=2.0), "lru_root")
            if on("cmp"):
                for n in "kv":
                    for h in range(2):
                        key = ("hid_" + n, h)
                        drain(key, [(hidT[n][:, h, :], bank(key)[:, 0:4 * NCMP], ACT.Gelu_apprx_tanh, {})])
                for t in range(NT):
                    act.wait_ge(sem("cmp_shifted"), t + 1)
                    v = cmp_s[:, t].rearrange("p h c -> p (h c)")
                    done(act.activation(v, v, ACT.Exp), "cmp_exp")
                for i in range(8):
                    key = ("cmp_turn", i)
                    t, q4 = i // 4, i % 4
                    act.wait_ge(sem("lru_scanned"), 1)
                    drain(key, [(cmp_PT[0:NCMP, q4 * 4:q4 * 4 + 4, t * P:(t + 1) * P],
                                 bank(key)[0:NCMP, :].rearrange("p (a s) -> p a s", a=4), ACT.Copy, {})])
            if on("att"):
                for kind, u in attention_order():
                    key = ("att_" + kind, u)
                    b = bank(key)
                    if kind == "score":
                        E = att_E[u % 3] if UNITS[u][2] else att_E0[u % 3]
                        softmax_unit("att_max", u + 1, [(E[:, br, :], att_nm[:, u % 3, br:br + 1],
                                                         att_sum[:, u % 3, br:br + 1]) for br in range(2)], "att_exp")
                    if kind == "gate":
                        dst, f = [(gma, ACT.Sigmoid), (gr, ACT.Gelu_apprx_tanh), (gmr, ACT.Sigmoid)][u // 4]
                        i = u % 4
                        drain(key, [(dst[:, 2 * i:2 * i + 2, :], two(b[:, :]), f, {})])
                    if kind == "turn":
                        n = 2 * (UNITS[u][2] + 1)
                        drain(key, [(att_PT[u % 2][:, 0:n, :], b[:, 0:n * P].rearrange("p (a s) -> p a s", a=n), ACT.Copy,
                                     {})])
            if on("mix"):
                squares_of_product("mix_out")
                for t in range(NT):
                    act.wait_ge(sem("post_sum"), t + 1)
                    root(stat[:, 16 + t:17 + t], stat[:, 12 + t:13 + t], 1.0 / D, 0, "post_rms")
            if on("ffn"):
                for t in range(NT):
                    act.wait_ge(sem("x_mixed"), t + 1)
                    done(act.activation(xn[:, t, :], x[:, t, :], ACT.Square, accum_out=stat[:, t:t + 1]), "act_step")
                    root(stat[:, 2 + t:3 + t], stat[:, t:t + 1], 1.0 / D, 0, "rms_ready")
                for f in range(NF):
                    wait_filled(act, ("ffn_gu", f))
                    if f >= 2:
                        wait_drained(act, ("ffn_gu", f - 2))
                    done(act.activation(gate_s[f % 2], bank(("ffn_gu", f))[:, 0:S], ACT.Silu), "ffn_silu")
                squares_of_product("ffn_down")
                for t in range(NT):
                    act.wait_ge(sem("post_sum"), NT + t + 1)
                    root(stat[:, 16 + t:17 + t], stat[:, 12 + t:13 + t], 1.0 / D, 0, "post_rms")
            if on("ple"):
                for i in range(4):
                    t, h = i // 2, i % 2
                    act.wait_ge(sem("ple_biased"), i + 1)
                    v = tmp_tok[:, t, h * 512:(h + 1) * 512]
                    done(act.activation(v, v, ACT.Sigmoid), "ple_sigmoid")
            if on("gla"):
                for name, dst, scale in (("gla_q", gq, GDK ** -0.5), ("gla_k", gk, 1.0)):
                    for i in range(2):
                        drain((name, i), [(dst[0:GDK, 2 * i:2 * i + 2, :], two(bank((name, i))[0:GDK, :]), ACT.Copy,
                                           dict(scale=scale))])
                drain(("gla_g1", 0), [(g1T[0:16, :], bank(("gla_g1", 0))[0:16, 0:S], ACT.Copy, {})])
                act.wait_ge(sem("gla_abs"), 1)
                done(act.activation(ge[0:GDK], ge[0:GDK], ACT.Exp, scale=-1.0), "act_step")
                settle()
                done(act.activation(ge[0:GDK], ge[0:GDK], ACT.Ln, bias=c("eps")[0:GDK, 2:3]), "gla_softplus")
                drain(("qm0", 0), [(qmT[:, :, :], two(bank(("qm0", 0))[:, :]), ACT.Copy, dict(scale=HD ** -0.5))])
                act.wait_ge(sem("gla_cumsum"), 1)
                done(act.activation(geb[0:GDK], gb[0:GDK], ACT.Exp), "gla_exp")
                done(act.activation(gf[0:GDK], gb[0:GDK], ACT.Exp, scale=-1.0), "gla_exp")
                act.wait_ge(sem("gla_tail"), 1)
                done(act.activation(gt[0:GDK], gt[0:GDK], ACT.Exp), "gla_exp")
                for name, dst, f in (("gla_v", gv, ACT.Copy), ("gla_r", grs, ACT.Silu)):
                    for i in range(4):
                        t, h = i // 2, i % 2
                        drain((name, i), [(dst[:, t, h * 384:(h + 1) * 384], bank((name, i))[:, 0:384], f, {})])
                for i in range(4):
                    wait_filled(act, ("gla_o", i))
                    for h in range(2):
                        col = 20 + 2 * i + h
                        done(act.activation(tmp_sq[:, 0:GDV], bank(("gla_o", i))[:, h * GDV:(h + 1) * GDV], ACT.Square,
                                            accum_out=stat[:, col:col + 1]), "act_step")
                        settle()
                root(stat[:, 32:40], stat[:, 20:28], 1.0 / GDV, 0, "gla_rms")
                for pair in range(3):
                    key = ("gla_mixT", pair)
                    drain(key, [(mixT[:, 2 * pair:2 * pair + 2, :], two(bank(key)[:, :]), ACT.Copy, {})])
            for l in range(2):
                if l == 1 and on("dil"):
                    for i in range(3):
                        drain(("dil_k", i), [(dkT[:, 2 * i:2 * i + 2, :], two(bank(("dil_k", i))[:, :]), ACT.Copy, {})])
                    for i in range(4):
                        t, h = i // 2, i % 2
                        drain(("dil_v", i), [(dv[:, t, h * 384:(h + 1) * 384], bank(("dil_v", i))[:, 0:384], ACT.Copy, {})])
                    for i in range(9):
                        drain(("dil_q", i), [(dqT[:, 2 * i:2 * i + 2, :], two(bank(("dil_q", i))[:, :]), ACT.Copy, {})])
                    drain(("qm1", 0), [(qmT[:, :, :], two(bank(("qm1", 0))[:, :]), ACT.Copy, dict(scale=HD ** -0.5))])
                    for kind, u in pipelined(len(DIL_UNITS)):
                        t = DIL_UNITS[u][1]
                        if kind == "score":
                            E = (dil_E[u % 3] if t else dil_E0[u % 3]).rearrange("p g k -> p (g k)")
                            softmax_unit("dil_max", u + 1, [(E, att_nm[:, u % 3, 0:1], att_sum[:, u % 3, 0:1])], "dil_exp")
                        if kind == "turn":
                            key = ("dil_turn", 2 * u)
                            n = t + 1
                            drain(key, [(dil_PT[u % 2][:, 0:n, :], bank(key)[:, 0:n * P].rearrange("p (a s) -> p a s", a=n),
                                         ACT.Copy, {})])
                if on(f"memat{l}"):
                    for kind, u in pipelined(len(MEM_UNITS)):
                        key = (f"mem_{kind}{l}", 2 * u)
                        if kind == "score":
                            softmax_unit("mem_max", l * len(MEM_UNITS) + u + 1,
                                         [(mem_E[u % 3][:, s, :], att_nm[:, u % 3, s:s + 1], att_sum[:, u % 3, s:s + 1])
                                          for s in range(2)], "mem_exp")
                        if kind == "turn":
                            drain(key, [(mem_PT[u % 2][:, :, :], bank(key)[:, :].rearrange("p (a s) -> p a s", a=4),
                                         ACT.Copy, {})])
                if on(f"out{l}"):
                    for t in range(NT):
                        act.wait_ge(sem("ln_var"), l * 2 * NT + t + 1)
                        root(stat[:, 50 + t:51 + t], stat[:, 43 + 2 * t:44 + 2 * t], 1.0, 1, "ln_std")
                if on(f"peer{l}"):
                    for kind, h in peer_head_order():
                        key = (f"peer_{kind}{l}", h)
                        if kind == "q":
                            drain(key, [(pq[h % 2], two(bank(key)[:, :]), ACT.Copy, {})])
                        else:
                            drain(key, [(sc[t][:, 2 * h:2 * h + 2, :],
                                         bank(key)[:, t * 2 * P:(t + 1) * 2 * P].rearrange("p (a s) -> p a s", a=2),
                                         ACT.Copy, {}) for t in range(NT)])
                    for t in range(NT):
                        act.wait_ge(sem("peer_shifted"), (l * NT + t + 1) * TURNS)
                        v = gate_w[t].rearrange("p h k -> p (h k)")
                        done(act.activation(v, v, ACT.Exp), "peer_exp")
                        act.wait_ge(sem("peer_dots"), l * NT + t + 1)
                        done(act.activation(hdot[t], hdot[t], ACT.Gelu), "peer_gelu")
                        act.wait_ge(sem("ln_var"), (l * 2 + 1) * NT + t + 1)
                        root(stat[:, 50 + t:51 + t], stat[:, 43 + 2 * t:44 + 2 * t], 1.0, 1, "ln_std")
            if dump is not None:
                settle()
                act.sem_inc(sem("dbg_act"), 1)

        @block.gpsimd
        def _(pool):
            pool.dma_start(cst[:, :], consts).then_inc(sem("consts_loaded"), 16)

            def load_row(n):
                pool.dma_start(rows[:, n % NROW, :], rows_in[n:n + 1, :].to_broadcast([P, D]))\
                    .then_inc(sem(f"row_loaded{n % NROW}"), 16)

            for n in range(NROW):
                load_row(n)
            if on("peer0"):
                for n in range(NROW, len(ROWS)):
                    pool.wait_ge(sem("rows_used"), n - NROW + 1)
                    load_row(n)
            n = 0
            for l in range(2):
                if not on(f"peer{l}"):
                    continue
                for kind, t in PASSES:
                    table = peer_u if kind == "u" else peer_v
                    with pool.Fori(0, TURNS) as i:
                        pool.wait_ge(sem("peer_experts"), i + ((l * NT + t) * TURNS + 1))
                        for h in range(2):
                            pool.tensor_copy(stage[:, h * 16:(h + 1) * 16].bitcast(U32),
                                             expert[t][:, bass.ds(i * BODY + h * 16, 16)].bitcast(U32))\
                                .then_inc(sem("indices_staged"), 1)
                            pool.wait_ge(sem("indices_staged"), i * 2 + (n * TURNS * 2 + h + 1))
                            for k in range(16):
                                s = h * 16 + k
                                pool.wait_ge(sem("gather_free"), i * BODY + (n * P + s + 1))
                                pool.sem_inc(sem("gather_turn"), 1)
                                pool.indirect_dma_start(gbuf[s % GBUF], None, table, bass.IndirectOffsetOnAxis(
                                    ap=stage[:, s:s + 1].bitcast(U32), axis=0)).then_inc(sem(f"gathered{s % GBUF}"), 16)
                    n += 1
            if dump is not None:
                pool.sem_inc(sem("dbg_pool"), 1)

        @block.vector
        def _(dve):
            done, settle, count = counter(dve)

            def step(ins, name="dve_step"):
                done(ins, name)
                settle()

            def row(n):
                dve.wait_ge(sem(f"row_loaded{n % NROW}"), 16 * (n // NROW + 1))
                return rows[:, n % NROW, :]

            def turned(stage_name, gain=None):
                for pair in range(4):
                    key = (stage_name, pair)
                    wait_filled(dve, key)
                    src = bank(key)[:, :].rearrange("p (a s) -> p a s", a=2)
                    dst = xT[:, 2 * pair:2 * pair + 2, :]
                    if gain is None:
                        done(dve.tensor_copy(dst, src), "drained_by_dve")
                    else:
                        g = c(gain)[:, 2 * pair:2 * pair + 2].unsqueeze(2).to_broadcast([P, 2, S])
                        done(dve.tensor_tensor(dst, src, g, ALU.mult), "drained_by_dve")

            def normalised_x(first):
                for t in range(NT):
                    dve.wait_ge(sem("rms_ready"), first + t + 1)
                    step(dve.reciprocal(stat[:, 4 + t:5 + t], stat[:, 2 + t:3 + t]))
                    step(dve.tensor_scalar(xn[:, t, :], x[:, t, :], stat[:, 4 + t:5 + t], None, ALU.mult), "xn_ready")

            def post_norm(stage_name, first, g, name):
                gain = row(g)
                for t in range(NT):
                    dve.wait_ge(sem("post_squares"), 2 * first + 2 * t + 2)
                    step(dve.tensor_tensor(stat[:, 12 + t:13 + t], stat[:, 8 + 2 * t:9 + 2 * t],
                                           stat[:, 9 + 2 * t:10 + 2 * t], ALU.add), "post_sum")
                for t in range(NT):
                    dve.wait_ge(sem("post_rms"), first + t + 1)
                    step(dve.reciprocal(stat[:, 18 + t:19 + t], stat[:, 16 + t:17 + t]))
                    for h in range(2):
                        key = (stage_name, 2 * t + h)
                        cols = slice(h * 512, (h + 1) * 512)
                        step(dve.scalar_tensor_tensor(tmp_tok[:, t, cols], bank(key)[:, :], stat[:, 18 + t:19 + t],
                                                      gain[:, cols], ALU.mult, ALU.mult), "drained_by_dve")
                    step(dve.tensor_tensor(x[:, t, :], x[:, t, :], tmp_tok[:, t, :], ALU.add), name)
                dve.sem_inc(sem("rows_used"), 1)

            def layer_norm(n, g, b, name, tiles=(0, 1)):
                stats = peer_st
                for t in tiles:
                    for h in range(2):
                        done(dve.bn_stats(stats[:, 12 * t + 6 * h:12 * t + 6 * h + 6], x[:, t, h * 512:(h + 1) * 512]),
                             "dve_step")
                settle()
                for t in tiles:
                    step(dve.bn_aggr(stat[:, 42 + 2 * t:44 + 2 * t], stats[:, 12 * t:12 * t + 12]), "ln_var")
                gain, bias = row(g), row(b)
                for t in tiles:
                    dve.wait_ge(sem("ln_std"), n * NT + t + 1)
                    step(dve.reciprocal(stat[:, 54 + t:55 + t], stat[:, 50 + t:51 + t]))
                    step(dve.tensor_scalar(x[:, t, :], x[:, t, :], stat[:, 42 + 2 * t:43 + 2 * t], stat[:, 54 + t:55 + t],
                                           ALU.subtract, ALU.mult))
                    step(dve.tensor_tensor(x[:, t, :], x[:, t, :], gain, ALU.mult))
                    step(dve.tensor_tensor(x[:, t, :], x[:, t, :], bias, ALU.add), name)
                if tiles[-1] == NT - 1:
                    dve.sem_inc(sem("rows_used"), 2)

            def row_max(E, nm, name):
                step(dve.tensor_reduce(nm, E, AX, ALU.max, negate=True), name)

            def route(l, t, g):
                lowest = -3.0e38
                hs = slice(g * TH, (g + 1) * TH)
                wait_drained(dve, (f"peer_s{l}", (g + 1) * TH - 1))

                def sixteen(n, val, pos, width):
                    src = sc[t][:, 2 * TH * g:2 * TH * (g + 1), :].rearrange("p a n -> p (a n)")\
                        .rearrange("p (a n) -> p a n", n=width)
                    left = rest.rearrange("p (a n) -> p a n", n=width)
                    for r in range(n):
                        done(dve.max(val[:, r, 0:8], src[:, r, :]), "dve_step")
                    settle()
                    for r in range(n):
                        done(dve.match_replace(left[:, r, :], val[:, r, 0:8], src[:, r, :], lowest), "dve_step")
                    for r in range(n):
                        done(dve.max_index(pos[:, r, 0:8].bitcast(U32), val[:, r, 0:8], src[:, r, :]), "dve_step")
                    settle()
                    for r in range(n):
                        done(dve.max(val[:, r, 8:16], left[:, r, :]), "dve_step")
                    settle()
                    for r in range(n):
                        done(dve.max_index(pos[:, r, 8:16].bitcast(U32), val[:, r, 8:16], left[:, r, :]), "dve_step")
                    settle()

                sixteen(2 * TH, top_v, top_i, PN)
                done(dve.tensor_copy(top_f, top_i.bitcast(U32)), "dve_step")
                grid = [P, TH, PK, PK]
                cand = sc[t][:, 2 * TH * g:2 * TH * (g + 1), :].rearrange("p a n -> p (a n)")\
                    .rearrange("p (h a b) -> p h a b", h=TH, a=PK)
                tv = top_v.rearrange("p (h q) k -> p h q k", q=2)
                step(dve.tensor_tensor(cand, tv[:, :, 0, :].unsqueeze(3).to_broadcast(grid),
                                       tv[:, :, 1, :].unsqueeze(2).to_broadcast(grid), ALU.add))
                sixteen(TH, best_v, best_j, PK * PK)
                done(dve.tensor_tensor(gate_w[t][:, hs, :], best_v, best_v[:, :, 0:1].to_broadcast([P, TH, PK]),
                                       ALU.subtract), "peer_shifted")
                tf = top_f.rearrange("p (h q) k -> p h q k", q=2)
                for q, (pos, sel) in enumerate(((pos_a, sel_a), (pos_b, sel_b))):
                    op, val = (ALU.logical_shift_right, 4) if q == 0 else (ALU.bitwise_and, 15)
                    step(dve.tensor_scalar(pos_u.bitcast(U32), best_j.bitcast(U32), val, None, op))
                    step(dve.tensor_copy(pos, pos_u.bitcast(U32)))
                    iota = c("iota").unsqueeze(1).to_broadcast([P, TH * PK, PK])
                    oh = onehot.rearrange("p h k c -> p (h k) c")
                    step(dve.tensor_tensor(oh, iota, pos.rearrange("p h k -> p (h k)").unsqueeze(2)
                                           .to_broadcast([P, TH * PK, PK]), ALU.is_equal))
                    step(dve.tensor_tensor(onehot, onehot, tf[:, :, q, :].unsqueeze(2).to_broadcast(grid), ALU.mult))
                    step(dve.tensor_reduce(sel.rearrange("p h k -> p (h k)"), oh, AX, ALU.add))
                step(dve.tensor_scalar(sel_a, sel_a, float(PN), float(l * EXPERTS), ALU.mult, ALU.add))
                step(dve.tensor_tensor(expert[t][:, g * BODY:(g + 1) * BODY].bitcast(U32),
                                       sel_a.rearrange("p h k -> p (h k)"), sel_b.rearrange("p h k -> p (h k)"),
                                       ALU.add), "peer_experts")

            def slot_in(weights_of, g, i, s):
                return weights_of[:, bass.ds(i * BODY + (g * BODY + s), 1)]

            def landed(l, t, kind, g, i, s):
                n = ((l * NT + t) * 2 + kind) * P + g * BODY + s
                dve.wait_ge(sem(f"gathered{s % GBUF}"), i * (16 * BODY // GBUF) + 16 * (n // GBUF + 1))

            def dots(l, t, g, i):
                for s in range(BODY):
                    rows_of = gbuf[s % GBUF]
                    landed(l, t, 0, g, i, s)
                    dve.scalar_tensor_tensor(rows_of, rows_of, 1.0, x[:, t, :], ALU.mult, ALU.mult,
                                             accum_out=slot_in(hdot[t], g, i, s)).then_inc(sem("gather_free"), 1)

            def sums(l, t, g, i):
                n = (l * NT + t) * 2 * P + P + g * BODY
                for s in range(BODY):
                    landed(l, t, 1, g, i, s)
                    dve.wait_ge(sem("gather_free"), i * BODY + (n + s + GBUF - 1))
                    dve.scalar_tensor_tensor(acc[s % 2], gbuf[s % GBUF], slot_in(hdot[t], g, i, s), acc[s % 2],
                                             ALU.mult, ALU.add).then_inc(sem("gather_free"), 1)

            dve.wait_ge(sem("consts_loaded"), 16)
            normalised_x(0)
            if on("z"):
                done(dve.memset(xr_pad[:, :, 0:3], 0.0), "pad_zeroed")
                lam = c("lam")
                step(dve.tensor_scalar(lam_t[:, 4, :], lam, -1.0, None, ALU.mult))
                step(dve.tensor_tensor(lam_t[:, 0, :], lam, lam_t[:, 4, :], ALU.max), "lam_abs")
                dve.wait_ge(sem("lam_exp"), 1)
                step(dve.tensor_scalar(lam_t[:, 2, :], lam_t[:, 1, :], 1.0, None, ALU.add), "lam_w")
                step(dve.tensor_scalar(lam_t[:, 5, :], lam_t[:, 2, :], -1.0, None, ALU.add))
                step(dve.tensor_scalar(lam_t[:, 6, :], lam_t[:, 5, :], 0.0, None, ALU.is_equal))
                step(dve.tensor_tensor(lam_t[:, 5, :], lam_t[:, 5, :], lam_t[:, 6, :], ALU.add))
                step(dve.reciprocal(lam_t[:, 5, :], lam_t[:, 5, :]))
                dve.wait_ge(sem("lam_ln"), 1)
                step(dve.tensor_tensor(lam_t[:, 6, :], lam_t[:, 3, :], lam_t[:, 6, :], ALU.add))
                step(dve.tensor_tensor(lam_t[:, 6, :], lam_t[:, 6, :], lam_t[:, 1, :], ALU.mult))
                step(dve.tensor_tensor(lam_t[:, 6, :], lam_t[:, 6, :], lam_t[:, 5, :], ALU.mult))
                step(dve.tensor_scalar(lam_t[:, 4, :], lam_t[:, 4, :], 0.0, None, ALU.max))
                step(dve.tensor_tensor(lam_t[:, 4, :], lam_t[:, 4, :], lam_t[:, 6, :], ALU.add))
                step(dve.tensor_scalar(lam_t[:, 8, :], lam_t[:, 4, :], 8.0, None, ALU.mult))
                step(dve.tensor_scalar(lam_t[:, 9, :], lam_t[:, 4, :], -8.0, None, ALU.mult), "lam_rate")
                turned("xT_mix", "g_mix")
                wait_drained(dve, ("xr", 3))
                cw = c("conv_w", 4, NK)
                for k in range(4):
                    for j in range(NK):
                        src = xr_pad[:, j, k:k + S]
                        if k == 0:
                            done(dve.tensor_scalar(xc[:, j, :], src, cw[:, k, j:j + 1], c("conv_b")[:, j:j + 1],
                                                   ALU.mult, ALU.add), "dve_step")
                        else:
                            done(dve.scalar_tensor_tensor(xc[:, j, :], src, cw[:, k, j:j + 1], xc[:, j, :], ALU.mult,
                                                          ALU.add), "dve_step")
                    settle()
                dve.sem_inc(sem("conv_done"), 1)
                for n in "kv":
                    key = (n + "c", 0)
                    wait_filled(dve, key)
                    src = bank(key)[:, :].rearrange("p (a l) -> p a l", l=8)
                    for h in range(2):
                        pos = c("pos_" + n)[:, h * 8:(h + 1) * 8].unsqueeze(1).to_broadcast([P, 64, 8])
                        done(dve.tensor_tensor(cmp_in[n][h].rearrange("p g (c l) -> p (g c) l", l=8), src, pos, ALU.add),
                             "drained_by_dve" if h else "dve_step")
            if on("lru"):
                flat = [v.rearrange("p a s -> p (a s)") for v in (lru_t, lru_i, xc, lru_a)]
                wait_drained(dve, ("lru_i", 3))
                step(dve.tensor_tensor(flat[1], flat[1], flat[2], ALU.mult))
                dve.wait_ge(sem("lru_tanh"), NK)
                step(dve.tensor_scalar(flat[2], flat[0], 1.0, None, ALU.add))
                step(dve.reciprocal(flat[2], flat[2]))
                step(dve.tensor_tensor(flat[0], flat[0], flat[2], ALU.mult), "lru_b2")
                dve.wait_ge(sem("lru_root"), 1)
                step(dve.tensor_tensor(flat[1], flat[1], flat[0], ALU.mult))
                dve.wait_ge(sem("lru_exp"), NK)
                for j in range(NK):
                    done(dve.tensor_tensor_scan(xc[:, j, :], lru_a[:, j, :], lru_i[:, j, :], 0.0, ALU.mult, ALU.add),
                         "dve_step")
                settle()
                dve.sem_inc(sem("lru_scanned"), 1)
            if on("cmp"):
                wait_filled(dve, ("k_cmp", 0))
                step(dve.tensor_copy(k_cmp[:, :, :].rearrange("p m c -> p (m c)"), bank(("k_cmp", 0))[:, 0:2 * NCMP]),
                     "drained_by_dve")
                wait_filled(dve, ("v_cmp", 0))
                step(dve.tensor_copy(v_cmp[0:NCMP, :], bank(("v_cmp", 0))[0:NCMP, 0:256]), "drained_by_dve")
                wait_drained(dve, ("nsa_gate", 0))
                bias = c("cmp_bias", NT * NK, 2, NCMP)
                mask = c("cmp_mask", NT, NCMP)
                full = [P, HEADS, NCMP]
                for t in range(NT):
                    s, st = cmp_s[:, t], cmp_st[:, t]
                    for h in range(2):
                        key = ("cmp_score", 2 * t + h)
                        wait_filled(dve, key)
                        done(dve.tensor_tensor(s.rearrange("p (j h) c -> p h j c", h=2)[:, h],
                                               bank(key)[:, 0:NK * NCMP].rearrange("p (j c) -> p j c", j=NK),
                                               bias[:, t * NK:(t + 1) * NK, h, :], ALU.add), "drained_by_dve")
                    settle()
                    step(dve.tensor_reduce(st[:, 0, :], s, AX, ALU.max))
                    step(dve.tensor_tensor(s, s, st[:, 0, :].unsqueeze(2).to_broadcast(full), ALU.subtract), "cmp_shifted")
                for t in range(NT):
                    s, st = cmp_s[:, t], cmp_st[:, t]
                    dve.wait_ge(sem("cmp_exp"), t + 1)
                    step(dve.tensor_tensor(s, s, mask[:, t, :].unsqueeze(1).to_broadcast(full), ALU.mult))
                    step(dve.tensor_reduce(st[:, 1, :], s, AX, ALU.add))
                    step(dve.tensor_scalar(st[:, 1, :], st[:, 1, :], 1e-30, None, ALU.max))
                    step(dve.reciprocal(st[:, 2, :], st[:, 1, :]))
                    step(dve.tensor_tensor(st[:, 2, :], st[:, 2, :], nsa_g[:, t, 0, :], ALU.mult))
                    step(dve.tensor_tensor(s, s, st[:, 2, :].unsqueeze(2).to_broadcast(full), ALU.mult), "cmp_probs")
            if on("att"):
                def normaliser(u):
                    j, s, t = UNITS[u]
                    dve.wait_ge(sem("att_exp"), u + 1)
                    r = att_rec[:, u % 3, :]
                    step(dve.reciprocal(r, att_sum[:, u % 3, :]))
                    step(dve.tensor_tensor(r, r, nsa_g[:, t, 1:3, 2 * j + s], ALU.mult))
                    for br in range(2):
                        done(dve.tensor_scalar(att_diag[u % 3][:, br, :], ident, r[:, br:br + 1], None, ALU.mult),
                             "att_diag" if br else "dve_step")
                        if br == 0:
                            settle()

                nd = c("neg_dist")
                for kind, u in attention_order():
                    key = ("att_" + kind, u)
                    if kind == "gate":
                        continue
                    j, s, t = UNITS[u]
                    if kind == "score":
                        wait_filled(dve, key)
                        nk = (t + 1) * P
                        E = att_E[u % 3] if t else att_E0[u % 3]
                        bias = nd[:, S - nk:S].unsqueeze(1).to_broadcast([P, 2, nk])
                        step(dve.scalar_tensor_tensor(E, bias, SLOPES[2 * j + s],
                                                      bank(key)[:, 0:2 * nk].rearrange("p (b k) -> p b k", b=2),
                                                      ALU.mult, ALU.add), "drained_by_dve")
                        row_max(E, att_nm[:, u % 3, :], "att_max")
                        if u:
                            normaliser(u - 1)
                        if u == len(UNITS) - 1:
                            normaliser(u)
                    if kind == "value":
                        wait_filled(dve, key)
                        wait_drained(dve, ("att_gate", j // 2))
                        h64 = slice(s * HD, (s + 1) * HD)
                        cols = slice(t * P, (t + 1) * P)
                        done(dve.tensor_tensor(yT[h64, j, cols], bank(key)[h64, 0:P], gma[h64, j, cols], ALU.mult),
                             "drained_by_dve")
                wait_drained(dve, ("att_gate", NZ - 1))
                settle()
                fl = [v.rearrange("p a s -> p (a s)") for v in (xc, gr, gmr, yT)]
                step(dve.tensor_tensor(fl[0], fl[0], fl[1], ALU.mult))
                step(dve.tensor_tensor(fl[0], fl[0], fl[2], ALU.mult))
                step(dve.tensor_tensor(fl[3], fl[3], fl[0], ALU.add), "y_ready")
            if on("mix"):
                post_norm("mix_out", 0, 0, "x_mixed")
            if on("ffn"):
                normalised_x(NT)
                turned("xT_ffn", "g_ffn")
                for f in range(NF):
                    dve.wait_ge(sem("ffn_silu"), f + 1)
                    if f >= 3:
                        pass
                    done(dve.tensor_tensor(act_T[f % 3], gate_s[f % 2], bank(("ffn_gu", f))[:, S:2 * S], ALU.mult),
                         "drained_by_dve")
                post_norm("ffn_down", NT, 1, "x_ready")
            if on("ple"):
                turned("xT_ple")
                bias = row(2)
                for i in range(4):
                    t, cols = i // 2, slice((i % 2) * 512, (i % 2 + 1) * 512)
                    wait_filled(dve, ("ple_gate", i))
                    done(dve.tensor_tensor(tmp_tok[:, t, cols], bank(("ple_gate", i))[:, :], bias[:, cols], ALU.add),
                         "drained_by_dve")
                    settle()
                    dve.sem_inc(sem("ple_biased"), 1)
                dve.sem_inc(sem("rows_used"), 1)
                for i in range(4):
                    t, cols = i // 2, slice((i % 2) * 512, (i % 2 + 1) * 512)
                    wait_filled(dve, ("ple_proj", i))
                    dve.wait_ge(sem("ple_sigmoid"), i + 1)
                    step(dve.tensor_tensor(tmp_tok[:, t, cols], bank(("ple_proj", i))[:, :], tmp_tok[:, t, cols],
                                           ALU.mult), "drained_by_dve")
                    step(dve.tensor_tensor(x[:, t, cols], x[:, t, cols], tmp_tok[:, t, cols], ALU.add),
                         "x_ready" if i % 2 else "dve_step")
            if on("gla"):
                turned("xT_in0")
                K = slice(0, GDK)
                for pair in range(2):
                    key = ("gla_gate", pair)
                    wait_filled(dve, key)
                    for i in range(2):
                        h = 2 * pair + i
                        done(dve.tensor_scalar(gf[K, h * S:(h + 1) * S], bank(key)[K, i * S:(i + 1) * S],
                                               c("gla_b")[K, h:h + 1], None, ALU.add),
                             "drained_by_dve" if i else "dve_step")
                settle()
                step(dve.tensor_scalar(ge[K], gf[K], -1.0, None, ALU.mult))
                step(dve.tensor_tensor(ge[K], ge[K], gf[K], ALU.max), "gla_abs")
                step(dve.tensor_scalar(gf[K], gf[K], 0.0, None, ALU.min))
                step(dve.memset(scan_mask[K], 1.0))
                step(dve.memset(scan_mask.rearrange("p (n c) -> p n c", c=CH)[K, :, 0:1], 0.0))
                dve.wait_ge(sem("gla_softplus"), 1)
                step(dve.tensor_tensor(gf[K], gf[K], ge[K], ALU.subtract))
                step(dve.tensor_scalar(gf[K], gf[K], 1.0 / 16.0, None, ALU.mult))
                step(dve.tensor_tensor_scan(gb[K], scan_mask[K], gf[K], 0.0, ALU.mult, ALU.add), "gla_cumsum")
                b3 = gb.rearrange("p (n c) -> p n c", c=CH)
                step(dve.tensor_tensor(gt.rearrange("p (n c) -> p n c", c=CH)[K],
                                       b3[K, :, CH - 1:CH].to_broadcast([GDK, GH * NCH, CH]), b3[K], ALU.subtract),
                     "gla_tail")
                dve.wait_ge(sem("gla_exp"), 3)
                wait_drained(dve, ("gla_k", 1))
                q2, k2, kt2, ke2 = (v.rearrange("p h s -> p (h s)") for v in (gq, gk, gkt, gke))
                done(dve.tensor_tensor(q2[K], q2[K], geb[K], ALU.mult), "dve_step")
                done(dve.tensor_tensor(kt2[K], k2[K], gf[K], ALU.mult), "dve_step")
                done(dve.tensor_tensor(ke2[K], k2[K], gt[K], ALU.mult), "dve_step")
                settle()
                dve.sem_inc(sem("gla_decayed"), 1)
                gain = row(3)
                wait_drained(dve, ("gla_r", 3))
                for t in range(NT):
                    done(dve.tensor_tensor(grs[:, t, :], grs[:, t, :], gain[:, 0:768], ALU.mult), "dve_step")
                settle()
                dve.sem_inc(sem("rows_used"), 1)
                for t in range(NT):
                    key = ("gla_kendT", t)
                    wait_filled(dve, key)
                    done(dve.tensor_copy(kendT[:, t].rearrange("p h k -> p (h k)"), bank(key)[:, 0:GH * GDK]),
                         "drained_by_dve")
                wait_filled(dve, ("gla_intra", 0))
                done(dve.tensor_tensor(attnT.rearrange("p t h c -> p (t h) c"),
                                       bank(("gla_intra", 0))[:, :].rearrange("p (a c) -> p a c", c=CH),
                                       c("tri").unsqueeze(1).to_broadcast([P, 8, CH]), ALU.mult), "drained_by_dve")
                dec = geb.rearrange("p (h n c) -> p h n c", h=GH, n=NCH)
                for n in range(NCH - 1):
                    for hp in range(2):
                        key = ("gla_kv", 2 * n + hp)
                        wait_filled(dve, key)
                        for i in range(2):
                            h = 2 * hp + i
                            cols = slice(h * GDV, (h + 1) * GDV)
                            src = bank(key)[K, i * GDV:(i + 1) * GDV]
                            name = "drained_by_dve" if i else "dve_step"
                            if n == 0:
                                done(dve.tensor_copy(state[K, 0, cols], src), name)
                            else:
                                done(dve.scalar_tensor_tensor(state[K, n, cols], state[K, n - 1, cols],
                                                              dec[K, h, n, CH - 1:CH], src, ALU.mult, ALU.add), name)
                    settle()
                    dve.sem_inc(sem("gla_state"), 1)
                dve.wait_ge(sem("gla_rms"), 1)
                step(dve.reciprocal(stat[:, 32:40], stat[:, 32:40]))
                for i in range(4):
                    t, hp = i // 2, i % 2
                    for h in range(2):
                        cols = slice((2 * hp + h) * GDV, (2 * hp + h + 1) * GDV)
                        done(dve.scalar_tensor_tensor(mixin[:, t, cols], bank(("gla_o", i))[:, h * GDV:(h + 1) * GDV],
                                                      stat[:, 32 + 2 * i + h:33 + 2 * i + h], grs[:, t, cols], ALU.mult,
                                                      ALU.mult), "drained_by_dve" if h else "dve_step")
                    if hp:
                        settle()
                        dve.sem_inc(sem("mix_ready"), 1)
            for l in range(2):
                if l == 1 and on("dil"):
                    turned("xT_in1")

                    def normaliser(u):
                        dve.wait_ge(sem("dil_exp"), u + 1)
                        r = att_rec[:, u % 3, 0:1]
                        step(dve.reciprocal(r, att_sum[:, u % 3, 0:1]))
                        step(dve.tensor_scalar(dil_diag[u % 3], ident, r, None, ALU.mult), "dil_diag")

                    for kind, u in pipelined(len(DIL_UNITS)):
                        s, t = DIL_UNITS[u]
                        nk = (t + 1) * P
                        if kind == "score":
                            E = dil_E[u % 3] if t else dil_E0[u % 3]
                            mask = c(f"dil_mask{t}", 3, nk)
                            for part in range(t + 1):
                                key = ("dil_score", 2 * u + part)
                                wait_filled(dve, key)
                                lo, n = (0, 3) if t == 0 else ((0, 2) if part == 0 else (2, 1))
                                done(dve.scalar_tensor_tensor(
                                    E[:, lo:lo + n, :], bank(key)[:, 0:n * nk].rearrange("p (g k) -> p g k", g=n),
                                    P ** -0.5, mask[:, lo:lo + n, :], ALU.mult, ALU.add), "drained_by_dve")
                            settle()
                            row_max(E.rearrange("p g k -> p (g k)"), att_nm[:, u % 3, 0:1], "dil_max")
                            if u:
                                normaliser(u - 1)
                            if u == len(DIL_UNITS) - 1:
                                normaliser(u)
                        if kind == "value":
                            key = ("dil_value", 2 * u)
                            wait_filled(dve, key)
                            done(dve.tensor_copy(mixT[:, s, t * P:(t + 1) * P], bank(key)[:, 0:P]), "drained_by_dve")
                if on(f"memat{l}"):
                    def mem_normaliser(u):
                        dve.wait_ge(sem("mem_exp"), l * len(MEM_UNITS) + u + 1)
                        r = att_rec[:, u % 3, :]
                        step(dve.reciprocal(r, att_sum[:, u % 3, :]))
                        for s in range(2):
                            done(dve.tensor_scalar(mem_diag[u % 3][:, s, :], ident, r[:, s:s + 1], None, ALU.mult),
                                 "mem_diag" if s else "dve_step")
                            if s == 0:
                                settle()

                    for kind, u in pipelined(len(MEM_UNITS)):
                        key = (f"mem_{kind}{l}", 2 * u)
                        m, t = MEM_UNITS[u]
                        if kind == "score":
                            E = mem_E[u % 3]
                            for s in range(2):
                                key = (f"mem_score{l}", 2 * u + s)
                                wait_filled(dve, key)
                                done(dve.tensor_copy(E[:, s, :], bank(key)[:, 0:S]), "drained_by_dve")
                            settle()
                            row_max(E, att_nm[:, u % 3, :], "mem_max")
                            if u:
                                mem_normaliser(u - 1)
                            if u == len(MEM_UNITS) - 1:
                                mem_normaliser(u)
                        if kind == "value":
                            wait_filled(dve, key)
                            done(dve.tensor_copy(mixT[:, 6 + m, t * P:(t + 1) * P], bank(key)[:, 0:P]), "drained_by_dve")
                if on(f"out{l}"):
                    for i in range(4):
                        t, cols = i // 2, slice((i % 2) * 512, (i % 2 + 1) * 512)
                        wait_filled(dve, (f"out{l}", i))
                        done(dve.scalar_tensor_tensor(x[:, t, cols], x[:, t, cols], ALPHA, bank((f"out{l}", i))[:, :],
                                                      ALU.mult, ALU.add), "drained_by_dve")
                    settle()
                    layer_norm(2 * l, 4 + 4 * l, 5 + 4 * l, "x_ready")
                if on(f"peer{l}"):
                    turned(f"xT_peer{l}")
                    if l == 0:
                        dve.sem_inc(sem("gather_free"), GBUF)
                    route(l, 0, 0)
                    route(l, 0, 1)
                    for t in range(NT):
                        if t == 0:
                            for g in range(TURNS):
                                dots(l, t, g, 0)
                                if g + 2 < TURNS:
                                    route(l, 0, g + 2)
                        else:
                            with dve.Fori(0, TURNS) as i:
                                dots(l, t, 0, i)
                        dve.wait_ge(sem("gather_free"), (l * NT + t) * 2 * P + P + GBUF)
                        dve.sem_inc(sem("peer_dots"), 1)
                        dve.wait_ge(sem("peer_exp"), l * NT + t + 1)
                        gs = peer_st[:, 48:56]
                        step(dve.tensor_reduce(gs, gate_w[t], AX, ALU.add))
                        step(dve.reciprocal(gs, gs))
                        step(dve.tensor_tensor(gate_w[t], gate_w[t], gs.unsqueeze(2).to_broadcast([P, PH, PK]), ALU.mult))
                        dve.wait_ge(sem("peer_gelu"), l * NT + t + 1)
                        step(dve.tensor_tensor(hdot[t], hdot[t], gate_w[t].rearrange("p h k -> p (h k)"), ALU.mult))
                        for b in range(2):
                            done(dve.memset(acc[b], 0.0), "dve_step")
                        settle()
                        if t == 0:
                            for g in range(TURNS):
                                route(l, 1, g)
                                sums(l, t, g, 0)
                        else:
                            with dve.Fori(0, TURNS) as i:
                                sums(l, t, 0, i)
                        dve.wait_ge(sem("gather_free"), (l * NT + t + 1) * 2 * P + GBUF)
                        step(dve.tensor_tensor(acc[0], acc[0], acc[1], ALU.add))
                        step(dve.scalar_tensor_tensor(x[:, t, :], x[:, t, :], ALPHA, acc[0], ALU.mult, ALU.add))
                        layer_norm(2 * l + 1, 6 + 4 * l, 7 + 4 * l, "x_ready" if l == 0 else "x_final", [t])
            if dump is not None:
                settle()
                dve.sem_inc(sem("dbg_dve"), 1)


def prepare(inputs):
    a = {k: np.asarray(v) for k, v in inputs.items()}
    cols = constant_columns(a)
    where, at = {}, 0
    for name, v in cols.items():
        where[name] = (at, at + v.shape[1])
        at += v.shape[1]
    arrays = {
        "x_in": np.ascontiguousarray(a["x"][0]),
        "memT_in": np.ascontiguousarray(a["mem_2"][0].T),
        "weights": weight_slots(a),
        "consts": np.concatenate(list(cols.values()), 1),
        "rows_in": row_vectors(a),
        "peer_u": a["peer_u_2"].reshape(2 * EXPERTS, D),
        "peer_v": a["peer_v_2"].reshape(2 * EXPERTS, D),
    }
    return arrays, where


def kernel(**inputs):
    import concourse.bacc as bacc
    from concourse.bass_utils import run_bass_kernel_spmd

    arrays, where = prepare(inputs)
    nc = bacc.Bacc("TRN2", target_bir_lowering=False, num_devices=1)
    aps = {name: nc.dram_tensor(name, v.shape, mybir.dt.from_np(v.dtype), kind="ExternalInput").ap()
           for name, v in arrays.items()}
    out = nc.dram_tensor("x_out", (S, D), F32, kind="ExternalOutput").ap()
    build(nc, aps["x_in"], aps["memT_in"], aps["weights"], aps["consts"], where, aps["rows_in"], aps["peer_u"],
          aps["peer_v"], out)
    r = run_bass_kernel_spmd(nc, [arrays], core_ids=[0])
    return r.results[0]["x_out"].reshape(1, S, D)
```

```python
from contextlib import ExitStack

import numpy as np

import concourse.bass as bass
from concourse import mybir

F32 = mybir.dt.float32
U32 = mybir.dt.uint32
F32R = mybir.dt.float32r
HIGH = 0xFFFFF000
ALU = mybir.AluOpType
ACT = mybir.ActivationFunctionType
AX = mybir.AxisListType.X

P = 128
D = 1024
S = 256
NT = S // P
NK = D // P
SLOT = 1024
RING = 12
NEG = -1e30

HEADS, HD, GROUPS = 16, 64, 4
NCMP = 15
FF = 2816
NF = FF // P
PLE = 256
GH, GDK, GDV = 4, 96, 192
CH = 64
NCH = S // CH
DSLOTS, DGROUPS = 6, 3
MH = 4
PH, PN, PK = 8, 128, 16
EXPERTS = PN * PN
ALPHA = 4.0 ** 0.25
GBUF = 8
BODY = 32
TURNS = P // BODY
TH = BODY // 16
SPLITS = 4
NROW = 4

BLOCKS = [(2 * (j // 4) + s) * 4 + j % 4 for j in range(8) for s in range(2)]
SLOPES = [2.0 ** (-8.0 * (b + 1) / HEADS) for b in BLOCKS]

UNITS = [(j, s, t) for j in range(8) for s in range(2) for t in range(NT)]
NZ = 12
NZ0 = 3


def attention_order():
    order = []
    for u in range(len(UNITS) + 3):
        if u < len(UNITS):
            order.append(("score", u))
        order += [("gate", NZ0 + n) for n in range(NZ - NZ0) if n * 5 // 2 == u]
        if 0 <= u - 2 < len(UNITS):
            order.append(("turn", u - 2))
        if 0 <= u - 3 < len(UNITS):
            order.append(("value", u - 3))
    return order


def pipelined(n):
    order = []
    for u in range(n + 3):
        if u < n:
            order.append(("score", u))
        if 0 <= u - 2 < n:
            order.append(("turn", u - 2))
        if 0 <= u - 3 < n:
            order.append(("value", u - 3))
    return order


def peer_head_order():
    order = [("q", 0), ("q", 1), ("s", 0), ("s", 1), ("q", 2)]
    for h in range(3, PH + 1):
        order += [("q", h), ("s", h - 1)] if h < PH else [("s", h - 1)]
    return order


MEM_UNITS = [(m, t) for m in range(2) for t in range(NT)]

CHUNK = 8
CHUNKS = P // CHUNK
PE_SLABS = range(3, P, 4)
DIAGS = 4


def by_twos(name, n):
    steps = pipelined(n)
    at = [i for i, (kind, _) in enumerate(steps) if kind == "score"] + [len(steps)]
    rounds = [steps[i:j] for i, j in zip(at, at[1:])]
    tail = rounds.pop()
    rounds += [tail[:1]] + [tail[1:]]
    return [(name, sum(rounds[i:i + 2], [])) for i in range(0, len(rounds), 2)]


def mixer_pieces():
    wait = [("wait", None)]
    first = wait * 6 + by_twos("dil", DSLOTS) + by_twos("mem", 2) + wait + [("out", None)]
    assert len(first) <= CHUNKS
    pieces = dict(enumerate(first))
    pieces.update(routing_pieces(1, [CHUNKS + n * 4 // 3 for n in range(3 * TURNS)], range(TURNS)))
    return pieces


def routing_pieces(layer, places, turns):
    parts = [(f"route{layer}", (g, part)) for g in turns for part in range(3)]
    return dict(zip(places, parts))


def ffn_order():
    order = []
    for f in range(NF + 1):
        if f < NF:
            order += [("gate", f), ("up", f)]
        if f >= 1:
            order.append(("down", f - 1))
    return order


def job_plan():
    ids, drains, banks = {}, [], []
    state = {"bank": 0, "of": 8}

    def plan(stage, n, drain, fixed=None):
        for i in range(n):
            ids[(stage, i)] = len(drains)
            drains.append(drain)
            if fixed is None:
                banks.append(state["bank"])
                state["bank"] = (state["bank"] + 1) % state["of"]
            else:
                banks.append(fixed[i % len(fixed)])

    plan("xT_mix", 4, "dve")
    plan("xr", 4, "act")
    plan("kc", 1, "dve")
    plan("vc", 1, "dve")
    plan("k_sel", 1, "act")
    plan("k_win", 1, "act")
    plan("lru_r", 4, "act")
    plan("lru_i", 4, "act")
    plan("v_sw", 2, "act")
    plan("nsa_gate", 1, "act")
    plan("hid_k", 2, "act")
    plan("hid_v", 2, "act")
    plan("q", 4, "act")
    plan("k_cmp", 1, "dve")
    plan("v_cmp", 1, "dve")
    plan("cmp_score", 4, "dve")
    plan("att_gate", NZ0, "act")
    plan("cmp_turn", 8, "act")
    for kind, u in attention_order():
        drain = {"score": "dve", "gate": "act", "turn": "act", "value": "dve"}[kind]
        ids[("att_" + kind, u)] = len(drains)
        drains.append(drain)
        banks.append(state["bank"])
        state["bank"] = (state["bank"] + 1) % state["of"]
    plan("mix_out", 4, "dve")
    plan("mem_k0", 1, "act")
    plan("xT_ffn", 4, "dve")
    for f in range(NF):
        for i, kind in enumerate(("gate", "up")):
            ids[("ffn_" + kind, f)] = len(drains)
            drains.append("dve")
            banks.append((2 * f + i) % 4)
    plan("ffn_down", 4, "dve", [4, 5, 6, 7])
    state["bank"] = 0
    plan("mem_v0", 2, "act")
    plan("xT_ple", 4, "act")
    plan("ple_gate", 4, "dve")
    plan("ple_proj", 4, "dve")
    def plan_steps(steps, prefix, suffix, per_score):
        for kind, u in steps:
            for i in range(per_score if kind == "score" else 1):
                ids[(f"{prefix}_{kind}{suffix}", 2 * u + i)] = len(drains)
                drains.append({"score": "dve", "turn": "act", "value": "dve"}[kind])
                banks.append(state["bank"])
                state["bank"] = (state["bank"] + 1) % state["of"]

    plan("xT_in0", 4, "act")
    plan("gla_q", 2, "act")
    plan("gla_k", 2, "act")
    plan("gla_g1", 1, "act")
    plan("gla_gate", 2, "dve")
    plan("qm0", 1, "act")
    plan("gla_v", 4, "act")
    plan("gla_kendT", 2, "dve")
    plan("gla_intra", 1, "dve")
    plan("gla_kv", 6, "dve")
    plan("gla_r", 4, "act")
    plan("gla_o", 4, "dve")
    plan_steps(pipelined(len(MEM_UNITS)), "mem", "0", 2)
    plan("gla_mixT", 3, "act")
    plan("out0", 4, "dve")
    plan("xT_peer0", 4, "act")
    for kind, h in peer_head_order():
        ids[(f"peer_{kind}0", h)] = len(drains)
        drains.append("act")
        banks.append(state["bank"])
        state["bank"] = (state["bank"] + 1) % state["of"]
    plan("mem_k1", 1, "act")
    plan("mem_v1", 2, "act")
    state.update(bank=0, of=6)
    plan("sum0_0", 2, "dve", [6, 7])
    for t in range(NT):
        plan(f"xT_in1_{t}", 2, "act")
        plan(f"dil_k_{t}", 2, "act")
        plan(f"dil_v_{t}", 2, "act")
        plan(f"dil_q_{t}", 5, "act")
        plan(f"qm1_{t}", 1, "act")
        plan_steps(pipelined(DSLOTS), "dil", f"_{t}", t + 1)
        plan_steps(pipelined(2), "mem", f"1_{t}", 2)
        plan(f"out1_{t}", 2, "dve")
        plan(f"xT_peer1_{t}", 2, "act")
        for g in range(TURNS):
            plan(f"peer_q1_{t}_{g}", 1, "act")
            plan(f"peer_s1_{t}_{g}", 1, "act")
        plan(("sum0_1", "sum1_0")[t], 2, "dve", [6, 7])
    plan("sum1_1", 2, "dve", [6, 7])
    before, last = [], {}
    for n, b in enumerate(banks):
        before.append(last.get(b))
        last[b] = n
    freed = []
    seen = {"act": 0, "dve": 0}
    for d in drains:
        seen[d] += 1
        freed.append(seen[d])
    return ids, drains, banks, before, freed



def slots_of_columns(w, width=P):
    k, n = w.shape
    out = []
    for c in range(0, n, width):
        blk = w[:, c:c + width]
        out.append(blk.reshape(k // P, P, blk.shape[1]).transpose(1, 0, 2).reshape(P, -1))
    return out


def slots_of_rows(w):
    k, n = w.shape
    per = max(1, SLOT // n)
    out = []
    for c in range(0, k, per * P):
        blk = w[c:c + per * P]
        out.append(blk.reshape(-1, P, n).transpose(1, 0, 2).reshape(P, -1))
    return out


def block_order(w, axis=-1):
    w = np.moveaxis(w, axis, -1)
    w = w.reshape(w.shape[:-1] + (16, 64))[..., BLOCKS, :].reshape(w.shape)
    return np.moveaxis(w, -1, axis)


def block_diagonal(w):
    out = np.zeros((P, 8, P), np.float32)
    for j in range(8):
        for s in range(2):
            out[64 * s:64 * s + 64, j, 64 * s:64 * s + 64] = w[BLOCKS[2 * j + s]]
    return out.reshape(P, -1)


def weight_slots(a):
    w_in = a["w_in"][0]
    cuts = dict(xr=(0, 1024), gr=(1024, 2048), q=(2048, 3072), kc=(3072, 3328), vc=(3328, 3584),
                ks=(3584, 3840), vs=(3840, 4096), kw=(4096, 4352), vw=(4352, 4608), g=(4608, 4656),
                gmr=(4656, 5680), gma=(5680, 6704))
    z = {n: w_in[:, i:j] for n, (i, j) in cuts.items()}
    out = []
    mem_k = [slots_of_columns(a["w_mem_kv_2"][l][:, :256]) for l in range(2)]
    mem_v = [slots_of_rows(a["w_mem_kv_2"][l][:, 256:]) for l in range(2)]
    out += slots_of_columns(block_order(z["xr"]))
    out += slots_of_columns(z["kc"]) + slots_of_columns(z["vc"])
    out += slots_of_columns(z["ks"]) + slots_of_columns(z["kw"])
    out += [block_diagonal(a["lru_wa"][0]), block_diagonal(a["lru_wx"][0])]
    out += slots_of_rows(np.concatenate([z["vs"], z["vw"]], 1))
    out += slots_of_columns(z["g"].reshape(D, 16, 3)[:, BLOCKS].transpose(0, 2, 1).reshape(D, 48), 48)
    out += slots_of_rows(a["cmp_k_w1"][0]) + slots_of_rows(a["cmp_v_w1"][0])
    out += slots_of_columns(block_order(z["q"]))
    out += slots_of_columns(block_order(z["gma"])) + slots_of_columns(block_order(z["gr"]))
    out += slots_of_columns(block_order(z["gmr"]))
    out += slots_of_rows(block_order(a["w_out"][0], 0)) + mem_k[0]
    ffn_slot = len(out)
    gate = slots_of_columns(a["ffn_w_gate_up"][0][:, :FF])
    up = slots_of_columns(a["ffn_w_gate_up"][0][:, FF:])
    down = slots_of_rows(a["ffn_w_down"][0])
    out += [{"gate": gate, "up": up, "down": down}[kind][f] for kind, f in ffn_order()]
    out += mem_v[0]
    out += slots_of_rows(a["ple_w_gate"][0]) + slots_of_rows(a["ple_w_proj"][0])
    aw = a["a_w_in_2"][0]
    qk, vw = GH * GDK, GH * GDV
    out += slots_of_columns(aw[:, :2 * qk], GDK)
    g0 = 2 * qk + 2 * vw
    out += slots_of_columns(aw[:, g0:g0 + 16], 16)
    out += slots_of_columns(aw[:, g0 + 16:])
    out += slots_of_rows(aw[:, 2 * qk:2 * qk + vw]) + slots_of_rows(aw[:, 2 * qk + vw:g0])
    out += slots_of_rows(a["w_out_2"][0]) + slots_of_columns(a["peer_w_q_2"][0])
    out += mem_k[1] + mem_v[1]
    kv = a["shared_w_kv_2"]
    bw = a["b_w_in_2"][0]
    q = bw[:, :2304].reshape(D, 3, 6, 128).transpose(0, 2, 1, 3).reshape(D, 2304)
    layer = slots_of_columns(kv[:, :768]) + slots_of_rows(kv[:, 768:])
    layer += slots_of_columns(q) + slots_of_columns(bw[:, 2304:])
    layer += slots_of_rows(a["w_out_2"][1]) + slots_of_columns(a["peer_w_q_2"][1])
    out += layer * NT
    pad = -len(out) % RING
    w = np.zeros((len(out) + pad, P, SLOT), np.float32)
    for n, s in enumerate(out):
        w[n, :, :s.shape[1]] = s
    return w, ffn_slot


def constant_columns(a):
    i = np.arange(P)[:, None]
    cols = {}

    def put(name, x):
        x = np.asarray(x, np.float32)
        full = np.zeros((P, x.reshape(x.shape[0], -1).shape[1]), np.float32)
        full[:x.shape[0]] = x.reshape(x.shape[0], -1)
        cols[name] = full

    def col(v):
        return v.reshape(NK, P).T

    put("ident", np.eye(P))
    put("eps", np.broadcast_to(np.array([1e-6, 1e-5, 1.0, 0.0]), (P, 4)))
    put("g_mix", col(a["norm_mix_pre"][0]))
    put("g_ffn", col(a["norm_ffn_pre"][0]))
    put("conv_w", np.stack([col(block_order(a["conv_w"][0][k])) for k in range(4)], 1))
    for name, key in (("conv_b", "conv_b"), ("lru_ba", "lru_ba"), ("lru_bx", "lru_bx"), ("lam", "lru_lambda")):
        put(name, col(block_order(a[key][0])))
    dist = P + i - np.arange(S)[None, :]
    put("neg_dist", np.where(dist >= 0, -dist, NEG))
    t = (np.arange(NT)[None, :] * P + i)[:, :, None]
    dc = t - (np.arange(NCMP) * 16 + 31)[None, None, :]
    put("cmp_bias", np.where(dc[:, :, None] >= 0, -dc[:, :, None] * np.array(SLOPES)[None, None, :, None], NEG))
    put("cmp_mask", dc >= 0)
    put("tri", (np.arange(CH)[None, :] >= i % CH))
    j = np.arange(S)[None, :]
    rel = P + i - j
    m1 = [np.where((rel >= 0) & (rel <= 128), 0, NEG), np.where((rel >= 0) & (rel % 4 == 0), 0, NEG),
          np.where((rel >= 0) & (rel % 16 == 0), 0, NEG)]
    put("dil_mask1", np.stack(m1, 1))
    put("dil_mask0", np.stack([m[:, P:] for m in m1], 1))
    put("iota", np.broadcast_to(np.arange(PK), (P, PK)))
    put("gla_b", a["a_b_gate_2"][0].reshape(GH, GDK).T)
    for n in "kv":
        put("pos_" + n, a[f"cmp_pos_{n}"][0].reshape(16, 2 * HD).T)
        put("w2_" + n, a[f"cmp_{n}_w2"][0].reshape(2, P, HD).transpose(1, 0, 2))
    put("w_gate2", a["a_w_gate2_2"][0])
    put("keysT", a["peer_sub_keys_2"].transpose(3, 0, 1, 2))
    put("pT", a["p"][0, 0].reshape(S, 2, P).transpose(2, 1, 0))
    return cols


ROWS = ["norm_mix_post", "norm_ffn_post", "ple_b_gate", "a_norm_g_2", "mix_g0", "mix_b0", "ffn_g0", "ffn_b0",
        "mix_g1", "mix_b1", "ffn_g1", "ffn_b1"]


def row_vectors(a):
    out = np.zeros((len(ROWS), D), np.float32)
    for n, name in enumerate(ROWS):
        if name in a:
            v = a[name][0]
        else:
            v = a[f"ln_{name[:3]}_{name[4]}_2"][int(name[5])]
        out[n, :v.shape[0]] = v
    return out



def build(nc, x_in, memT_in, weights, consts, where, rows_in, peer_u, peer_v, out, upto=None, dump=None):
    ids, drains, banks, before, freed_count = job_plan()
    n_slots = weights.shape[0]
    n_const = consts.shape[1]
    n_early = where["lam"][1]
    ctx = ExitStack()
    with ctx:
        def sb(name, shape, dt=F32):
            return ctx.enter_context(nc.sbuf_tensor(name, shape, dt))

        named = {}

        def sem(name):
            if name not in named:
                named[name] = ctx.enter_context(nc.semaphore(name))
            return named[name]

        ring = sb("weight_ring", [P, RING, SLOT])
        rows = sb("row_ring", [P, NROW, D])
        cst = sb("const_tile", [P, n_const])
        x = sb("x_tok", [P, NT, D])
        xT = sb("xT", [P, NK, S])
        mem_k = sb("mem_k", [P, 2, 2, S])
        memT = sb("memT", [P, NK, S])
        mem_v = sb("mem_v", [P, 2, 2, S])
        with ExitStack() as inner:
            def place(name, size, dt=F32R):
                return inner.enter_context(nc.sbuf_tensor(name, [P, size], dt))

            place("before_splits", 4096, F32)
            x_split_r = place("x_split", NK * 2 * S)
            w_split_r = place("w_split", SPLITS * 2 * SLOT)
            act_split_r = place("act_split", 3 * 2 * S)
        arena = sb("arena", [P, 24300])
        ps = [ctx.enter_context(nc.psum_tensor(f"bank{b}", [P, 512], F32)) for b in range(8)]

        def c(name, *dims):
            lo, hi = where[name]
            v = cst[:, lo:hi]
            if len(dims) == 2:
                v = v.rearrange("p (a b) -> p a b", a=dims[0])
            if len(dims) == 3:
                v = v.rearrange("p (a b c) -> p a b c", a=dims[0], b=dims[1])
            return v

        def area(lo, *dims):
            n = int(np.prod(dims))
            assert lo + n <= 24300, (lo, dims)
            v = arena[:, lo:lo + n]
            if len(dims) == 2:
                v = v.rearrange("p (a b) -> p a b", a=dims[0])
            if len(dims) == 3:
                v = v.rearrange("p (a b c) -> p a b c", a=dims[0], b=dims[1])
            if len(dims) == 4:
                v = v.rearrange("p (a b c d) -> p a b c d", a=dims[0], b=dims[1], c=dims[2])
            return v

        ident = c("ident")
        xr_pad = area(0, NK, S + 3)
        xc = area(2080, NK, S)
        lru_a = area(4128, NK, S)
        lru_i = area(6176, NK, S)
        lru_t = area(8224, NK, S)
        gr = area(10272, NK, S)
        qT = area(12320, NK, S)
        kT = [area(14368, 2, S), area(14880, 2, S)]
        v_sw = area(15392, NT, 512)
        gmr = area(16416, NK, S)
        gma = area(18464, NK, S)
        yT = area(20512, NK, S)
        xn = area(20512, NT, D)
        cmp_in = {n: [area(20512 + 1024 * (n == "v") + 512 * h, GROUPS, P) for h in range(2)] for n in "kv"}
        att_E = [area(512 * b, 2, S) for b in range(3)]
        att_E0 = [area(512 * b, 2, P) for b in range(3)]
        att_PT = [area(4128 + 512 * b, 4, P) for b in range(2)]
        att_diag = [area(5152 + 256 * b, 2, P) for b in range(3)]
        cmp_PT = area(6176, HEADS, S)
        small = 22560
        hidT = {n: area(small + 120 * (n == "v"), 2, 4 * NCMP) for n in "kv"}
        k_cmp = area(small + 240, 2, NCMP)
        v_cmp = area(small + 270, 256)
        nsa_g = area(small + 526, NT, 3, HEADS)
        cmp_s = area(small + 622, NT, HEADS, NCMP)
        stat = area(small + 1102, 128)
        lam_t = area(small + 1230, 10, NK)
        att_nm = area(small + 1310, 3, 2)
        att_sum = area(small + 1316, 3, 2)
        att_rec = area(small + 1322, 3, 2)
        cmp_st = area(small + 1328, NT, 4, HEADS)
        assert small + 1328 + 128 <= 24300
        gate_s = [area(256 * b, S) for b in range(2)]
        act_T = area(512, S)
        up_s = [area(1280 + 256 * b, S) for b in range(2)]
        x_split = x_split_r[:, :].rearrange("p (a b c) -> p a b c", a=NK, b=2)
        w_split = [w_split_r[:, 2 * SLOT * b:2 * SLOT * (b + 1)].rearrange("p (a b) -> p a b", a=2) for b in range(SPLITS)]
        act_split = [act_split_r[:, 2 * S * b:2 * S * (b + 1)].rearrange("p (a b) -> p a b", a=2) for b in range(3)]
        masked = [area(17920 + SLOT * b, SLOT) for b in range(2)]
        tmp_tok = area(2048, NT, D)
        gq = area(0, GH, S)
        gk = area(1024, GH, S)
        gf = area(2048, GH * S)
        ge = area(3072, GH * S)
        gb = area(4096, GH * S)
        geb = area(5120, GH * S)
        gt = area(6144, GH * S)
        gkt = area(7168, GH, S)
        gke = area(8192, GH, S)
        scan_mask = area(9216, GH * S)
        kendT = area(10240, NT, GH, GDK)
        attnT = area(11008, NT, GH, CH)
        gv = area(11520, NT, GH * GDV)
        grs = area(13056, NT, GH * GDV)
        state = area(14592, NCH - 1, GH * GDV)
        mixin = area(16896, NT, GH * GDV)
        mixT = area(18432, NK, S)
        qmT = area(20480, 2, S)
        g1T = area(20992, S)
        tmp_sq = area(21248, S)
        mem_E = [area(2048 + 512 * b, 2, S) for b in range(3)]
        mem_PT = [area(4096 + 512 * b, 4, P) for b in range(2)]
        mem_diag = [area(5120 + 256 * b, 2, P) for b in range(3)]
        gbuf = [area(1024 * b, D) for b in range(GBUF)]
        acc = [area(8192 + 1024 * b, D) for b in range(2)]
        sc = [area(10240 + 2048 * t, 16, PN) for t in range(NT)]
        pq = [area(14336 + 512 * b, 2, S) for b in range(2)]
        rest = area(15360, 2 * TH * PN)
        onehot = area(15360, TH, PK, PK)
        top_v, top_i, top_f = (area(15872 + 64 * n, 2 * TH, PK) for n in range(3))
        best_v, best_j, pos_a, pos_b, sel_a, sel_b, pos_u = (area(16064 + 32 * n, TH, PK) for n in range(7))
        expert = [area(16288 + 128 * t, P) for t in range(NT)]
        gate_w = [area(16544 + 128 * t, PH, PK) for t in range(NT)]
        hdot = [area(16800 + 128 * t, P) for t in range(NT)]
        stage = area(17056, BODY)
        dkT = area(17184, DSLOTS, S)
        dv = area(18720, NT, 768)
        dqT = area(20256, 18, P)
        tile_qmT = area(22560, 2, P)
        peer_st = area(22816, 64)
        diag = [area(22880 + 128 * b, P) for b in range(DIAGS)]
        tile_xT = xT[:, 0:4, :].rearrange("p k s -> p (k s)").rearrange("p (k s) -> p k s", k=NK)
        tile_mixT = xT[:, 4:8, :].rearrange("p k s -> p (k s)").rearrange("p (k s) -> p k s", k=NK)
        dil_E = [area(10240 + 768 * b, 3, S) for b in range(3)]
        dil_E0 = [area(10240 + 768 * b, 3, P) for b in range(3)]
        dil_PT = [area(12544 + 256 * b, 2, P) for b in range(2)]
        dil_diag = [area(13056 + 128 * b, P) for b in range(3)]
        mem1_E = [area(10240 + 512 * b, 2, S) for b in range(3)]
        mem1_PT = [area(11776 + 512 * b, 4, P) for b in range(2)]
        mem1_diag = [area(12800 + 256 * b, 2, P) for b in range(3)]

        STAGES = ["z", "lru", "cmp", "att", "mix", "ffn", "ple", "gla", "memat0", "out0", "peer0", "peer1"]
        limit = len(STAGES) if upto is None else STAGES.index(upto) + 1

        def on(stage_name):
            return STAGES.index(stage_name) < limit

        def wait_filled(e, key):
            e.wait_ge(sem("psum_filled"), ids[key] + 1)

        def wait_drained(e, key):
            n = ids[key]
            e.wait_ge(sem("drained_by_" + drains[n]), freed_count[n])

        def bank(key):
            return ps[banks[ids[key]]]

        def counter(e):
            count, pending = {}, {}

            def done(ins, name, n=1):
                ins.then_inc(sem(name), n)
                count[name] = count.get(name, 0) + n
                pending[name] = count[name]
                return ins

            def settle():
                for name, v in pending.items():
                    e.wait_ge(sem(name), v)
                pending.clear()

            return done, settle, count

        def tile_pq(g):
            return pq[g % 2].rearrange("p q s -> p (q s)").rearrange("p (a s) -> p a s", a=2 * TH)

        def load_row(e, n):
            e.dma_start(rows[:, n % NROW, :], rows_in[n:n + 1, :].to_broadcast([P, D]))\
                .then_inc(sem(row_sem(n)), 16)

        def row_sem(n):
            return f"last_row{n % NROW}_loaded" if n >= 10 else f"row_loaded{n % NROW}"

        def uses_before(l, t, kind, s):
            return (((l * NT + t) * 2 + kind) * P + s) // GBUF

        def wait_freed(e, l, t, kind, s):
            e.wait_ge(sem(f"buffer_free{s % GBUF}"), uses_before(l, t, kind, s) + 2)

        def v_chunk(n):
            return [s for s in PE_SLABS if s // CHUNK == n]

        def group_at(n):
            return {4 * g - 3: g for g in range(1, TURNS)}.get(n)

        block = ctx.enter_context(nc.Block())
        PIECES = mixer_pieces()
        FFN_SLOT = where["ffn_slot"]
        PASSES = [(kind, t) for t in range(NT) for kind in "uv"]

        wt = {"n": 0, "owed": 0}

        @block.tensor
        def _(pe):
            def next_weights():
                n = wt["n"]
                pe.wait_ge(sem(f"weight_loaded{n % RING}"), 16 * (n // RING + 1))
                if n and not wt.pop("given", False):
                    wt["owed"] += 1
                wt["n"] = n + 1
                return ring[:, n % RING, :]

            def mm(o, lhsT, rhs, start, stop, end=False, turn=False):
                ins = pe.matmul(o, lhsT, rhs, start=start, stop=stop, is_transpose=turn or None)
                if end:
                    ins.then_inc(sem("psum_filled"), 1)
                elif wt["owed"]:
                    wt["owed"] -= 1
                    ins.then_inc(sem("weight_free"), 1)

            def begin(key):
                b = before[ids[key]]
                if b is not None:
                    pe.wait_ge(sem("drained_by_" + drains[b]), freed_count[b])
                return bank(key)

            def columns(stage_name, n, rhs, width=P, tokens=S):
                per = 512 // tokens
                for job in range(-(-n // per)):
                    b = begin((stage_name, job))
                    for i in range(per * job, min(n, per * job + per)):
                        w = next_weights()
                        at = (i % per) * tokens
                        for k in range(NK):
                            mm(b[0:width, at:at + tokens], w[:, k * width:(k + 1) * width], rhs[:, k, :], k == 0,
                               k == NK - 1, end=(k == NK - 1 and (i % per == per - 1 or i == n - 1)))

            def token_rows(stage_name, lhs, nk, n, parts, tiles=NT):
                bs = [begin((stage_name, i)) for i in range(tiles * len(parts))]
                per = max(1, SLOT // n)
                for k in range(nk):
                    if k % per == 0:
                        w = next_weights()
                    for t in range(tiles):
                        for h, (lo, width) in enumerate(parts):
                            at = (k % per) * n + lo
                            mm(bs[t * len(parts) + h][:, 0:width], lhs[:, k, t * P:(t + 1) * P], w[:, at:at + width],
                               k == 0, k == nk - 1, end=k == nk - 1)

            def turn_tokens(stage_name, src, ready, count):
                for i in range(4):
                    t = i // 2
                    b = begin((stage_name, i))
                    if i % 2 == 0:
                        pe.wait_ge(sem(ready), count[t])
                    for n in range(4):
                        k = 4 * (i % 2) + n
                        mm(b[:, n * P:(n + 1) * P], src[:, t, k * P:(k + 1) * P], ident, True, True, end=n == 3, turn=True)

            half = [(0, 512), (512, 512)]
            pe.sem_inc(sem("weight_free"), RING)
            if on("z"):
                pe.wait_ge(sem("early_consts_loaded"), 16)
                turn_tokens("xT_mix", xn, "xn_ready", [1, 2])
                wait_drained(pe, ("xT_mix", 3))
                columns("xr", NK, xT)
                for n in "kv":
                    columns(n + "c", 2, xT)
                columns("k_sel", 2, xT)
                columns("k_win", 2, xT)
                for stage_name in ("lru_r", "lru_i"):
                    w = next_weights()
                    if stage_name == "lru_r":
                        pe.wait_ge(sem("conv_done"), 1)
                    for pair in range(4):
                        b = begin((stage_name, pair))
                        for i in range(2):
                            j = 2 * pair + i
                            mm(b[:, i * S:(i + 1) * S], w[:, j * P:(j + 1) * P], xc[:, j, :], True, True, end=i == 1)
                token_rows("v_sw", xT, NK, 512, [(0, 512)])
                w = next_weights()
                b = begin(("nsa_gate", 0))
                for t in range(NT):
                    for k in range(NK):
                        mm(b[:, t * 48:(t + 1) * 48], xT[:, k, t * P:(t + 1) * P], w[:, k * 48:(k + 1) * 48],
                           k == 0, k == NK - 1, end=(t == 1 and k == NK - 1))
            if on("cmp"):
                for n in "kv":
                    bs = [begin(("hid_" + n, h)) for h in range(2)]
                    wait_drained(pe, (n + "c", 0))
                    for lp in range(16):
                        if lp % 4 == 0:
                            w = next_weights()
                        src = cmp_in[n][lp // 8].rearrange("p g (c l) -> p g c l", l=8)
                        rhs = src[:, :, lp // 8:lp // 8 + NCMP, lp % 8]
                        for h in range(2):
                            at = (lp % 4) * 256 + h * P
                            mm(bs[h][:, 0:4 * NCMP].rearrange("p (g c) -> p g c", g=4), w[:, at:at + P], rhs,
                               lp == 0, lp == 15, end=lp == 15)
                columns("q", NK, xT)
                pe.wait_ge(sem("consts_loaded"), 16)
                wait_drained(pe, ("hid_v", 1))
                b = begin(("k_cmp", 0))
                for s in range(2):
                    for h in range(2):
                        rhs = hidT["k"][:, h, :].rearrange("p (m s c) -> p s m c", m=2, s=2)[:, s]
                        mm(b[s * HD:(s + 1) * HD, 0:2 * NCMP].rearrange("p (m c) -> p m c", m=2), c("w2_k", 2, HD)[:, h, :],
                           rhs, h == 0, h == 1, end=(s == 1 and h == 1))
                b = begin(("v_cmp", 0))
                for g in range(GROUPS):
                    for h in range(2):
                        mm(b[0:NCMP, g * HD:(g + 1) * HD], hidT["v"][:, h, g * NCMP:(g + 1) * NCMP],
                           c("w2_v", 2, HD)[:, h, :], h == 0, h == 1, end=(g == 3 and h == 1))
                wait_drained(pe, ("k_cmp", 0))
                wait_drained(pe, ("q", 3))
                for t in range(NT):
                    for s in range(2):
                        b = begin(("cmp_score", 2 * t + s))
                        for j in range(NK):
                            mm(b[:, j * NCMP:(j + 1) * NCMP], qT[s * HD:(s + 1) * HD, j, t * P:(t + 1) * P],
                               k_cmp[s * HD:(s + 1) * HD, j // 4, :], True, True, end=j == NK - 1)
                columns("att_gate", 2 * NZ0, xT)
                for t in range(NT):
                    pe.wait_ge(sem("cmp_probs"), t + 1)
                    for q4 in range(4):
                        b = begin(("cmp_turn", t * 4 + q4))
                        for i in range(4):
                            mm(b[0:NCMP, i * P:(i + 1) * P], cmp_s[:, t, q4 * 4 + i, :], ident, True, True, end=i == 3,
                               turn=True)
            if on("att"):
                wait_drained(pe, ("v_cmp", 0))
                wait_drained(pe, ("cmp_turn", 7))
                for kind, u in attention_order():
                    b = begin(("att_" + kind, u))
                    if kind == "gate":
                        for i in range(2):
                            w = next_weights()
                            for k in range(NK):
                                mm(b[:, i * S:(i + 1) * S], w[:, k * P:(k + 1) * P], xT[:, k, :], k == 0, k == NK - 1,
                                   end=(i == 1 and k == NK - 1))
                        continue
                    j, s, t = UNITS[u]
                    m, nk = j // 4, (t + 1) * P
                    h64 = slice(s * HD, (s + 1) * HD)
                    if kind == "score":
                        for br in range(2):
                            mm(b[:, br * nk:(br + 1) * nk], qT[h64, j, t * P:(t + 1) * P], kT[br][h64, m, 0:nk],
                               True, True, end=br == 1)
                    if kind == "turn":
                        pe.wait_ge(sem("att_diag"), u + 1)
                        E = att_E[u % 3] if t else att_E0[u % 3]
                        for br in range(2):
                            for kb in range(t + 1):
                                mm(b[:, (br * (t + 1) + kb) * P:(br * (t + 1) + kb + 1) * P],
                                   E[:, br, kb * P:(kb + 1) * P], att_diag[u % 3][:, br, :], True, True,
                                   end=(br == 1 and kb == t))
                    if kind == "value":
                        wait_drained(pe, ("att_turn", u))
                        g = 2 * m + s
                        hd = 2 * j + s
                        mm(b[h64, 0:P], v_cmp[0:NCMP, g * HD:(g + 1) * HD], cmp_PT[0:NCMP, hd, t * P:(t + 1) * P],
                           True, False)
                        for br in range(2):
                            for kb in range(t + 1):
                                last = br == 1 and kb == t
                                at = br * 256 + g * HD
                                mm(b[h64, 0:P], v_sw[:, kb, at:at + HD], att_PT[u % 2][:, br * (t + 1) + kb, :],
                                   False, last, end=last)
            if on("mix"):
                pe.wait_ge(sem("y_ready"), 1)
                token_rows("mix_out", yT, NK, D, half)
            if on("ffn"):
                pe.wait_ge(sem("memT_loaded"), 16)
                columns("mem_k0", 2, memT)
                wt["owed"] += 1
                turn_tokens("xT_ffn", xn, "xn_ready", [3, 4])
                first_slot = wt["n"]
                assert first_slot == FFN_SLOT
                down = [begin(("ffn_down", i)) for i in range(4)]

                def split_mm(o, lhsT, rhs, start, stop, end=False, used=False):
                    ins = pe.matmul(o, lhsT, rhs, start=start, stop=stop)
                    if end:
                        ins.then_inc(sem("psum_filled"), 1)
                    elif used:
                        ins.then_inc(sem("split_used"), 1)

                for n, (kind, f) in enumerate(ffn_order()):
                    pe.wait_ge(sem("weight_free"), RING + first_slot + n + 1)
                    pe.wait_ge(sem("slot_high"), n + 1)
                    w = w_split[n % SPLITS]
                    if kind in ("gate", "up"):
                        b = begin(("ffn_" + kind, f))
                        for k in range(NK):
                            cols = slice(k * P, (k + 1) * P)
                            if n == 0 and k % 4 == 0:
                                pe.wait_ge(sem("x_split"), k // 2 + 2)
                            split_mm(b[:, :], w[:, 0, cols], x_split[:, k].rearrange("p a s -> p (a s)"), k == 0, False,
                                     used=k == 0 and n > 0)
                            split_mm(b[:, 0:S], w[:, 1, cols], x_split[:, k, 0, :], False, k == NK - 1,
                                     end=k == NK - 1)
                    else:
                        pe.wait_ge(sem("act_split"), f + 1)
                        for t in range(NT):
                            for h in range(2):
                                for i, (a, v) in enumerate(((0, 0), (0, 1), (1, 0))):
                                    split_mm(down[2 * t + h][:, :], act_split[f % 3][:, a, t * P:(t + 1) * P],
                                             w[:, v, h * 512:(h + 1) * 512], f == 0 and i == 0, f == NF - 1 and i == 2,
                                             end=f == NF - 1 and i == 2, used=i == 0 and t == 0 and h == 0)
                wt["n"] += len(ffn_order())
                wt["given"] = True
            if on("ple"):
                token_rows("mem_v0", memT, NK, 256, [(0, 256)])
                turn_tokens("xT_ple", x, "x_ready", [1, 2])
                wait_drained(pe, ("xT_ple", 3))
                token_rows("ple_gate", xT, NK, D, half)
                token_rows("ple_proj", c("pT", 2, S), 2, D, half)
            for l in range(1):
                if l == 0 and on("gla"):
                    turn_tokens("xT_in0", x, "x_ready", [3, 4])
                    wait_drained(pe, ("xT_in0", 3))
                    columns("gla_q", GH, xT, GDK)
                    columns("gla_k", GH, xT, GDK)
                    b = begin(("gla_g1", 0))
                    w = next_weights()
                    for k in range(NK):
                        mm(b[0:16, 0:S], w[:, k * 16:(k + 1) * 16], xT[:, k, :], k == 0, k == NK - 1, end=k == NK - 1)
                    wait_drained(pe, ("gla_g1", 0))
                    for pair in range(2):
                        b = begin(("gla_gate", pair))
                        for i in range(2):
                            h = 2 * pair + i
                            mm(b[0:GDK, i * S:(i + 1) * S], c("w_gate2")[0:16, h * GDK:(h + 1) * GDK], g1T[0:16, :],
                               True, True, end=i == 1)
                    columns("qm0", 2, xT)
                    parts = [(0, 384), (384, 384)]
                    token_rows("gla_v", xT, NK, GH * GDV, parts)
                    pe.wait_ge(sem("gla_decayed"), 1)
                    for t in range(NT):
                        b = begin(("gla_kendT", t))
                        for h in range(GH):
                            mm(b[:, h * GDK:(h + 1) * GDK], gke[0:GDK, h, t * P:(t + 1) * P], ident[0:GDK, 0:GDK],
                               True, True, end=h == GH - 1, turn=True)
                    b = begin(("gla_intra", 0))
                    for n in range(NCH):
                        for h in range(GH):
                            o = (n % 2) * CH
                            mm(b[o:o + CH, (n // 2) * 256 + h * CH:(n // 2) * 256 + (h + 1) * CH],
                               gkt[0:GDK, h, n * CH:(n + 1) * CH], gq[0:GDK, h, n * CH:(n + 1) * CH], True, True,
                               end=(n == NCH - 1 and h == GH - 1))
                    wait_drained(pe, ("gla_kendT", 1))
                    wait_drained(pe, ("gla_v", 3))
                    for n in range(NCH - 1):
                        o = slice((n % 2) * CH, (n % 2 + 1) * CH)
                        for hp in range(2):
                            b = begin(("gla_kv", 2 * n + hp))
                            for i in range(2):
                                h = 2 * hp + i
                                mm(b[0:GDK, i * GDV:(i + 1) * GDV], kendT[o, n // 2, h, :],
                                   gv[o, n // 2, h * GDV:(h + 1) * GDV], True, True, end=i == 1)
                    token_rows("gla_r", xT, NK, GH * GDV, parts)
                    wait_drained(pe, ("gla_intra", 0))
                    pe.wait_ge(sem("gla_state"), NCH - 1)
                    for t in range(NT):
                        for hp in range(2):
                            b = begin(("gla_o", 2 * t + hp))
                            for par in range(2):
                                n = 2 * t + par
                                o = slice(par * CH, (par + 1) * CH)
                                for i in range(2):
                                    h = 2 * hp + i
                                    vcol = slice(h * GDV, (h + 1) * GDV)
                                    last = par == 1 and i == 1
                                    mm(b[o, i * GDV:(i + 1) * GDV], attnT[o, t, h, :], gv[o, t, vcol], True, n == 0)
                                    if n:
                                        mm(b[o, i * GDV:(i + 1) * GDV], gq[0:GDK, h, n * CH:(n + 1) * CH],
                                           state[0:GDK, n - 1, vcol], False, True, end=last)
                if on(f"memat{l}"):
                    wait_drained(pe, (f"qm{l}", 0))
                    for kind, u in pipelined(len(MEM_UNITS)):
                        m, t = MEM_UNITS[u]
                        if kind == "score":
                            for s in range(2):
                                b = begin((f"mem_score{l}", 2 * u + s))
                                h64 = slice(s * HD, (s + 1) * HD)
                                mm(b[:, 0:S], qmT[h64, m, t * P:(t + 1) * P], mem_k[h64, l, m, :], True, True, end=True)
                            continue
                        b = begin((f"mem_{kind}{l}", 2 * u))
                        if kind == "turn":
                            pe.wait_ge(sem("mem_diag"), l * len(MEM_UNITS) + u + 1)
                            for s in range(2):
                                for kb in range(2):
                                    mm(b[:, (2 * s + kb) * P:(2 * s + kb + 1) * P], mem_E[u % 3][:, s, kb * P:(kb + 1) * P],
                                       mem_diag[u % 3][:, s, :], True, True, end=(s == 1 and kb == 1))
                        if kind == "value":
                            wait_drained(pe, (f"mem_turn{l}", 2 * u))
                            for s in range(2):
                                h64 = slice(s * HD, (s + 1) * HD)
                                for kb in range(2):
                                    at = (2 * m + s) * HD
                                    mm(b[h64, 0:P], mem_v[:, l, kb, at:at + HD], mem_PT[u % 2][:, 2 * s + kb, :],
                                       kb == 0, kb == 1, end=(s == 1 and kb == 1))
                if l == 0 and on("memat0"):
                    pe.wait_ge(sem("mix_ready"), 2)
                    for pair in range(3):
                        b = begin(("gla_mixT", pair))
                        for i in range(2):
                            for t in range(NT):
                                k = 2 * pair + i
                                mm(b[:, (i * 2 + t) * P:(i * 2 + t + 1) * P], mixin[:, t, k * P:(k + 1) * P], ident,
                                   True, True, end=(i == 1 and t == 1), turn=True)
                if on(f"out{l}"):
                    wait_drained(pe, (f"mem_value{l}", 2 * len(MEM_UNITS) - 2))
                    if l == 0:
                        wait_drained(pe, ("gla_mixT", 2))
                    token_rows(f"out{l}", mixT, NK, D, half)
                if on(f"peer{l}"):
                    n0 = 5 + 4 * l
                    turn_tokens(f"xT_peer{l}", x, "x_ready", [n0, n0 + 1])
                    wait_drained(pe, (f"xT_peer{l}", 3))
                    for kind, h in peer_head_order():
                        key = (f"peer_{kind}{l}", h)
                        b = begin(key)
                        if kind == "q":
                            for q in range(2):
                                w = next_weights()
                                for k in range(NK):
                                    mm(b[:, q * S:(q + 1) * S], w[:, k * P:(k + 1) * P], xT[:, k, :], k == 0,
                                       k == NK - 1, end=(q == 1 and k == NK - 1))
                        else:
                            wait_drained(pe, (f"peer_q{l}", h))
                            for t in range(NT):
                                for q in range(2):
                                    mm(b[:, (2 * t + q) * P:(2 * t + q + 1) * P], pq[h % 2][:, q, t * P:(t + 1) * P],
                                       c("keysT", 2, 2, PN)[:, l, q, :], True, True, end=(t == 1 and q == 1))
                    if l == 0:
                        columns("mem_k1", 2, memT)
                        token_rows("mem_v1", memT, NK, 256, [(0, 256)])
            def add_chunk(l, t, n):
                for s in v_chunk(n):
                    k = PE_SLABS.index(s)
                    pe.wait_ge(sem("diag_ready"), (l * NT + t) * len(PE_SLABS) + k + 1)
                    pe.wait_ge(sem(f"gathered{s % GBUF}"), 16 * (uses_before(l, t, 1, s) + 1))
                    last = k == len(PE_SLABS) - 1
                    for h in range(2):
                        key = (f"sum{l}_{t}", h)
                        b = begin(key) if k == 0 else bank(key)
                        ins = pe.matmul(b[:, :], diag[k % DIAGS], gbuf[s % GBUF][:, h * 512:(h + 1) * 512], start=k == 0,
                                        stop=last)
                        if h == 1:
                            ins.then_inc(sem(f"buffer_free{s % GBUF}"), 1)
                if n == CHUNKS - 1:
                    wait_freed(pe, l, t, 1, PE_SLABS[-1])
                    pe.sem_inc(sem("psum_filled"), 2)

            def peer_group(t, g):
                columns(f"peer_q1_{t}_{g}", 2 * TH, tile_xT, tokens=P)
                wait_drained(pe, (f"peer_q1_{t}_{g}", 0))
                b = begin((f"peer_s1_{t}_{g}", 0))
                for hp in range(2 * TH):
                    mm(b[:, hp * P:(hp + 1) * P], tile_pq(g)[:, hp, :], c("keysT", 2, 2, PN)[:, 1, hp % 2, :],
                       True, True, end=hp == 2 * TH - 1)

            if on("peer0"):
                for n in range(CHUNKS):
                    add_chunk(0, 0, n)
            for t in range(NT if on("peer1") else 0):
                def turn_tile(stage_name, nth):
                    pe.wait_ge(sem("x_ready"), nth)
                    for i in range(2):
                        b = begin((stage_name, i))
                        for n in range(4):
                            k = 4 * i + n
                            mm(b[:, n * P:(n + 1) * P], x[:, t, k * P:(k + 1) * P], ident, True, True, end=n == 3,
                               turn=True)
                    wait_drained(pe, (stage_name, 1))

                def heads_turned(key, E, diag, blocks):
                    b = begin(key)
                    for n, (group, kb) in enumerate(blocks):
                        for m, g in enumerate(group):
                            mm(b[:, n * P:(n + 1) * P], E[:, g, kb * P:(kb + 1) * P], diag(g), m == 0,
                               m == len(group) - 1, end=(n == len(blocks) - 1 and m == len(group) - 1))

                turn_tile(f"xT_in1_{t}", 7 + 2 * t)
                columns(f"dil_k_{t}", DSLOTS, tile_xT, tokens=P)
                token_rows(f"dil_v_{t}", tile_xT, NK, 768, [(0, 384), (384, 384)], tiles=1)
                columns(f"dil_q_{t}", 18, tile_xT, tokens=P)
                columns(f"qm1_{t}", 2, tile_xT, tokens=P)
                wait_drained(pe, (f"dil_q_{t}", 4))
                nk = (t + 1) * P
                for kind, u in pipelined(DSLOTS):
                    key = (f"dil_{kind}_{t}", 2 * u)
                    if kind == "score":
                        for part in range(t + 1):
                            b = begin((key[0], 2 * u + part))
                            gs = [0, 1, 2] if t == 0 else ([0, 1] if part == 0 else [2])
                            for g in gs:
                                at = (g - gs[0]) * nk
                                mm(b[:, at:at + nk], dqT[:, u * 3 + g, :], dkT[:, u, 0:nk], True, True, end=g == gs[-1])
                    if kind == "turn":
                        pe.wait_ge(sem("dil_diag"), DSLOTS * t + u + 1)
                        heads_turned(key, (dil_E if t else dil_E0)[u % 3], lambda g: dil_diag[u % 3],
                                     [((0, 1, 2), kb) for kb in range(t + 1)])
                    if kind == "value":
                        b = begin(key)
                        wait_drained(pe, (f"dil_turn_{t}", 2 * u))
                        for kb in range(t + 1):
                            mm(b[:, 0:P], dv[:, kb, u * P:(u + 1) * P], dil_PT[u % 2][:, kb, :], kb == 0, kb == t,
                               end=kb == t)
                wait_drained(pe, (f"qm1_{t}", 0))
                for kind, m in pipelined(2):
                    key = (f"mem_{kind}1_{t}", 2 * m)
                    if kind == "score":
                        for s in range(2):
                            b = begin((key[0], 2 * m + s))
                            h64 = slice(s * HD, (s + 1) * HD)
                            mm(b[:, 0:S], tile_qmT[h64, m, :], mem_k[h64, 1, m, :], True, True, end=True)
                    if kind == "turn":
                        pe.wait_ge(sem("mem_diag"), len(MEM_UNITS) + 2 * t + m + 1)
                        heads_turned(key, mem1_E[m], lambda g: mem1_diag[m][:, g, :],
                                     [((g,), kb) for g in range(2) for kb in range(2)])
                    if kind == "value":
                        b = begin(key)
                        wait_drained(pe, (f"mem_turn1_{t}", 2 * m))
                        for s in range(2):
                            for kb in range(2):
                                at = (2 * m + s) * HD
                                mm(b[s * HD:(s + 1) * HD, 0:P], mem_v[:, 1, kb, at:at + HD], mem1_PT[m][:, 2 * s + kb, :],
                                   kb == 0, kb == 1, end=(s == 1 and kb == 1))
                wait_drained(pe, (f"mem_value1_{t}", 2))
                token_rows(f"out1_{t}", tile_mixT, NK, D, half, tiles=1)
                turn_tile(f"xT_peer1_{t}", 8 + 2 * t)
                peer_group(t, 0)
                for n in range(CHUNKS):
                    if group_at(n) is not None:
                        peer_group(t, group_at(n))
                    add_chunk(t, 1 - t, n)
            if on("peer1"):
                for n in range(CHUNKS):
                    add_chunk(1, 1, n)
            if dump is not None:
                pe.sem_inc(sem("dbg_pe"), 1)

        @block.sync
        def _(sp):
            for t in range(NT):
                sp.dma_start(x[:, t, :], x_in[t * P:(t + 1) * P, :]).then_inc(sem(f"x_loaded{t}"), 16)
                if t == 0:
                    sp.dma_start(cst[:, 0:n_early], consts[:, 0:n_early]).then_inc(sem("early_consts_loaded"), 16)
            with sp.Fori(0, -(-wt["n"] // RING)) as i:
                for s in range(RING):
                    sp.wait_ge(sem("weight_free"), i * RING + (s + 1))
                    sp.dma_start(ring[:, s, :], weights[bass.ds(i * RING + s, 1), :, :].rearrange("a p n -> p (a n)"))\
                      .then_inc(sem(f"weight_loaded{s}"), 16)
            if dump is None:
                for t in range(NT):
                    sp.wait_ge(sem("x_final"), t + 1)
                    sp.dma_start(out[t * P:(t + 1) * P, :], x[:, t, :]).then_inc(sem("stored"), 16)
                sp.wait_ge(sem("stored"), 16 * NT)
            else:
                for en in ("act", "dve", "pe", "pool"):
                    sp.wait_ge(sem("dbg_" + en), 1)
                sp.dma_start(out.rearrange("(t p) d -> p t d", p=P), x[:, :, :]).then_inc(sem("stored"), 16)
                sp.wait_ge(sem("stored"), 16)

        @block.scalar
        def _(act):
            done, settle, count = counter(act)

            def drain(key, pieces):
                wait_filled(act, key)
                for n, (o, i, f, kw) in enumerate(pieces):
                    last = n == len(pieces) - 1
                    done(act.activation(o, i, f, **kw), "drained_by_act" if last else "act_step")

            def two(src):
                return src.rearrange("p (a s) -> p a s", a=2)

            def root(o, i, scale, eps, name):
                settle()
                done(act.activation(o, i, ACT.Sqrt, bias=c("eps")[:, eps:eps + 1], scale=scale), name)

            def rms_of_x(first):
                for t in range(NT):
                    if first:
                        act.wait_ge(sem(f"x_loaded{t}"), 16)
                        act.wait_ge(sem("early_consts_loaded"), 16)
                    done(act.activation(xn[:, t, :], x[:, t, :], ACT.Square, accum_out=stat[:, t:t + 1]), "act_step")
                    root(stat[:, 2 + t:3 + t], stat[:, t:t + 1], 1.0 / D, 0, "rms_ready")

            def squares_of_product(stage_name):
                for i in range(4):
                    wait_filled(act, (stage_name, i))
                    t, h = i // 2, i % 2
                    done(act.activation(tmp_tok[:, t, h * 512:(h + 1) * 512], bank((stage_name, i))[:, :], ACT.Square,
                                        accum_out=stat[:, 8 + i:9 + i]), "post_squares")

            def softmax_unit(nm_sem, n, parts, exp_sem):
                act.wait_ge(sem(nm_sem), n)
                for k, (tile, nm, total) in enumerate(parts):
                    last = k == len(parts) - 1
                    done(act.activation(tile, tile, ACT.Exp, bias=nm, accum_out=total), exp_sem if last else "act_step")

            def drain_mem_k(l):
                drain((f"mem_k{l}", 0), [(mem_k[:, l, :, :], two(bank((f"mem_k{l}", 0))[:, :]), ACT.Copy, {})])

            def drain_mem_v(l):
                for mt in range(2):
                    key = (f"mem_v{l}", mt)
                    drain(key, [(mem_v[:, l, mt, :], bank(key)[:, 0:256], ACT.Copy, {})])

            def routed(l, t):
                act.wait_ge(sem("peer_shifted"), (l * NT + t + 1) * TURNS)
                v = gate_w[t].rearrange("p h k -> p (h k)")
                done(act.activation(v, v, ACT.Exp), "peer_exp")

            def dotted(l, t):
                act.wait_ge(sem("peer_dots"), l * NT + t + 1)
                done(act.activation(hdot[t], hdot[t], ACT.Gelu), "peer_gelu")

            def diagonals(l, t, n):
                if n == 0:
                    act.wait_ge(sem("peer_weights"), l * NT + t + 1)
                for s in v_chunk(n):
                    k = PE_SLABS.index(s)
                    if k >= DIAGS:
                        wait_freed(act, l, t, 1, s - 4 * DIAGS)
                    elif l or t:
                        wait_freed(act, l if t else 0, 1 - t, 1, PE_SLABS[-1])
                    done(act.activation(diag[k % DIAGS], ident, ACT.Copy, scale=hdot[t][:, s:s + 1]), "diag_ready")

            def peer_group(t, g):
                for key, dst in (((f"peer_q1_{t}_{g}", 0), tile_pq(g)),
                                 ((f"peer_s1_{t}_{g}", 0), sc[t][:, 2 * TH * g:2 * TH * (g + 1), :])):
                    drain(key, [(dst, bank(key)[:, :].rearrange("p (a s) -> p a s", a=4), ACT.Copy, {})])

            def norm_root(t, n):
                act.wait_ge(sem("ln_var"), n + 1)
                root(stat[:, 50 + t:51 + t], stat[:, 43 + 2 * t:44 + 2 * t], 1.0, 1, "ln_std")

            def turned_tile(stage_name):
                for i in range(2):
                    key = (stage_name, i)
                    drain(key, [(tile_xT[:, 4 * i:4 * i + 4, :], bank(key)[:, :].rearrange("p (a s) -> p a s", a=4),
                                 ACT.Copy, {})])

            def drain_gate(n):
                dst, f = [(gma, ACT.Sigmoid if n < NZ0 else ACT.Copy), (gr, ACT.Copy), (gmr, ACT.Copy)][n // 4]
                i = n % 4
                drain(("att_gate", n), [(dst[:, 2 * i:2 * i + 2, :], two(bank(("att_gate", n))[:, :]), f, {})])
                if n in (3, 7, 11):
                    settle()
                    v = dst[:, 2 * NZ0 if n == 3 else 0:, :].rearrange("p k s -> p (k s)")
                    done(act.activation(v, v, ACT.Gelu_apprx_tanh if n == 7 else ACT.Sigmoid), "gates_shaped")

            def turned(stage_name):
                for i in range(4):
                    key = (stage_name, i)
                    drain(key, [(xT[:, 4 * (i % 2):4 * (i % 2) + 4, (i // 2) * P:(i // 2 + 1) * P],
                                 bank(key)[:, :].rearrange("p (a s) -> p a s", a=4), ACT.Copy, {})])

            rms_of_x(True)
            if on("z"):
                act.wait_ge(sem("lam_abs"), 1)
                done(act.activation(lam_t[:, 1, :], lam_t[:, 0, :], ACT.Exp, scale=-1.0), "lam_exp")
                act.wait_ge(sem("lam_w"), 1)
                done(act.activation(lam_t[:, 3, :], lam_t[:, 2, :], ACT.Ln), "lam_ln")
                for i in range(4):
                    act.wait_ge(sem("pad_zeroed"), 1)
                    drain(("xr", i), [(xr_pad[:, 2 * i:2 * i + 2, 3:], two(bank(("xr", i))[:, :]), ACT.Copy, {})])
                for n, br in (("k_sel", 0), ("k_win", 1)):
                    drain((n, 0), [(kT[br][:, :, :], two(bank((n, 0))[:, :]), ACT.Copy, {})])
                for name, dst, bias in (("lru_r", lru_a, "lru_ba"), ("lru_i", lru_i, "lru_bx")):
                    for i in range(4):
                        b = bank((name, i))
                        drain((name, i), [(dst[:, 2 * i + h, :], b[:, h * S:(h + 1) * S], ACT.Sigmoid,
                                           dict(bias=c(bias)[:, 2 * i + h:2 * i + h + 1])) for h in range(2)])
                act.wait_ge(sem("lam_rate"), 1)
                settle()
                for j in range(NK):
                    done(act.activation(lru_t[:, j, :], lru_a[:, j, :], ACT.Tanh, scale=lam_t[:, 8, j:j + 1]), "lru_tanh")
                settle()
                for j in range(NK):
                    done(act.activation(lru_a[:, j, :], lru_a[:, j, :], ACT.Exp, scale=lam_t[:, 9, j:j + 1]), "lru_exp")
                for t in range(NT):
                    drain(("v_sw", t), [(v_sw[:, t, :], bank(("v_sw", t))[:, :], ACT.Copy, {})])
                drain(("nsa_gate", 0), [(nsa_g.rearrange("p t b h -> p (t b h)"), bank(("nsa_gate", 0))[:, 0:96],
                                         ACT.Sigmoid, {})])
                act.wait_ge(sem("lru_b2"), 1)
                done(act.activation(lru_t.rearrange("p a s -> p (a s)"), lru_t.rearrange("p a s -> p (a s)"), ACT.Sqrt,
                                    scale=2.0), "lru_root")
            if on("cmp"):
                for n in "kv":
                    for h in range(2):
                        key = ("hid_" + n, h)
                        drain(key, [(hidT[n][:, h, :], bank(key)[:, 0:4 * NCMP], ACT.Gelu_apprx_tanh, {})])
                for i in range(4):
                    drain(("q", i), [(qT[:, 2 * i:2 * i + 2, :], two(bank(("q", i))[:, :]), ACT.Copy,
                                      dict(scale=HD ** -0.5))])
                for t in range(NT):
                    act.wait_ge(sem("cmp_shifted"), t + 1)
                    v = cmp_s[:, t].rearrange("p h c -> p (h c)")
                    done(act.activation(v, v, ACT.Exp), "cmp_exp")
                for g in range(NZ0):
                    drain_gate(g)
                for i in range(8):
                    key = ("cmp_turn", i)
                    t, q4 = i // 4, i % 4
                    act.wait_ge(sem("lru_scanned"), 1)
                    drain(key, [(cmp_PT[0:NCMP, q4 * 4:q4 * 4 + 4, t * P:(t + 1) * P],
                                 bank(key)[0:NCMP, :].rearrange("p (a s) -> p a s", a=4), ACT.Copy, {})])
            if on("att"):
                for kind, u in attention_order():
                    key = ("att_" + kind, u)
                    b = bank(key)
                    if kind == "score":
                        E = att_E[u % 3] if UNITS[u][2] else att_E0[u % 3]
                        softmax_unit("att_max", u + 1, [(E[:, br, :], att_nm[:, u % 3, br:br + 1],
                                                         att_sum[:, u % 3, br:br + 1]) for br in range(2)], "att_exp")
                    if kind == "gate":
                        drain_gate(u)
                    if kind == "turn":
                        n = 2 * (UNITS[u][2] + 1)
                        drain(key, [(att_PT[u % 2][:, 0:n, :], b[:, 0:n * P].rearrange("p (a s) -> p a s", a=n), ACT.Copy,
                                     {})])
            if on("mix"):
                squares_of_product("mix_out")
                for t in range(NT):
                    act.wait_ge(sem("post_sum"), t + 1)
                    root(stat[:, 16 + t:17 + t], stat[:, 12 + t:13 + t], 1.0 / D, 0, "post_rms")
            if on("ffn"):
                for t in range(NT):
                    act.wait_ge(sem("x_mixed"), t + 1)
                    done(act.activation(xn[:, t, :], x[:, t, :], ACT.Square, accum_out=stat[:, t:t + 1]), "act_step")
                    root(stat[:, 2 + t:3 + t], stat[:, t:t + 1], 1.0 / D, 0, "rms_ready")
                drain_mem_k(0)
                order = ffn_order()

                def slot_high(n):
                    act.wait_ge(sem("slot_masked"), n + 1)
                    done(act.activation(w_split[n % SPLITS][:, 0, :], masked[n % 2], ACT.Copy), "slot_high")

                for n in range(3):
                    slot_high(n)
                for n, (kind, f) in enumerate(order):
                    if n + 3 < len(order):
                        slot_high(n + 3)
                    if kind == "down":
                        continue
                    wait_filled(act, ("ffn_" + kind, f))
                    if f >= 2:
                        act.wait_ge(sem("act_split"), f - 1)
                    dst = gate_s if kind == "gate" else up_s
                    done(act.activation(dst[f % 2], bank(("ffn_" + kind, f))[:, S:2 * S], ACT.Copy), "ffn_low")
                    if kind == "up":
                        wait_drained(act, ("ffn_gate", f))
                        done(act.activation(gate_s[f % 2], gate_s[f % 2], ACT.Silu), "ffn_silu")
                squares_of_product("ffn_down")
                for t in range(NT):
                    act.wait_ge(sem("post_sum"), NT + t + 1)
                    root(stat[:, 16 + t:17 + t], stat[:, 12 + t:13 + t], 1.0 / D, 0, "post_rms")
            if on("ple"):
                drain_mem_v(0)
                turned("xT_ple")
                for i in range(4):
                    t, h = i // 2, i % 2
                    act.wait_ge(sem("ple_biased"), i + 1)
                    v = tmp_tok[:, t, h * 512:(h + 1) * 512]
                    done(act.activation(v, v, ACT.Sigmoid), "ple_sigmoid")
            if on("gla"):
                turned("xT_in0")
                for name, dst, scale in (("gla_q", gq, GDK ** -0.5), ("gla_k", gk, 1.0)):
                    for i in range(2):
                        drain((name, i), [(dst[0:GDK, 2 * i:2 * i + 2, :], two(bank((name, i))[0:GDK, :]), ACT.Copy,
                                           dict(scale=scale))])
                drain(("gla_g1", 0), [(g1T[0:16, :], bank(("gla_g1", 0))[0:16, 0:S], ACT.Copy, {})])
                act.wait_ge(sem("gla_abs"), 1)
                done(act.activation(ge[0:GDK], ge[0:GDK], ACT.Exp, scale=-1.0), "act_step")
                settle()
                done(act.activation(ge[0:GDK], ge[0:GDK], ACT.Ln, bias=c("eps")[0:GDK, 2:3]), "gla_softplus")
                drain(("qm0", 0), [(qmT[:, :, :], two(bank(("qm0", 0))[:, :]), ACT.Copy, dict(scale=HD ** -0.5))])
                act.wait_ge(sem("gla_cumsum"), 1)
                done(act.activation(geb[0:GDK], gb[0:GDK], ACT.Exp), "gla_exp")
                done(act.activation(gf[0:GDK], gb[0:GDK], ACT.Exp, scale=-1.0), "gla_exp")
                act.wait_ge(sem("gla_tail"), 1)
                done(act.activation(gt[0:GDK], gt[0:GDK], ACT.Exp), "gla_exp")
                for name, dst, f in (("gla_v", gv, ACT.Copy), ("gla_r", grs, ACT.Silu)):
                    for i in range(4):
                        t, h = i // 2, i % 2
                        drain((name, i), [(dst[:, t, h * 384:(h + 1) * 384], bank((name, i))[:, 0:384], f, {})])
                for i in range(4):
                    wait_filled(act, ("gla_o", i))
                    for h in range(2):
                        col = 20 + 2 * i + h
                        done(act.activation(tmp_sq[:, 0:GDV], bank(("gla_o", i))[:, h * GDV:(h + 1) * GDV], ACT.Square,
                                            accum_out=stat[:, col:col + 1]), "act_step")
                        settle()
                root(stat[:, 32:40], stat[:, 20:28], 1.0 / GDV, 0, "gla_rms")
            for l in range(1):
                if on(f"memat{l}"):
                    for kind, u in pipelined(len(MEM_UNITS)):
                        key = (f"mem_{kind}{l}", 2 * u)
                        if kind == "score":
                            softmax_unit("mem_max", l * len(MEM_UNITS) + u + 1,
                                         [(mem_E[u % 3][:, s, :], att_nm[:, u % 3, s:s + 1], att_sum[:, u % 3, s:s + 1])
                                          for s in range(2)], "mem_exp")
                        if kind == "turn":
                            drain(key, [(mem_PT[u % 2][:, :, :], bank(key)[:, :].rearrange("p (a s) -> p a s", a=4),
                                         ACT.Copy, {})])
                if l == 0 and on("memat0"):
                    for pair in range(3):
                        key = ("gla_mixT", pair)
                        drain(key, [(mixT[:, 2 * pair:2 * pair + 2, :], two(bank(key)[:, :]), ACT.Copy, {})])
                if on(f"out{l}"):
                    for t in range(NT):
                        norm_root(t, t)
                if on(f"peer{l}"):
                    turned(f"xT_peer{l}")
                    for kind, h in peer_head_order():
                        key = (f"peer_{kind}{l}", h)
                        if kind == "q":
                            drain(key, [(pq[h % 2], two(bank(key)[:, :]), ACT.Copy, {})])
                        else:
                            drain(key, [(sc[t][:, 2 * h:2 * h + 2, :],
                                         bank(key)[:, t * 2 * P:(t + 1) * 2 * P].rearrange("p (a s) -> p a s", a=2),
                                         ACT.Copy, {}) for t in range(NT)])
                    if l == 0:
                        drain_mem_k(1)
                        drain_mem_v(1)
                    for t in range(NT):
                        routed(0, t)
                        if t == 0:
                            dotted(0, 0)
                            for n in range(CHUNKS):
                                diagonals(0, 0, n)
                            norm_root(0, 2)
            for t in range(NT if on("peer1") else 0):
                turned_tile(f"xT_in1_{t}")
                if t == 1:
                    for r in range(10, len(ROWS)):
                        act.wait_ge(sem("rows_used"), r - NROW + 1)
                        load_row(act, r)
                cols = slice(t * P, (t + 1) * P)
                for i in range(2):
                    n = min(4, DSLOTS - 4 * i)
                    key = (f"dil_k_{t}", i)
                    drain(key, [(dkT[:, 4 * i:4 * i + n, cols],
                                 bank(key)[:, 0:n * P].rearrange("p (a s) -> p a s", a=n), ACT.Copy, {})])
                for h in range(2):
                    key = (f"dil_v_{t}", h)
                    drain(key, [(dv[:, t, h * 384:(h + 1) * 384], bank(key)[:, 0:384], ACT.Copy, {})])
                for i in range(5):
                    n = min(4, 18 - 4 * i)
                    key = (f"dil_q_{t}", i)
                    drain(key, [(dqT[:, 4 * i:4 * i + n, :], bank(key)[:, 0:n * P].rearrange("p (a s) -> p a s", a=n),
                                 ACT.Copy, {})])
                key = (f"qm1_{t}", 0)
                drain(key, [(tile_qmT[:, :, :], bank(key)[:, 0:2 * P].rearrange("p (a s) -> p a s", a=2), ACT.Copy,
                             dict(scale=HD ** -0.5))])
                for n in range(CHUNKS):
                    name, what = PIECES.get(n, ("wait", None))
                    if name == "dil":
                        for kind, u in what:
                            if kind == "score":
                                E = (dil_E if t else dil_E0)[u % 3].rearrange("p g k -> p (g k)")
                                softmax_unit("dil_max", DSLOTS * t + u + 1,
                                             [(E, att_nm[:, u % 3, 0:1], att_sum[:, u % 3, 0:1])], "dil_exp")
                            if kind == "turn":
                                key = (f"dil_turn_{t}", 2 * u)
                                nb = t + 1
                                drain(key, [(dil_PT[u % 2][:, 0:nb, :],
                                             bank(key)[:, 0:nb * P].rearrange("p (a s) -> p a s", a=nb), ACT.Copy, {})])
                    if name == "mem":
                        for kind, m in what:
                            if kind == "score":
                                softmax_unit("mem_max", len(MEM_UNITS) + 2 * t + m + 1,
                                             [(mem1_E[m][:, s, :], att_nm[:, m, s:s + 1], att_sum[:, m, s:s + 1])
                                              for s in range(2)], "mem_exp")
                            if kind == "turn":
                                key = (f"mem_turn1_{t}", 2 * m)
                                drain(key, [(mem1_PT[m][:, :, :], bank(key)[:, :].rearrange("p (a s) -> p a s", a=4),
                                             ACT.Copy, {})])
                    if name == "out":
                        norm_root(t, 3 + 2 * t)
                        turned_tile(f"xT_peer1_{t}")
                peer_group(t, 0)
                dotted(t, 1 - t)
                for n in range(CHUNKS):
                    if group_at(n) is not None:
                        peer_group(t, group_at(n))
                    diagonals(t, 1 - t, n)
                routed(1, t)
                norm_root(1 - t, 4 + 2 * t)
            if on("peer1"):
                dotted(1, 1)
                for n in range(CHUNKS):
                    diagonals(1, 1, n)
                norm_root(1, 7)
            if dump is not None:
                settle()
                act.sem_inc(sem("dbg_act"), 1)

        @block.gpsimd
        def _(pool):
            pool.wait_ge(sem("psum_filled"), ids[("xT_mix", 3)] + 1)
            pool.dma_start(cst[:, n_early:], consts[:, n_early:]).then_inc(sem("consts_loaded"), 16)
            pool.dma_start(memT[:, :, :], memT_in.rearrange("(k p) s -> p k s", p=P)).then_inc(sem("memT_loaded"), 16)

            for n in range(NROW):
                load_row(pool, n)
            if on("att"):
                pool.wait_ge(sem("lru_scanned"), 1)
                pool.wait_ge(sem("gates_shaped"), 2)
                pool.tensor_tensor(xc, xc, gr, ALU.mult).then_inc(sem("pool_step"), 1)
                pool.wait_ge(sem("pool_step"), 1)
                pool.wait_ge(sem("gates_shaped"), 3)
                pool.tensor_tensor(xc, xc, gmr, ALU.mult).then_inc(sem("recurrence_gated"), 1)
            n = 0
            for l in range(2):
                if not on(f"peer{l}") and l or not on("out0"):
                    continue
                if l == 0:
                    for r in range(NROW, 10):
                        pool.wait_ge(sem("rows_used"), r - NROW + 1)
                        load_row(pool, r)
                if not on(f"peer{l}"):
                    continue
                for kind, t in PASSES:
                    table = peer_u if kind == "u" else peer_v
                    with pool.Fori(0, TURNS) as i:
                        pool.wait_ge(sem("peer_experts"), i + ((l * NT + t) * TURNS + 1))
                        for h in range(2):
                            pool.tensor_copy(stage[:, h * 16:(h + 1) * 16].bitcast(U32),
                                             expert[t][:, bass.ds(i * BODY + h * 16, 16)].bitcast(U32))\
                                .then_inc(sem("indices_staged"), 1)
                            pool.wait_ge(sem("indices_staged"), i * 2 + (n * TURNS * 2 + h + 1))
                            for k in range(16):
                                s = h * 16 + k
                                pool.wait_ge(sem(f"buffer_free{s % GBUF}"),
                                             i * (BODY // GBUF) + ((n * P + s) // GBUF + 1))
                                pool.sem_inc(sem("gather_turn"), 1)
                                pool.indirect_dma_start(gbuf[s % GBUF], None, table, bass.IndirectOffsetOnAxis(
                                    ap=stage[:, s:s + 1].bitcast(U32), axis=0)).then_inc(sem(f"gathered{s % GBUF}"), 16)
                    n += 1
            if dump is not None:
                pool.sem_inc(sem("dbg_pool"), 1)

        @block.vector
        def _(dve):
            done, settle, count = counter(dve)

            def step(ins, name="dve_step"):
                done(ins, name)
                settle()

            def row(n):
                dve.wait_ge(sem(row_sem(n)), 16 if n >= 10 else 16 * (n // NROW + 1))
                return rows[:, n % NROW, :]

            def turned(stage_name, gain):
                for i in range(4):
                    key = (stage_name, i)
                    wait_filled(dve, key)
                    ks = slice(4 * (i % 2), 4 * (i % 2) + 4)
                    done(dve.tensor_tensor(xT[:, ks, (i // 2) * P:(i // 2 + 1) * P],
                                           bank(key)[:, :].rearrange("p (a s) -> p a s", a=4),
                                           c(gain)[:, ks].unsqueeze(2).to_broadcast([P, 4, P]), ALU.mult),
                         "drained_by_dve")

            def normalised_x(first):
                for t in range(NT):
                    dve.wait_ge(sem("rms_ready"), first + t + 1)
                    step(dve.reciprocal(stat[:, 4 + t:5 + t], stat[:, 2 + t:3 + t]))
                    step(dve.tensor_scalar(xn[:, t, :], x[:, t, :], stat[:, 4 + t:5 + t], None, ALU.mult), "xn_ready")

            def post_norm(stage_name, first, g, name):
                gain = row(g)
                for t in range(NT):
                    dve.wait_ge(sem("post_squares"), 2 * first + 2 * t + 2)
                    step(dve.tensor_tensor(stat[:, 12 + t:13 + t], stat[:, 8 + 2 * t:9 + 2 * t],
                                           stat[:, 9 + 2 * t:10 + 2 * t], ALU.add), "post_sum")
                for t in range(NT):
                    dve.wait_ge(sem("post_rms"), first + t + 1)
                    step(dve.reciprocal(stat[:, 18 + t:19 + t], stat[:, 16 + t:17 + t]))
                    for h in range(2):
                        key = (stage_name, 2 * t + h)
                        cols = slice(h * 512, (h + 1) * 512)
                        step(dve.scalar_tensor_tensor(tmp_tok[:, t, cols], bank(key)[:, :], stat[:, 18 + t:19 + t],
                                                      gain[:, cols], ALU.mult, ALU.mult), "drained_by_dve")
                    step(dve.tensor_tensor(x[:, t, :], x[:, t, :], tmp_tok[:, t, :], ALU.add), name)
                dve.sem_inc(sem("rows_used"), 1)

            def layer_norm(n, g, b, name, tiles=(0, 1)):
                stats = peer_st
                for t in tiles:
                    for h in range(2):
                        done(dve.bn_stats(stats[:, 12 * t + 6 * h:12 * t + 6 * h + 6], x[:, t, h * 512:(h + 1) * 512]),
                             "dve_step")
                settle()
                for t in tiles:
                    step(dve.bn_aggr(stat[:, 42 + 2 * t:44 + 2 * t], stats[:, 12 * t:12 * t + 12]), "ln_var")
                gain, bias = row(g), row(b)
                for i, t in enumerate(tiles):
                    dve.wait_ge(sem("ln_std"), n + i + 1)
                    step(dve.reciprocal(stat[:, 54 + t:55 + t], stat[:, 50 + t:51 + t]))
                    step(dve.scalar_tensor_tensor(x[:, t, :], x[:, t, :], stat[:, 42 + 2 * t:43 + 2 * t], gain,
                                                  ALU.subtract, ALU.mult))
                    step(dve.scalar_tensor_tensor(x[:, t, :], x[:, t, :], stat[:, 54 + t:55 + t], bias,
                                                  ALU.mult, ALU.add), name)
                if tiles[-1] == NT - 1:
                    dve.sem_inc(sem("rows_used"), 2)

            def row_max(E, nm, name):
                step(dve.tensor_reduce(nm, E, AX, ALU.max, negate=True), name)

            def sixteen(t, g, n, val, pos, width):
                src = sc[t][:, 2 * TH * g:2 * TH * (g + 1), :].rearrange("p a n -> p (a n)")\
                    .rearrange("p (a n) -> p a n", n=width)
                lowest = -3.0e38
                left = rest.rearrange("p (a n) -> p a n", n=width)
                for r in range(n):
                    done(dve.max(val[:, r, 0:8], src[:, r, :]), "dve_step")
                settle()
                for r in range(n):
                    done(dve.match_replace(left[:, r, :], val[:, r, 0:8], src[:, r, :], lowest), "dve_step")
                for r in range(n):
                    done(dve.max_index(pos[:, r, 0:8].bitcast(U32), val[:, r, 0:8], src[:, r, :]), "dve_step")
                settle()
                for r in range(n):
                    done(dve.max(val[:, r, 8:16], left[:, r, :]), "dve_step")
                settle()
                for r in range(n):
                    done(dve.max_index(pos[:, r, 8:16].bitcast(U32), val[:, r, 8:16], left[:, r, :]), "dve_step")
                settle()

            def best_keys(l, t, g):
                wait_drained(dve, (f"peer_s0", (g + 1) * TH - 1) if l == 0 else (f"peer_s1_{t}_{g}", 0))
                sixteen(t, g, 2 * TH, top_v, top_i, PN)
                step(dve.tensor_copy(top_f, top_i.bitcast(U32)))

            def best_pairs(l, t, g):
                hs = slice(g * TH, (g + 1) * TH)
                grid = [P, TH, PK, PK]
                cand = sc[t][:, 2 * TH * g:2 * TH * (g + 1), :].rearrange("p a n -> p (a n)")\
                    .rearrange("p (h a b) -> p h a b", h=TH, a=PK)
                tv = top_v.rearrange("p (h q) k -> p h q k", q=2)
                step(dve.tensor_tensor(cand, tv[:, :, 0, :].unsqueeze(3).to_broadcast(grid),
                                       tv[:, :, 1, :].unsqueeze(2).to_broadcast(grid), ALU.add))
                sixteen(t, g, TH, best_v, best_j, PK * PK)
                step(dve.tensor_tensor(gate_w[t][:, hs, :], best_v, best_v[:, :, 0:1].to_broadcast([P, TH, PK]),
                                       ALU.subtract), "peer_shifted")

            def experts(l, t, g):
                grid = [P, TH, PK, PK]
                tf = top_f.rearrange("p (h q) k -> p h q k", q=2)
                for q, (pos, sel) in enumerate(((pos_a, sel_a), (pos_b, sel_b))):
                    op, val = (ALU.logical_shift_right, 4) if q == 0 else (ALU.bitwise_and, 15)
                    step(dve.tensor_scalar(pos_u.bitcast(U32), best_j.bitcast(U32), val, None, op))
                    step(dve.tensor_copy(pos, pos_u.bitcast(U32)))
                    iota = c("iota").unsqueeze(1).to_broadcast([P, TH * PK, PK])
                    oh = onehot.rearrange("p h k c -> p (h k) c")
                    step(dve.tensor_tensor(oh, iota, pos.rearrange("p h k -> p (h k)").unsqueeze(2)
                                           .to_broadcast([P, TH * PK, PK]), ALU.is_equal))
                    step(dve.tensor_tensor(onehot, onehot, tf[:, :, q, :].unsqueeze(2).to_broadcast(grid), ALU.mult))
                    step(dve.tensor_reduce(sel.rearrange("p h k -> p (h k)"), oh, AX, ALU.add))
                step(dve.tensor_scalar(sel_a, sel_a, float(PN), float(l * EXPERTS), ALU.mult, ALU.add))
                step(dve.tensor_tensor(expert[t][:, g * BODY:(g + 1) * BODY].bitcast(U32),
                                       sel_a.rearrange("p h k -> p (h k)"), sel_b.rearrange("p h k -> p (h k)"),
                                       ALU.add), "peer_experts")

            def slot_in(weights_of, g, i, s):
                return weights_of[:, bass.ds(i * BODY + (g * BODY + s), 1)]

            def landed(l, t, kind, g, i, s):
                n = ((l * NT + t) * 2 + kind) * P + g * BODY + s
                dve.wait_ge(sem(f"gathered{s % GBUF}"), i * (16 * BODY // GBUF) + 16 * (n // GBUF + 1))

            def dots(l, t, g, i, part=slice(0, BODY)):
                for s in range(BODY)[part]:
                    rows_of = gbuf[s % GBUF]
                    landed(l, t, 0, g, i, s)
                    dve.scalar_tensor_tensor(rows_of, rows_of, 1.0, x[:, t, :], ALU.mult, ALU.mult,
                                             accum_out=slot_in(hdot[t], g, i, s))\
                        .then_inc(sem(f"buffer_free{s % GBUF}"), 1)

            def sums(l, t, g, i, part=slice(0, BODY)):
                mine = [s for s in range(BODY) if s not in PE_SLABS]
                for s in range(BODY)[part]:
                    if s not in mine:
                        continue
                    landed(l, t, 1, g, i, s)
                    k = mine.index(s)
                    before = mine[k - 2] - (BODY if k < 2 else 0)
                    n = ((l * NT + t) * 2 + 1) * P + g * BODY + before
                    dve.wait_ge(sem(f"buffer_free{before % GBUF}"), i * (BODY // GBUF) + (n // GBUF + 2))
                    dve.scalar_tensor_tensor(acc[k % 2], gbuf[s % GBUF], slot_in(hdot[t], g, i, s), acc[k % 2],
                                             ALU.mult, ALU.add).then_inc(sem(f"buffer_free{s % GBUF}"), 1)

            def gathered_pass(work, l, t, pieces, first):
                if not any(first <= n < first + CHUNKS for n in pieces):
                    with dve.Fori(0, TURNS) as i:
                        work(l, t, 0, i)
                    return
                for n in range(CHUNKS):
                    if first + n in pieces:
                        piece(l, t, *pieces[first + n])
                    g, at = divmod(n * CHUNK, BODY)
                    work(l, t, g, 0, slice(at, at + CHUNK))

            def norm_after(t, n, g, b, name, pieces):
                return {**pieces, 1: ("norm", (t, n, g, b, name))}

            def passes(l, t, pieces):
                gathered_pass(dots, l, t, pieces, 0)
                for s in range(P - GBUF, P):
                    wait_freed(dve, l, t, 0, s)
                dve.sem_inc(sem("peer_dots"), 1)
                dve.wait_ge(sem("peer_exp"), l * NT + t + 1)
                gs = peer_st[:, 48:56]
                step(dve.tensor_reduce(gs, gate_w[t], AX, ALU.add))
                step(dve.reciprocal(gs, gs))
                step(dve.tensor_tensor(gate_w[t], gate_w[t], gs.unsqueeze(2).to_broadcast([P, PH, PK]), ALU.mult))
                dve.wait_ge(sem("peer_gelu"), l * NT + t + 1)
                step(dve.tensor_tensor(hdot[t], hdot[t], gate_w[t].rearrange("p h k -> p (h k)"), ALU.mult),
                     "peer_weights")
                done(dve.tensor_scalar(acc[0], x[:, t, :], ALPHA, None, ALU.mult), "dve_step")
                done(dve.memset(acc[1], 0.0), "dve_step")
                settle()
                gathered_pass(sums, l, t, pieces, CHUNKS)
                for s in range(P - GBUF, P):
                    wait_freed(dve, l, t, 1, s)
                step(dve.tensor_tensor(x[:, t, :], acc[0], acc[1], ALU.add))
                for h in range(2):
                    key = (f"sum{l}_{t}", h)
                    wait_filled(dve, key)
                    cols = slice(h * 512, (h + 1) * 512)
                    done(dve.tensor_tensor(x[:, t, cols], x[:, t, cols], bank(key)[:, :], ALU.add), "drained_by_dve")
                settle()

            def piece(l, t, name, what):
                o = 1 - t
                if name == "norm":
                    tile, n, gain, bias, ready = what
                    layer_norm(n, gain, bias, ready, [tile])
                if name == "dil":
                    for kind, u in what:
                        dilated(o, kind, u)
                if name == "mem":
                    for kind, m in what:
                        memory(o, kind, m)
                if name == "out":
                    for h in range(2):
                        key = (f"out1_{o}", h)
                        wait_filled(dve, key)
                        cols = slice(h * 512, (h + 1) * 512)
                        done(dve.scalar_tensor_tensor(x[:, o, cols], x[:, o, cols], ALPHA, bank(key)[:, :], ALU.mult,
                                                      ALU.add), "drained_by_dve")
                    settle()
                    layer_norm(3 + 2 * o, 8, 9, "x_ready", [o])
                if name.startswith("route"):
                    layer, tile = (1, o) if name == "route1" else (0, int(name[-1]))
                    (best_keys, best_pairs, experts)[what[1]](layer, tile, what[0])

            def dilated(t, kind, u):
                def normaliser(u):
                    dve.wait_ge(sem("dil_exp"), DSLOTS * t + u + 1)
                    r = att_rec[:, u % 3, 0:1]
                    step(dve.reciprocal(r, att_sum[:, u % 3, 0:1]))
                    step(dve.tensor_scalar(dil_diag[u % 3], ident, r, None, ALU.mult), "dil_diag")

                nk = (t + 1) * P
                if kind == "score":
                    E = (dil_E if t else dil_E0)[u % 3]
                    mask = c(f"dil_mask{t}", 3, nk)
                    for part in range(t + 1):
                        key = (f"dil_score_{t}", 2 * u + part)
                        wait_filled(dve, key)
                        lo, n = (0, 3) if t == 0 else ((0, 2) if part == 0 else (2, 1))
                        done(dve.scalar_tensor_tensor(
                            E[:, lo:lo + n, :], bank(key)[:, 0:n * nk].rearrange("p (g k) -> p g k", g=n),
                            P ** -0.5, mask[:, lo:lo + n, :], ALU.mult, ALU.add), "drained_by_dve")
                    settle()
                    row_max(E.rearrange("p g k -> p (g k)"), att_nm[:, u % 3, 0:1], "dil_max")
                    if u:
                        normaliser(u - 1)
                    if u == DSLOTS - 1:
                        normaliser(u)
                if kind == "value":
                    key = (f"dil_value_{t}", 2 * u)
                    wait_filled(dve, key)
                    done(dve.tensor_copy(tile_mixT[:, u, :], bank(key)[:, 0:P]), "drained_by_dve")

            def memory(t, kind, m):
                if kind == "score":
                    for s in range(2):
                        key = (f"mem_score1_{t}", 2 * m + s)
                        wait_filled(dve, key)
                        done(dve.tensor_copy(mem1_E[m][:, s, :], bank(key)[:, 0:S]), "drained_by_dve")
                    settle()
                    row_max(mem1_E[m], att_nm[:, m, :], "mem_max")
                    if m == 1:
                        for n in range(2):
                            dve.wait_ge(sem("mem_exp"), len(MEM_UNITS) + 2 * t + n + 1)
                            r = att_rec[:, n, :]
                            step(dve.reciprocal(r, att_sum[:, n, :]))
                            for s in range(2):
                                step(dve.tensor_scalar(mem1_diag[n][:, s, :], ident, r[:, s:s + 1], None, ALU.mult),
                                     "mem_diag" if s else "dve_step")
                if kind == "value":
                    key = (f"mem_value1_{t}", 2 * m)
                    wait_filled(dve, key)
                    done(dve.tensor_copy(tile_mixT[:, 6 + m, :], bank(key)[:, 0:P]), "drained_by_dve")

            normalised_x(0)
            if on("z"):
                done(dve.memset(xr_pad[:, :, 0:3], 0.0), "pad_zeroed")
                lam = c("lam")
                step(dve.tensor_scalar(lam_t[:, 4, :], lam, -1.0, None, ALU.mult))
                step(dve.tensor_tensor(lam_t[:, 0, :], lam, lam_t[:, 4, :], ALU.max), "lam_abs")
                dve.wait_ge(sem("lam_exp"), 1)
                step(dve.tensor_scalar(lam_t[:, 2, :], lam_t[:, 1, :], 1.0, None, ALU.add), "lam_w")
                step(dve.tensor_scalar(lam_t[:, 5, :], lam_t[:, 2, :], -1.0, None, ALU.add))
                step(dve.tensor_scalar(lam_t[:, 6, :], lam_t[:, 5, :], 0.0, None, ALU.is_equal))
                step(dve.tensor_tensor(lam_t[:, 5, :], lam_t[:, 5, :], lam_t[:, 6, :], ALU.add))
                step(dve.reciprocal(lam_t[:, 5, :], lam_t[:, 5, :]))
                dve.wait_ge(sem("lam_ln"), 1)
                step(dve.tensor_tensor(lam_t[:, 6, :], lam_t[:, 3, :], lam_t[:, 6, :], ALU.add))
                step(dve.tensor_tensor(lam_t[:, 6, :], lam_t[:, 6, :], lam_t[:, 1, :], ALU.mult))
                step(dve.tensor_tensor(lam_t[:, 6, :], lam_t[:, 6, :], lam_t[:, 5, :], ALU.mult))
                step(dve.tensor_scalar(lam_t[:, 4, :], lam_t[:, 4, :], 0.0, None, ALU.max))
                step(dve.tensor_tensor(lam_t[:, 4, :], lam_t[:, 4, :], lam_t[:, 6, :], ALU.add))
                step(dve.tensor_scalar(lam_t[:, 8, :], lam_t[:, 4, :], 8.0, None, ALU.mult))
                step(dve.tensor_scalar(lam_t[:, 9, :], lam_t[:, 4, :], -8.0, None, ALU.mult), "lam_rate")
                turned("xT_mix", "g_mix")
                wait_drained(dve, ("xr", 3))
                cw = c("conv_w", 4, NK)
                for k in range(4):
                    for j in range(NK):
                        src = xr_pad[:, j, k:k + S]
                        if k == 0:
                            done(dve.tensor_scalar(xc[:, j, :], src, cw[:, k, j:j + 1], c("conv_b")[:, j:j + 1],
                                                   ALU.mult, ALU.add), "dve_step")
                        else:
                            done(dve.scalar_tensor_tensor(xc[:, j, :], src, cw[:, k, j:j + 1], xc[:, j, :], ALU.mult,
                                                          ALU.add), "dve_step")
                    settle()
                dve.sem_inc(sem("conv_done"), 1)
                dve.wait_ge(sem("consts_loaded"), 16)
                for n in "kv":
                    key = (n + "c", 0)
                    wait_filled(dve, key)
                    for g in range(GROUPS):
                        for par in range(2):
                            ch = slice(par * HD, (par + 1) * HD)
                            src = bank(key)[(g % 2) * HD:(g % 2 + 1) * HD, (g // 2) * S + par:(g // 2 + 1) * S:2]\
                                .rearrange("p (c l) -> p c l", l=8)
                            for h in range(2):
                                pos = c("pos_" + n)[ch, h * 8:(h + 1) * 8].unsqueeze(1).to_broadcast([HD, 16, 8])
                                last = g == GROUPS - 1 and par == 1 and h == 1
                                done(dve.tensor_tensor(cmp_in[n][h][ch, g, :].rearrange("p (c l) -> p c l", l=8), src,
                                                       pos, ALU.add), "drained_by_dve" if last else "dve_step")
                    settle()
            if on("lru"):
                flat = [v.rearrange("p a s -> p (a s)") for v in (lru_t, lru_i, xc, lru_a)]
                wait_drained(dve, ("lru_i", 3))
                step(dve.tensor_tensor(flat[1], flat[1], flat[2], ALU.mult))
                dve.wait_ge(sem("lru_tanh"), NK)
                step(dve.tensor_scalar(flat[2], flat[0], 1.0, None, ALU.add))
                step(dve.reciprocal(flat[2], flat[2]))
                step(dve.tensor_tensor(flat[0], flat[0], flat[2], ALU.mult), "lru_b2")
                dve.wait_ge(sem("lru_root"), 1)
                step(dve.tensor_tensor(flat[1], flat[1], flat[0], ALU.mult))
                dve.wait_ge(sem("lru_exp"), NK)
                for j in range(NK):
                    done(dve.tensor_tensor_scan(xc[:, j, :], lru_a[:, j, :], lru_i[:, j, :], 0.0, ALU.mult, ALU.add),
                         "dve_step")
                settle()
                dve.sem_inc(sem("lru_scanned"), 1)
            if on("cmp"):
                wait_filled(dve, ("k_cmp", 0))
                step(dve.tensor_copy(k_cmp[:, :, :].rearrange("p m c -> p (m c)"), bank(("k_cmp", 0))[:, 0:2 * NCMP]),
                     "drained_by_dve")
                wait_filled(dve, ("v_cmp", 0))
                step(dve.tensor_copy(v_cmp[0:NCMP, :], bank(("v_cmp", 0))[0:NCMP, 0:256]), "drained_by_dve")
                wait_drained(dve, ("nsa_gate", 0))
                bias = c("cmp_bias", NT * NK, 2, NCMP)
                mask = c("cmp_mask", NT, NCMP)
                full = [P, HEADS, NCMP]
                for t in range(NT):
                    s, st = cmp_s[:, t], cmp_st[:, t]
                    for h in range(2):
                        key = ("cmp_score", 2 * t + h)
                        wait_filled(dve, key)
                        done(dve.tensor_tensor(s.rearrange("p (j h) c -> p h j c", h=2)[:, h],
                                               bank(key)[:, 0:NK * NCMP].rearrange("p (j c) -> p j c", j=NK),
                                               bias[:, t * NK:(t + 1) * NK, h, :], ALU.add), "drained_by_dve")
                    settle()
                    step(dve.tensor_reduce(st[:, 0, :], s, AX, ALU.max))
                    step(dve.tensor_tensor(s, s, st[:, 0, :].unsqueeze(2).to_broadcast(full), ALU.subtract), "cmp_shifted")
                for t in range(NT):
                    s, st = cmp_s[:, t], cmp_st[:, t]
                    dve.wait_ge(sem("cmp_exp"), t + 1)
                    step(dve.tensor_tensor(s, s, mask[:, t, :].unsqueeze(1).to_broadcast(full), ALU.mult))
                    step(dve.tensor_reduce(st[:, 1, :], s, AX, ALU.add))
                    step(dve.tensor_scalar(st[:, 1, :], st[:, 1, :], 1e-30, None, ALU.max))
                    step(dve.reciprocal(st[:, 2, :], st[:, 1, :]))
                    step(dve.tensor_tensor(st[:, 2, :], st[:, 2, :], nsa_g[:, t, 0, :], ALU.mult))
                    step(dve.tensor_tensor(s, s, st[:, 2, :].unsqueeze(2).to_broadcast(full), ALU.mult), "cmp_probs")
            if on("att"):
                def normaliser(u):
                    j, s, t = UNITS[u]
                    dve.wait_ge(sem("att_exp"), u + 1)
                    r = att_rec[:, u % 3, :]
                    step(dve.reciprocal(r, att_sum[:, u % 3, :]))
                    step(dve.tensor_tensor(r, r, nsa_g[:, t, 1:3, 2 * j + s], ALU.mult))
                    both = [P, 2, P]
                    step(dve.tensor_tensor(att_diag[u % 3], ident.unsqueeze(1).to_broadcast(both),
                                           r.unsqueeze(2).to_broadcast(both), ALU.mult), "att_diag")

                def add_recurrence(u):
                    if u == 28:
                        settle()
                        dve.wait_ge(sem("recurrence_gated"), 1)
                        step(dve.tensor_tensor(yT[:, 0:4, :], yT[:, 0:4, :], xc[:, 0:4, :], ALU.add))
                    if u == 29:
                        settle()
                        step(dve.tensor_tensor(yT[:, 4:7, :], yT[:, 4:7, :], xc[:, 4:7, :], ALU.add))
                    if u == len(UNITS) - 1:
                        settle()
                        step(dve.tensor_tensor(yT[:, 7, :], yT[:, 7, :], xc[:, 7, :], ALU.add), "y_ready")

                nd = c("neg_dist")
                for kind, u in attention_order():
                    key = ("att_" + kind, u)
                    if kind == "gate":
                        continue
                    j, s, t = UNITS[u]
                    if kind == "score":
                        wait_filled(dve, key)
                        nk = (t + 1) * P
                        E = att_E[u % 3] if t else att_E0[u % 3]
                        bias = nd[:, S - nk:S].unsqueeze(1).to_broadcast([P, 2, nk])
                        step(dve.scalar_tensor_tensor(E, bias, SLOPES[2 * j + s],
                                                      bank(key)[:, 0:2 * nk].rearrange("p (b k) -> p b k", b=2),
                                                      ALU.mult, ALU.add), "drained_by_dve")
                        row_max(E, att_nm[:, u % 3, :], "att_max")
                        if u:
                            normaliser(u - 1)
                        if u == len(UNITS) - 1:
                            normaliser(u)
                    if kind == "value":
                        wait_filled(dve, key)
                        if j // 2 < NZ0:
                            wait_drained(dve, ("att_gate", j // 2))
                        else:
                            dve.wait_ge(sem("gates_shaped"), 1)
                        h64 = slice(s * HD, (s + 1) * HD)
                        cols = slice(t * P, (t + 1) * P)
                        done(dve.tensor_tensor(yT[h64, j, cols], bank(key)[h64, 0:P], gma[h64, j, cols], ALU.mult),
                             "drained_by_dve")
                        add_recurrence(u)
            if on("mix"):
                post_norm("mix_out", 0, 0, "x_mixed")
            if on("ffn"):
                normalised_x(NT)
                order = ffn_order()
                first_slot = FFN_SLOT

                def split(src, high, low, tmp, name):
                    step(dve.tensor_scalar(tmp.bitcast(U32), src.bitcast(U32), HIGH, None, ALU.bitwise_and))
                    done(dve.tensor_tensor(low, src, tmp, ALU.subtract), "dve_step")
                    step(dve.tensor_copy(high, tmp), name)

                def split_slot(n):
                    slot = first_slot + n
                    if n == 0:
                        dve.wait_ge(sem("weight_free"), RING + first_slot)
                    if n >= SPLITS:
                        dve.wait_ge(sem("split_used"), n - SPLITS + 1)
                    dve.wait_ge(sem(f"weight_loaded{slot % RING}"), 16 * (slot // RING + 1))
                    w = w_split[n % SPLITS]
                    if n >= 2:
                        dve.wait_ge(sem("slot_high"), n - 1)
                    src, tmp = ring[:, slot % RING, :], masked[n % 2]
                    done(dve.tensor_scalar(tmp.bitcast(U32), src.bitcast(U32), HIGH, None, ALU.bitwise_and),
                         "slot_masked")
                    settle()
                    done(dve.tensor_tensor(w[:, 1, :], src, tmp, ALU.subtract), "weight_free")

                split_slot(0)
                turned("xT_ffn", "g_ffn")
                settle()
                for kh in range(2):
                    for t in range(NT):
                        ks, cols = slice(4 * kh, 4 * kh + 4), slice(t * P, (t + 1) * P)
                        tmp = masked[1][:, 0:4 * P].rearrange("p (k s) -> p k s", k=4)
                        split(xT[:, ks, cols], x_split[:, ks, 0, cols], x_split[:, ks, 1, cols], tmp, "x_split")
                split_slot(1)
                split_slot(2)
                for n, (kind, f) in enumerate(order):
                    if n + 3 < len(order):
                        split_slot(n + 3)
                    if kind in ("gate", "up"):
                        key = ("ffn_" + kind, f)
                        total = (gate_s if kind == "gate" else up_s)[f % 2]
                        dve.wait_ge(sem("ffn_low"), 2 * f + (kind == "up") + 1)
                        done(dve.tensor_tensor(total, total, bank(key)[:, 0:S], ALU.add), "drained_by_dve")
                    if kind == "up":
                        settle()
                        dve.wait_ge(sem("ffn_silu"), f + 1)
                        step(dve.tensor_tensor(act_T, gate_s[f % 2], up_s[f % 2], ALU.mult))
                        split(act_T, act_split[f % 3][:, 0, :], act_split[f % 3][:, 1, :], up_s[f % 2], "act_split")
                post_norm("ffn_down", NT, 1, "x_ready")
            if on("ple"):
                bias = row(2)
                for i in range(4):
                    t, cols = i // 2, slice((i % 2) * 512, (i % 2 + 1) * 512)
                    wait_filled(dve, ("ple_gate", i))
                    done(dve.tensor_tensor(tmp_tok[:, t, cols], bank(("ple_gate", i))[:, :], bias[:, cols], ALU.add),
                         "drained_by_dve")
                    settle()
                    dve.sem_inc(sem("ple_biased"), 1)
                dve.sem_inc(sem("rows_used"), 1)
                for i in range(4):
                    t, cols = i // 2, slice((i % 2) * 512, (i % 2 + 1) * 512)
                    wait_filled(dve, ("ple_proj", i))
                    dve.wait_ge(sem("ple_sigmoid"), i + 1)
                    step(dve.tensor_tensor(tmp_tok[:, t, cols], bank(("ple_proj", i))[:, :], tmp_tok[:, t, cols],
                                           ALU.mult), "drained_by_dve")
                    step(dve.tensor_tensor(x[:, t, cols], x[:, t, cols], tmp_tok[:, t, cols], ALU.add),
                         "x_ready" if i % 2 else "dve_step")
            if on("gla"):
                K = slice(0, GDK)
                for pair in range(2):
                    key = ("gla_gate", pair)
                    wait_filled(dve, key)
                    for i in range(2):
                        h = 2 * pair + i
                        done(dve.tensor_scalar(gf[K, h * S:(h + 1) * S], bank(key)[K, i * S:(i + 1) * S],
                                               c("gla_b")[K, h:h + 1], None, ALU.add),
                             "drained_by_dve" if i else "dve_step")
                settle()
                step(dve.tensor_scalar(ge[K], gf[K], -1.0, None, ALU.mult))
                step(dve.tensor_tensor(ge[K], ge[K], gf[K], ALU.max), "gla_abs")
                step(dve.tensor_scalar(gf[K], gf[K], 0.0, None, ALU.min))
                step(dve.memset(scan_mask[K], 1.0))
                step(dve.memset(scan_mask.rearrange("p (n c) -> p n c", c=CH)[K, :, 0:1], 0.0))
                dve.wait_ge(sem("gla_softplus"), 1)
                step(dve.tensor_tensor(gf[K], gf[K], ge[K], ALU.subtract))
                step(dve.tensor_scalar(gf[K], gf[K], 1.0 / 16.0, None, ALU.mult))
                step(dve.tensor_tensor_scan(gb[K], scan_mask[K], gf[K], 0.0, ALU.mult, ALU.add), "gla_cumsum")
                b3 = gb.rearrange("p (n c) -> p n c", c=CH)
                step(dve.tensor_tensor(gt.rearrange("p (n c) -> p n c", c=CH)[K],
                                       b3[K, :, CH - 1:CH].to_broadcast([GDK, GH * NCH, CH]), b3[K], ALU.subtract),
                     "gla_tail")
                dve.wait_ge(sem("gla_exp"), 3)
                wait_drained(dve, ("gla_k", 1))
                q2, k2, kt2, ke2 = (v.rearrange("p h s -> p (h s)") for v in (gq, gk, gkt, gke))
                done(dve.tensor_tensor(q2[K], q2[K], geb[K], ALU.mult), "dve_step")
                done(dve.tensor_tensor(kt2[K], k2[K], gf[K], ALU.mult), "dve_step")
                done(dve.tensor_tensor(ke2[K], k2[K], gt[K], ALU.mult), "dve_step")
                settle()
                dve.sem_inc(sem("gla_decayed"), 1)
                for t in range(NT):
                    key = ("gla_kendT", t)
                    wait_filled(dve, key)
                    done(dve.tensor_copy(kendT[:, t].rearrange("p h k -> p (h k)"), bank(key)[:, 0:GH * GDK]),
                         "drained_by_dve")
                wait_filled(dve, ("gla_intra", 0))
                done(dve.tensor_tensor(attnT.rearrange("p t h c -> p (t h) c"),
                                       bank(("gla_intra", 0))[:, :].rearrange("p (a c) -> p a c", c=CH),
                                       c("tri").unsqueeze(1).to_broadcast([P, 8, CH]), ALU.mult), "drained_by_dve")
                dec = geb.rearrange("p (h n c) -> p h n c", h=GH, n=NCH)
                for n in range(NCH - 1):
                    for hp in range(2):
                        key = ("gla_kv", 2 * n + hp)
                        wait_filled(dve, key)
                        for i in range(2):
                            h = 2 * hp + i
                            cols = slice(h * GDV, (h + 1) * GDV)
                            src = bank(key)[K, i * GDV:(i + 1) * GDV]
                            name = "drained_by_dve" if i else "dve_step"
                            if n == 0:
                                done(dve.tensor_copy(state[K, 0, cols], src), name)
                            else:
                                done(dve.scalar_tensor_tensor(state[K, n, cols], state[K, n - 1, cols],
                                                              dec[K, h, n, CH - 1:CH], src, ALU.mult, ALU.add), name)
                    settle()
                    dve.sem_inc(sem("gla_state"), 1)
                gain = row(3)
                wait_drained(dve, ("gla_r", 3))
                for t in range(NT):
                    done(dve.tensor_tensor(grs[:, t, :], grs[:, t, :], gain[:, 0:768], ALU.mult), "dve_step")
                settle()
                dve.sem_inc(sem("rows_used"), 1)
                dve.wait_ge(sem("gla_rms"), 1)
                step(dve.reciprocal(stat[:, 32:40], stat[:, 32:40]))
                for i in range(4):
                    t, hp = i // 2, i % 2
                    for h in range(2):
                        cols = slice((2 * hp + h) * GDV, (2 * hp + h + 1) * GDV)
                        done(dve.scalar_tensor_tensor(mixin[:, t, cols], bank(("gla_o", i))[:, h * GDV:(h + 1) * GDV],
                                                      stat[:, 32 + 2 * i + h:33 + 2 * i + h], grs[:, t, cols], ALU.mult,
                                                      ALU.mult), "drained_by_dve" if h else "dve_step")
                    if hp:
                        settle()
                        dve.sem_inc(sem("mix_ready"), 1)
            for l in range(1):
                if on(f"memat{l}"):
                    def mem_normaliser(u):
                        dve.wait_ge(sem("mem_exp"), l * len(MEM_UNITS) + u + 1)
                        r = att_rec[:, u % 3, :]
                        step(dve.reciprocal(r, att_sum[:, u % 3, :]))
                        for s in range(2):
                            done(dve.tensor_scalar(mem_diag[u % 3][:, s, :], ident, r[:, s:s + 1], None, ALU.mult),
                                 "mem_diag" if s else "dve_step")
                            if s == 0:
                                settle()

                    for kind, u in pipelined(len(MEM_UNITS)):
                        key = (f"mem_{kind}{l}", 2 * u)
                        m, t = MEM_UNITS[u]
                        if kind == "score":
                            E = mem_E[u % 3]
                            for s in range(2):
                                key = (f"mem_score{l}", 2 * u + s)
                                wait_filled(dve, key)
                                done(dve.tensor_copy(E[:, s, :], bank(key)[:, 0:S]), "drained_by_dve")
                            settle()
                            row_max(E, att_nm[:, u % 3, :], "mem_max")
                            if u:
                                mem_normaliser(u - 1)
                            if u == len(MEM_UNITS) - 1:
                                mem_normaliser(u)
                        if kind == "value":
                            wait_filled(dve, key)
                            done(dve.tensor_copy(mixT[:, 6 + m, t * P:(t + 1) * P], bank(key)[:, 0:P]), "drained_by_dve")
                if on(f"out{l}"):
                    for i in range(4):
                        t, cols = i // 2, slice((i % 2) * 512, (i % 2 + 1) * 512)
                        wait_filled(dve, (f"out{l}", i))
                        done(dve.scalar_tensor_tensor(x[:, t, cols], x[:, t, cols], ALPHA, bank((f"out{l}", i))[:, :],
                                                      ALU.mult, ALU.add), "drained_by_dve")
                    settle()
                    layer_norm(0, 4, 5, "x_ready")
                if on("peer0"):
                    for b in range(GBUF):
                        dve.sem_inc(sem(f"buffer_free{b}"), 1)
                    for g in range(2):
                        best_keys(0, 0, g)
                        best_pairs(0, 0, g)
                        experts(0, 0, g)
                    first = routing_pieces("0_0", [2, 3, 5, 7, 8, 10], [2, 3])
                    first.update(routing_pieces("0_1", [CHUNKS + n * 4 // 3 for n in range(3 * TURNS)], range(TURNS)))
                    passes(0, 0, first)
                    passes(0, 1, norm_after(0, 2, 6, 7, "x_ready", PIECES if on("peer1") else {}))
                    if not on("peer1"):
                        layer_norm(3, 6, 7, "x_ready", [1])
            if on("peer1"):
                passes(1, 0, norm_after(1, 4, 6, 7, "x_ready", PIECES))
                passes(1, 1, norm_after(0, 6, 10, 11, "x_final", {}))
                layer_norm(7, 10, 11, "x_final", [1])
            if dump is not None:
                settle()
                dve.sem_inc(sem("dbg_dve"), 1)


def prepare(inputs):
    a = {k: np.asarray(v) for k, v in inputs.items()}
    cols = constant_columns(a)
    where, at = {}, 0
    for name, v in cols.items():
        where[name] = (at, at + v.shape[1])
        at += v.shape[1]
    weights, where["ffn_slot"] = weight_slots(a)
    arrays = {
        "x_in": np.ascontiguousarray(a["x"][0]),
        "memT_in": np.ascontiguousarray(a["mem_2"][0].T),
        "weights": weights,
        "consts": np.concatenate(list(cols.values()), 1),
        "rows_in": row_vectors(a),
        "peer_u": a["peer_u_2"].reshape(2 * EXPERTS, D),
        "peer_v": a["peer_v_2"].reshape(2 * EXPERTS, D),
    }
    return arrays, where


def kernel(**inputs):
    import concourse.bacc as bacc
    from concourse.bass_utils import run_bass_kernel_spmd

    arrays, where = prepare(inputs)
    nc = bacc.Bacc("TRN2", target_bir_lowering=False, num_devices=1)
    aps = {name: nc.dram_tensor(name, v.shape, mybir.dt.from_np(v.dtype), kind="ExternalInput").ap()
           for name, v in arrays.items()}
    out = nc.dram_tensor("x_out", (S, D), F32, kind="ExternalOutput").ap()
    build(nc, aps["x_in"], aps["memT_in"], aps["weights"], aps["consts"], where, aps["rows_in"], aps["peer_u"],
          aps["peer_v"], out)
    r = run_bass_kernel_spmd(nc, [arrays], core_ids=[0])
    return r.results[0]["x_out"].reshape(1, S, D)
```
